# Optimizing a Trainium2 kernel written in Bass

```python
import jax, jax.numpy as jnp
from jax import lax
import numpy as np
import functools

D_MODEL = 1024
BATCH = 1
SEQ = 512
DEPTH = 1

GRID_W = 64
CTX_LEN = 256
FF_HALF = 2816
F_GROUPS = 4
F_GROUP_DIM = 128
F_WIDTH = F_GROUPS * F_GROUP_DIM
M_HEADS = 4
M_HEAD_DIM = 256
M_WIDTH = M_HEADS * M_HEAD_DIM
CONV_K = 3
CHUNK = 128
N_ADA = 9
EPS = 1e-6

COL_F = 0
COL_Q = COL_F + F_WIDTH
COL_K = COL_Q + M_WIDTH
COL_V = COL_K + M_WIDTH
COL_O = COL_V + M_WIDTH
COL_GATES = COL_O + M_WIDTH
COL_BR = COL_GATES + 4 * M_HEADS
IN_WIDTH = COL_BR + 2 * D_MODEL


def rmsnorm(x, g):
    xf = x.astype(jnp.float32)
    y = xf * lax.rsqrt(jnp.mean(xf * xf, axis=-1, keepdims=True) + EPS)
    return (y * g.astype(jnp.float32)).astype(x.dtype)

def modulate(x, shift, scale):
    return x * (1 + scale) + shift

def ada_params(cvec, w, b):
    m = jax.nn.silu(cvec) @ w + b
    return m.reshape(cvec.shape[0], N_ADA, 1, D_MODEL)

def swiglu(u, w13, w2):
    a, b = jnp.split(u @ w13, 2, axis=-1)
    return (jax.nn.silu(a) * b) @ w2

def half_ffn(h, shift, scale, gate, g_pre, g_post, w13, w2):
    u = modulate(rmsnorm(h, g_pre), shift, scale)
    return h + 0.5 * gate * rmsnorm(swiglu(u, w13, w2), g_post)

def dwconv(x, w, b):
    y = lax.conv_general_dilated(
        x, w[:, None, :].astype(x.dtype), window_strides=(1,),
        padding=[(CONV_K // 2, CONV_K // 2)],
        dimension_numbers=("NWC", "WIO", "NWC"),
        feature_group_count=x.shape[-1])
    return y + b

def to_heads(x):
    B, T, _ = x.shape
    return x.reshape(B, T, M_HEADS, M_HEAD_DIM).transpose(0, 2, 1, 3)

def fourier_latent(xf):
    B, T, _ = xf.shape
    rows = T // GRID_W
    z = xf.astype(jnp.float32).reshape(B, rows, GRID_W, F_GROUPS, F_GROUP_DIM)
    y = jnp.fft.fftn(z, axes=(1, 2, 4), norm="ortho").real
    return y.reshape(B, T, F_WIDTH).astype(xf.dtype)

def fourier_context(xf):
    B, T, _ = xf.shape
    z = xf.astype(jnp.float32).reshape(B, T, F_GROUPS, F_GROUP_DIM)
    y = jnp.fft.fftn(z, axes=(1, 3), norm="ortho").real
    return y.reshape(B, T, F_WIDTH).astype(xf.dtype)

def project(u, w_in, b_in, conv_w, conv_b):
    B, T, _ = u.shape
    p = u @ w_in + b_in
    xf = p[..., COL_F:COL_Q]
    qk = jax.nn.silu(dwconv(p[..., COL_Q:COL_V], conv_w, conv_b))
    q = to_heads(qk[..., :M_WIDTH])
    k = to_heads(qk[..., M_WIDTH:])
    v = to_heads(p[..., COL_V:COL_O])
    o = p[..., COL_O:COL_GATES]
    gates = p[..., COL_GATES:COL_BR].astype(jnp.float32)
    gates = gates.reshape(B, T, 4, M_HEADS).transpose(2, 0, 3, 1)
    gate_pre = (gates[0], jax.nn.log_sigmoid(gates[1]), gates[2], jax.nn.log_sigmoid(gates[3]))
    g_f = p[..., COL_BR:COL_BR + D_MODEL]
    g_m = p[..., COL_BR + D_MODEL:]
    return xf, q, k, v, o, gate_pre, g_f, g_m

def mlstm_scan(q, k, v, li, lf, state):
    B, H, T, DK = q.shape
    NC = T // CHUNK

    def chunks(a):
        a = a.astype(jnp.float32).reshape(B, H, NC, CHUNK, *a.shape[3:])
        return jnp.moveaxis(a, 2, 0)

    qc, kc, vc, lic, lfc = map(chunks, (q, k * (DK ** -0.5), v, li, lf))
    lower = jnp.tril(jnp.ones((CHUNK, CHUNK), dtype=bool))

    def step(carry, inp):
        C, n, m = carry
        qx, kx, vx, lix, lfx = inp
        b = jnp.cumsum(lfx, axis=-1)
        dmat = b[..., :, None] - b[..., None, :] + lix[..., None, :]
        dmat = jnp.where(lower, dmat, -jnp.inf)
        inter = b + m[..., None]
        m_t = jnp.maximum(inter, jnp.max(dmat, axis=-1))
        w = jnp.exp(dmat - m_t[..., None])
        a = jnp.exp(inter - m_t)
        s = jnp.einsum("bhtd,bhsd->bhts", qx, kx) * w
        num = a[..., None] * jnp.einsum("bhtd,bhde->bhte", qx, C) + jnp.einsum("bhts,bhse->bhte", s, vx)
        den = a * jnp.einsum("bhtd,bhd->bht", qx, n) + jnp.sum(s, axis=-1)
        h = num / jnp.maximum(jnp.abs(den), jnp.exp(-m_t))[..., None]
        bL = b[..., -1]
        g = bL[..., None] - b + lix
        m_new = jnp.maximum(bL + m, jnp.max(g, axis=-1))
        decay = jnp.exp(bL + m - m_new)
        wk = jnp.exp(g - m_new[..., None])
        C_new = decay[..., None, None] * C + jnp.einsum("bhsd,bhse->bhde", kx * wk[..., None], vx)
        n_new = decay[..., None] * n + jnp.einsum("bhs,bhsd->bhd", wk, kx)
        return (C_new, n_new, m_new), h

    state_out, hs = lax.scan(step, state, (qc, kc, vc, lic, lfc))
    h = jnp.moveaxis(hs, 0, 2).reshape(B, H, T, -1)
    return h.astype(q.dtype), state_out

def bidir_mlstm(q, k, v, gate_pre, state_f, state_b):
    li_f, lf_f, li_b, lf_b = gate_pre
    h_f, s_f = mlstm_scan(q, k, v, li_f, lf_f, state_f)
    flip = lambda a: jnp.flip(a, axis=2)
    h_b, s_b = mlstm_scan(flip(q), flip(k), flip(v), flip(li_b), flip(lf_b), state_b)
    return h_f + flip(h_b), s_f, s_b

def merge(y_fourier, h, o, g_f, g_m, head_g, w_four, w_mproj, w_out):
    B, H, T, dh = h.shape
    hn = rmsnorm(h.transpose(0, 2, 1, 3), head_g.reshape(M_HEADS, M_HEAD_DIM)).reshape(B, T, M_WIDTH)
    hm = jax.nn.sigmoid(o) * hn
    y = jax.nn.sigmoid(g_f) * (y_fourier @ w_four) + jax.nn.sigmoid(g_m) * (hm @ w_mproj)
    return y @ w_out

def token_mixing(h_lat, h_ctx, mod_l, mod_c, g_pre, g_post, w_in, b_in, conv_w, conv_b,
                 head_g, w_four, w_mproj, w_out, update_ctx):
    sh_l, sc_l, gt_l = mod_l
    sh_c, sc_c, gt_c = mod_c
    pl = project(modulate(rmsnorm(h_lat, g_pre), sh_l, sc_l), w_in, b_in, conv_w, conv_b)
    pc = project(modulate(rmsnorm(h_ctx, g_pre), sh_c, sc_c), w_in, b_in, conv_w, conv_b)
    B = h_ctx.shape[0]
    zero = (jnp.zeros((B, M_HEADS, M_HEAD_DIM, M_HEAD_DIM), jnp.float32),
            jnp.zeros((B, M_HEADS, M_HEAD_DIM), jnp.float32),
            jnp.zeros((B, M_HEADS), jnp.float32))
    h_c, s_f, s_b = bidir_mlstm(pc[1], pc[2], pc[3], pc[5], zero, zero)
    h_l, _, _ = bidir_mlstm(pl[1], pl[2], pl[3], pl[5], s_f, s_b)
    out_l = merge(fourier_latent(pl[0]), h_l, pl[4], pl[6], pl[7], head_g, w_four, w_mproj, w_out)
    new_lat = h_lat + gt_l * rmsnorm(out_l, g_post)
    new_ctx = None
    if update_ctx:
        out_c = merge(fourier_context(pc[0]), h_c, pc[4], pc[6], pc[7], head_g, w_four, w_mproj, w_out)
        new_ctx = h_ctx + gt_c * rmsnorm(out_c, g_post)
    return new_lat, new_ctx

def first_inputs(seed: int = 0) -> dict:
    key = jax.random.key(seed)
    ks = jax.random.split(key, 20)
    nrm = lambda k, shape, s: jax.random.normal(k, shape, jnp.float32) * s
    D = D_MODEL
    b_in = nrm(ks[10], (DEPTH, IN_WIDTH), 0.02)
    f_bias = jnp.linspace(3.0, 6.0, M_HEADS, dtype=jnp.float32)
    b_in = b_in.at[:, COL_GATES + M_HEADS:COL_GATES + 2 * M_HEADS].add(f_bias)
    b_in = b_in.at[:, COL_GATES + 3 * M_HEADS:COL_GATES + 4 * M_HEADS].add(f_bias)
    return {
        "x": nrm(ks[0], (BATCH, SEQ, D), 1.0),
        "c": nrm(ks[1], (BATCH, D), 1.0),
        "ctx": nrm(ks[2], (BATCH, CTX_LEN, D), 1.0),
        "c_ctx": nrm(ks[3], (D,), 1.0),
        "w_ada": nrm(ks[4], (DEPTH, D, N_ADA * D), D ** -0.5),
        "b_ada": nrm(ks[5], (DEPTH, N_ADA * D), 0.02),
        "norm_g": 1.0 + nrm(ks[6], (DEPTH, 6, D), 0.05),
        "w13_a": nrm(ks[7], (DEPTH, D, 2 * FF_HALF), D ** -0.5),
        "w2_a": nrm(ks[8], (DEPTH, FF_HALF, D), FF_HALF ** -0.5),
        "w_in": nrm(ks[9], (DEPTH, D, IN_WIDTH), D ** -0.5),
        "b_in": b_in,
        "conv_w": nrm(ks[11], (DEPTH, CONV_K, 2 * M_WIDTH), CONV_K ** -0.5),
        "conv_b": nrm(ks[12], (DEPTH, 2 * M_WIDTH), 0.02),
        "head_g": 1.0 + nrm(ks[13], (DEPTH, M_WIDTH), 0.05),
        "w_four": nrm(ks[14], (DEPTH, F_WIDTH, D), F_WIDTH ** -0.5),
        "w_mproj": nrm(ks[15], (DEPTH, M_WIDTH, D), M_WIDTH ** -0.5),
        "w_out": nrm(ks[16], (DEPTH, D, D), D ** -0.5),
        "w13_b": nrm(ks[17], (DEPTH, D, 2 * FF_HALF), D ** -0.5),
        "w2_b": nrm(ks[18], (DEPTH, FF_HALF, D), FF_HALF ** -0.5),
    }

def first_block(x, c, ctx, c_ctx, w_ada, b_ada, norm_g, w13_a, w2_a, w_in, b_in, conv_w, conv_b,
              head_g, w_four, w_mproj, w_out, w13_b, w2_b):
    h_lat = x
    h_ctx = ctx
    for l in range(DEPTH):
        last = l == DEPTH - 1
        ml = ada_params(c, w_ada[l], b_ada[l])
        mc = ada_params(c_ctx[None], w_ada[l], b_ada[l])
        g = norm_g[l]
        h_lat = half_ffn(h_lat, ml[:, 0], ml[:, 1], ml[:, 2], g[0], g[1], w13_a[l], w2_a[l])
        h_ctx = half_ffn(h_ctx, mc[:, 0], mc[:, 1], mc[:, 2], g[0], g[1], w13_a[l], w2_a[l])
        h_lat, h_ctx_new = token_mixing(
            h_lat, h_ctx, (ml[:, 3], ml[:, 4], ml[:, 5]), (mc[:, 3], mc[:, 4], mc[:, 5]),
            g[2], g[3], w_in[l], b_in[l], conv_w[l], conv_b[l], head_g[l],
            w_four[l], w_mproj[l], w_out[l], not last)
        h_lat = half_ffn(h_lat, ml[:, 6], ml[:, 7], ml[:, 8], g[4], g[5], w13_b[l], w2_b[l])
        if not last:
            h_ctx = half_ffn(h_ctx_new, mc[:, 6], mc[:, 7], mc[:, 8], g[4], g[5], w13_b[l], w2_b[l])
    return h_lat


DN_HEADS = 8
DN_HEAD_DIM = 128
DN_DIM = DN_HEADS * DN_HEAD_DIM
DN_CHUNK = 64
CONV_WIDTH = 4
SGU_GROUPS = 8
SGU_GROUP_DIM = 128
SGU_DIM = SGU_GROUPS * SGU_GROUP_DIM
SGU_CHUNK = 128
N_GROUPS = 4
EXPERTS_PER_GROUP = 4
N_EXPERTS = N_GROUPS * EXPERTS_PER_GROUP
TOP_K_IN_GROUP = 2
EXPERT_FF = 256
DEEPNORM_ALPHA = (2.0 * DEPTH) ** 0.25
DEEPNORM_BETA = (8.0 * DEPTH) ** -0.25
LN_EPS = 1e-5
NORM_EPS = 1e-6
PROJ_SIZES = (3 * DN_DIM, DN_DIM, DN_HEADS, DN_HEADS, 2 * SGU_DIM, D_MODEL, D_MODEL)
PROJ_DIM = sum(PROJ_SIZES)


def layer_norm(x, g, b):
    xf = x.astype(jnp.float32)
    xc = xf - jnp.mean(xf, axis=-1, keepdims=True)
    var = jnp.mean(xc * xc, axis=-1, keepdims=True)
    return (xc * lax.rsqrt(var + LN_EPS) * g + b).astype(x.dtype)

def l2_normalize(x):
    return x * lax.rsqrt(jnp.sum(x * x, axis=-1, keepdims=True) + NORM_EPS)

def causal_depthwise_conv(x, w):
    k = w.shape[0]
    return lax.conv_general_dilated(
        x, w[:, None, :], window_strides=(1,), padding=[(k - 1, 0)],
        dimension_numbers=("NWC", "WIO", "NWC"), feature_group_count=x.shape[-1])

def gated_delta_rule(q, k, v, g, beta):
    bsz, seq, heads, dk = q.shape
    dv = v.shape[-1]
    n = seq // DN_CHUNK

    def to_chunks(t):
        return jnp.swapaxes(t.reshape(bsz, n, DN_CHUNK, heads, *t.shape[3:]), 2, 3)

    q, k, v, g, beta = (to_chunks(t) for t in (q, k, v, g, beta))
    g_cum = jnp.cumsum(g, axis=-1)
    idx = jnp.arange(DN_CHUNK)
    causal = idx[:, None] >= idx[None, :]
    strict = idx[:, None] > idx[None, :]
    diff = g_cum[..., :, None] - g_cum[..., None, :]
    decay = jnp.where(causal, jnp.exp(jnp.where(causal, diff, 0.0)), 0.0)
    k_beta = k * beta[..., None]
    v_beta = v * beta[..., None]
    a_mat = jnp.where(strict, jnp.einsum("bnhtk,bnhsk->bnhts", k_beta, k) * decay, 0.0) \
        + jnp.eye(DN_CHUNK, dtype=q.dtype)
    solve = functools.partial(lax.linalg.triangular_solve, left_side=True, lower=True,
                              unit_diagonal=True)
    u = solve(a_mat, v_beta)
    w = solve(a_mat, k_beta * jnp.exp(g_cum)[..., None])
    qk = jnp.einsum("bnhtk,bnhsk->bnhts", q, k) * decay
    q_dec = q * jnp.exp(g_cum)[..., None]
    k_dec = k * jnp.exp(g_cum[..., -1:] - g_cum)[..., None]
    g_last = jnp.exp(g_cum[..., -1])

    def step(state, inp):
        qk_c, u_c, w_c, q_c, k_c, gl_c = inp
        v_new = u_c - jnp.einsum("bhtk,bhkv->bhtv", w_c, state)
        out = jnp.einsum("bhtk,bhkv->bhtv", q_c, state) + jnp.einsum("bhts,bhsv->bhtv", qk_c, v_new)
        state = state * gl_c[..., None, None] + jnp.einsum("bhsk,bhsv->bhkv", k_c, v_new)
        return state, out

    xs = tuple(jnp.moveaxis(t, 1, 0) for t in (qk, u, w, q_dec, k_dec, g_last))
    state0 = jnp.zeros((bsz, heads, dk, dv), jnp.float32)
    _, out = lax.scan(step, state0, xs)
    return jnp.transpose(out, (1, 0, 3, 2, 4)).reshape(bsz, seq, heads, dv)

def spatial_gating(uv, ln_g, ln_b, spatial_w, spatial_b, w_sgu_out):
    bsz, seq, _ = uv.shape
    n = seq // SGU_CHUNK
    u, v = jnp.split(jax.nn.gelu(uv, approximate=False), 2, axis=-1)
    v = layer_norm(v, ln_g, ln_b)
    v = v.reshape(bsz, n, SGU_CHUNK, SGU_GROUPS, SGU_GROUP_DIM)
    idx = jnp.arange(SGU_CHUNK)
    causal = idx[:, None] >= idx[None, :]
    w_causal = jnp.where(causal, spatial_w, 0)
    v = jnp.einsum("gts,bnsgc->bntgc", w_causal, v) + spatial_b.T[:, :, None]
    gated = u * v.reshape(bsz, seq, SGU_DIM)
    return jnp.einsum("blc,cd->bld", gated, w_sgu_out)

def hybrid_mixer(x, w_in, conv_w, a_log, dt_bias, dn_norm_g, w_dn_out,
                 sgu_ln_g, sgu_ln_b, spatial_w, spatial_b, w_sgu_out, w_out):
    bsz, seq, _ = x.shape
    f32 = jnp.float32
    proj = jnp.einsum("bld,dp->blp", x, w_in)
    offsets = np.cumsum(PROJ_SIZES)[:-1].tolist()
    qkv, z, a, b, uv, gate_dn, gate_sgu = jnp.split(proj, offsets, axis=-1)

    qkv = jax.nn.silu(causal_depthwise_conv(qkv, conv_w)).astype(f32)
    q, k, v = jnp.split(qkv, 3, axis=-1)
    to_heads = lambda t: t.reshape(bsz, seq, DN_HEADS, DN_HEAD_DIM)
    q = l2_normalize(to_heads(q)) * (DN_HEAD_DIM ** -0.5)
    k = l2_normalize(to_heads(k))
    v = to_heads(v)
    beta = jax.nn.sigmoid(b.astype(f32))
    g = -jnp.exp(a_log.astype(f32)) * jax.nn.softplus(a.astype(f32) + dt_bias.astype(f32))
    o = gated_delta_rule(q, k, v, g, beta)
    o = o * lax.rsqrt(jnp.mean(o * o, axis=-1, keepdims=True) + NORM_EPS) * dn_norm_g.astype(f32)
    o = o * jax.nn.silu(to_heads(z).astype(f32))
    y_dn = jnp.einsum("blc,cd->bld", o.reshape(bsz, seq, DN_DIM).astype(x.dtype), w_dn_out)

    y_sgu = spatial_gating(uv, sgu_ln_g, sgu_ln_b, spatial_w, spatial_b, w_sgu_out)

    y = jax.nn.sigmoid(gate_dn) * y_dn + jax.nn.sigmoid(gate_sgu) * y_sgu
    return jnp.einsum("bld,de->ble", y, w_out)

def hierarchical_moe(x, router_group_w, router_group_b, router_expert_w, router_expert_b,
                     expert_w_gate, expert_w_up, expert_w_down):
    bsz, seq, d = x.shape
    f32 = jnp.float32
    t = x.reshape(bsz * seq, d)
    n_tok = t.shape[0]
    group_logits = (t @ router_group_w + router_group_b).astype(f32)
    group_p, group_idx = lax.top_k(jax.nn.softmax(group_logits, axis=-1), 1)
    group_p, group_idx = group_p[:, 0], group_idx[:, 0]
    expert_logits = (t @ router_expert_w + router_expert_b).astype(f32)
    expert_logits = expert_logits.reshape(n_tok, N_GROUPS, EXPERTS_PER_GROUP)
    in_group = expert_logits[jnp.arange(n_tok), group_idx]
    exp_p, exp_idx = lax.top_k(jax.nn.softmax(in_group, axis=-1), TOP_K_IN_GROUP)
    exp_p = exp_p / jnp.sum(exp_p, axis=-1, keepdims=True)
    gate = group_p[:, None] * exp_p
    expert_id = group_idx[:, None] * EXPERTS_PER_GROUP + exp_idx
    combine = jnp.sum(jax.nn.one_hot(expert_id, N_EXPERTS, dtype=f32) * gate[..., None], axis=1)
    h = jax.nn.silu(jnp.einsum("td,edf->tef", t, expert_w_gate)) \
        * jnp.einsum("td,edf->tef", t, expert_w_up)
    h = h * combine[:, :, None].astype(h.dtype)
    y = jnp.einsum("tef,efd->td", h, expert_w_down)
    return y.reshape(bsz, seq, d)

def second_inputs(seed: int = 0) -> dict:
    key = jax.random.key(seed)
    ks = jax.random.split(key, 24)
    f32 = jnp.float32
    nrm = lambda k, shape, scale: jax.random.normal(k, shape, f32) * scale
    dt = jnp.exp(jax.random.uniform(ks[4], (DEPTH, DN_HEADS), f32,
                                    minval=float(np.log(1e-3)), maxval=float(np.log(1e-1))))
    return {
        "x": nrm(ks[0], (BATCH, SEQ, D_MODEL), 1.0),
        "w_in": nrm(ks[1], (DEPTH, D_MODEL, PROJ_DIM), D_MODEL ** -0.5),
        "conv_w": nrm(ks[2], (DEPTH, CONV_WIDTH, 3 * DN_DIM), CONV_WIDTH ** -0.5),
        "a_log": jnp.log(jax.random.uniform(ks[3], (DEPTH, DN_HEADS), f32, minval=1.0, maxval=16.0)),
        "dt_bias": dt + jnp.log(-jnp.expm1(-dt)),
        "dn_norm_g": 1.0 + nrm(ks[5], (DEPTH, DN_HEAD_DIM), 0.1),
        "w_dn_out": nrm(ks[6], (DEPTH, DN_DIM, D_MODEL), DN_DIM ** -0.5),
        "sgu_ln_g": 1.0 + nrm(ks[7], (DEPTH, SGU_DIM), 0.1),
        "sgu_ln_b": nrm(ks[8], (DEPTH, SGU_DIM), 0.02),
        "spatial_w": nrm(ks[9], (DEPTH, SGU_GROUPS, SGU_CHUNK, SGU_CHUNK), 0.05),
        "spatial_b": 1.0 + nrm(ks[10], (DEPTH, SGU_GROUPS, SGU_CHUNK), 0.1),
        "w_sgu_out": nrm(ks[11], (DEPTH, SGU_DIM, D_MODEL), SGU_DIM ** -0.5),
        "w_out": nrm(ks[12], (DEPTH, D_MODEL, D_MODEL), D_MODEL ** -0.5 * DEEPNORM_BETA),
        "ln1_g": 1.0 + nrm(ks[13], (DEPTH, D_MODEL), 0.1),
        "ln1_b": nrm(ks[14], (DEPTH, D_MODEL), 0.02),
        "router_group_w": nrm(ks[15], (DEPTH, D_MODEL, N_GROUPS), D_MODEL ** -0.5),
        "router_group_b": nrm(ks[16], (DEPTH, N_GROUPS), 0.01),
        "router_expert_w": nrm(ks[17], (DEPTH, D_MODEL, N_EXPERTS), D_MODEL ** -0.5),
        "router_expert_b": nrm(ks[18], (DEPTH, N_EXPERTS), 0.01),
        "expert_w_gate": nrm(ks[19], (DEPTH, N_EXPERTS, D_MODEL, EXPERT_FF), D_MODEL ** -0.5),
        "expert_w_up": nrm(ks[20], (DEPTH, N_EXPERTS, D_MODEL, EXPERT_FF), D_MODEL ** -0.5),
        "expert_w_down": nrm(ks[21], (DEPTH, N_EXPERTS, EXPERT_FF, D_MODEL), EXPERT_FF ** -0.5 * DEEPNORM_BETA),
        "ln2_g": 1.0 + nrm(ks[22], (DEPTH, D_MODEL), 0.1),
        "ln2_b": nrm(ks[23], (DEPTH, D_MODEL), 0.02),
    }

def second_block(x, w_in, conv_w, a_log, dt_bias, dn_norm_g, w_dn_out, sgu_ln_g, sgu_ln_b,
              spatial_w, spatial_b, w_sgu_out, w_out, ln1_g, ln1_b,
              router_group_w, router_group_b, router_expert_w, router_expert_b,
              expert_w_gate, expert_w_up, expert_w_down, ln2_g, ln2_b):
    h = x
    for l in range(DEPTH):
        mix = hybrid_mixer(h, w_in[l], conv_w[l], a_log[l], dt_bias[l], dn_norm_g[l], w_dn_out[l],
                           sgu_ln_g[l], sgu_ln_b[l], spatial_w[l], spatial_b[l], w_sgu_out[l], w_out[l])
        h = layer_norm(DEEPNORM_ALPHA * h + mix, ln1_g[l], ln1_b[l])
        ffn = hierarchical_moe(h, router_group_w[l], router_group_b[l], router_expert_w[l],
                               router_expert_b[l], expert_w_gate[l], expert_w_up[l], expert_w_down[l])
        h = layer_norm(DEEPNORM_ALPHA * h + ffn, ln2_g[l], ln2_b[l])
    return h


def setup_inputs(seed=0):
    out = dict(first_inputs(seed))
    for name, value in second_inputs(seed + 1).items():
        if name != "x":
            out[name + "_2"] = value
    return out


def reference(
    x, c, ctx, c_ctx, w_ada, b_ada, norm_g, w13_a, w2_a, w_in, b_in, conv_w, conv_b, head_g,
    w_four, w_mproj, w_out, w13_b, w2_b, w_in_2, conv_w_2, a_log_2, dt_bias_2, dn_norm_g_2,
    w_dn_out_2, sgu_ln_g_2, sgu_ln_b_2, spatial_w_2, spatial_b_2, w_sgu_out_2, w_out_2, ln1_g_2,
    ln1_b_2, router_group_w_2, router_group_b_2, router_expert_w_2, router_expert_b_2,
    expert_w_gate_2, expert_w_up_2, expert_w_down_2, ln2_g_2, ln2_b_2,
):
    x = first_block(
        x, c, ctx, c_ctx, w_ada, b_ada, norm_g, w13_a, w2_a, w_in, b_in, conv_w, conv_b, head_g,
        w_four, w_mproj, w_out, w13_b, w2_b,
    )
    return second_block(
        x, w_in_2, conv_w_2, a_log_2, dt_bias_2, dn_norm_g_2, w_dn_out_2, sgu_ln_g_2,
        sgu_ln_b_2, spatial_w_2, spatial_b_2, w_sgu_out_2, w_out_2, ln1_g_2, ln1_b_2,
        router_group_w_2, router_group_b_2, router_expert_w_2, router_expert_b_2,
        expert_w_gate_2, expert_w_up_2, expert_w_down_2, ln2_g_2, ln2_b_2,
    )


_drawn_inputs = setup_inputs


def setup_inputs(seed=0):
    import zlib

    import numpy as np

    out = dict(_drawn_inputs(seed))
    spreads = {}
    factors = {'conv_b': 36.957,
     'head_g': 2.782,
     'sgu_ln_g_2': 5.486,
     'sgu_ln_b_2': 30.532,
     'router_group_b_2': 6.702,
     'router_expert_b_2': 29.398,
     'ln2_b_2': 2.851,
     'dn_norm_g_2': 2.803,
     'spatial_b_2': 2.76}
    for name, (base, spread) in spreads.items():
        noise = np.random.default_rng([zlib.crc32(name.encode()), seed]).standard_normal(out[name].shape)
        drawn = base * np.exp(spread * noise) if base else spread * noise
        out[name] = __import__('jax').numpy.asarray(drawn.astype(out[name].dtype))
    for name, factor in factors.items():
        out[name] = (out[name] * factor).astype(out[name].dtype)
    return out
```

```python
import numpy as np
import concourse.bass as bass
from concourse import mybir

F32 = mybir.dt.float32
F32R = mybir.dt.float32r
ALU = mybir.AluOpType
ACT = mybir.ActivationFunctionType
ds = bass.ds

P = 128
D = 1024
KT = D // P
T = 512
TC = 256
W = T + TC
FFH = 2816
HTILES = FFH // P // 2
ADA = 9
MH = 4
DH = 256
NCH = T // P
NCC = TC // P
DNH = 8
NE = 16
EFF = 256
ETILES = NE * EFF // P // 2
EPS = 1e-6
LN_EPS = 1e-5
ALPHA = 2.0 ** 0.25
BIG = 1e30

BASE = 16512
RAW = BASE
WHI = RAW + 2 * 8192
WLO = WHI + 2 * 8192
CONST = WLO + 2 * 8192
TMP = CONST + 4608
MAIN = TMP + 5 * W * 4 + 1024
LIMIT = 229368

PARAM_SIZES = [("c", 8), ("c_ctx", 8), ("b_ada", 72), ("norm_g", 48), ("bk", 8), ("bq", 8), ("bgate", 1),
               ("bo", 8), ("bgf", 8), ("bgm", 8), ("conv_w", 48), ("conv_b", 16), ("head_g", 8),
               ("conv_w_2", 96), ("dn_g", 1), ("ln1_g", 8), ("ln1_b", 8), ("ln2_g", 8), ("ln2_b", 8),
               ("dt_bias", 1), ("a_log", 1)]
PARAM_AT = {}
_at = 0
for _n, _s in PARAM_SIZES:
    PARAM_AT[_n] = _at
    _at += _s
NPARAM = _at

STREAM = [("gu_a0", HTILES, 16), ("dn_a0", 8, HTILES), ("gu_a1", HTILES, 16), ("dn_a1", 8, HTILES),
          ("gates", 1, 8), ("wk", 4, 16), ("wq", 4, 16), ("wv", 4, 16), ("wxf", 2, 16),
          ("wo", 4, 16), ("wgf", 4, 16), ("wgm", 4, 16), ("w_four", 4, 8), ("w_mproj", 4, 16), ("w_out", 4, 16),
          ("gu_b0", HTILES, 16), ("dn_b0", 8, HTILES), ("gu_b1", HTILES, 16), ("dn_b1", 8, HTILES),
          ("gates2", 1, 8), ("wqkv2", 12, 16), ("wz2", 4, 16), ("wgd2", 4, 16), ("w_dn", 4, 16),
          ("wv2", 4, 16), ("wu2", 4, 16), ("wgs2", 4, 16), ("w_sgu", 4, 16), ("w_out2", 4, 16),
          ("router", 1, 2), ("e_up0", ETILES, 16), ("e_dn0", 8, ETILES), ("e_up1", ETILES, 16), ("e_dn1", 8, ETILES)]
START = {}
_at = 0
for _n, _s, _f in STREAM:
    START[_n] = (_at, _at + _s)
    _at += _s
NSLOTS = _at


class Env:
    pass


class Stage:

    def __init__(self, e, name):
        self.e, self.nc, self.name, self.used = e, e.nc, name, []

    def sem(self, name):
        s = self.nc.alloc_semaphore(f"{self.name}_{name}")
        self.used.append(s)
        return s

    def sb(self, name, shape, offset, dt=F32):
        size = int(np.prod(shape[1:])) * 4
        assert offset + size <= LIMIT, (self.name, name, offset + size - LIMIT)
        return self.nc.alloc_sbuf_tensor_at(f"{self.name}_{name}", shape, dt, offset=offset)

    def close(self):
        for s in self.used:
            self.nc.gpsimd.sem_clear(s)
        for s in self.e.cleared:
            self.nc.release_semaphore(s)
        self.e.cleared = self.used


def slots(eng, a, b, body):
    at = 0
    for name, n, _ in STREAM:
        lo, hi = max(a, at), min(b, at + n)
        if lo < hi:
            while lo < min(2, hi):
                body(name, lo - at, lo % 2, lo, (lo - at) // 2, lo // 2)
                lo += 1
            pairs = (hi - lo) // 2 if hi - lo >= 4 else 0
            if pairs:
                with eng.Fori(0, pairs) as i:
                    for s in range(2):
                        body(name, lo - at + s + 2 * i, (lo + s) % 2, lo + s + 2 * i, (lo - at + s) // 2 + i,
                             (lo + s) // 2 + i)
            for g in range(lo + 2 * pairs, hi):
                body(name, g - at, g % 2, g, (g - at) // 2, g // 2)
        at += n


def feed_ahead(e, b, more=0):
    upto = min(b + 1 + more, NSLOTS)
    pool, e.split_upto = (e.split_upto, upto), max(e.split_upto, upto)
    sp, e.loaded_upto = (e.loaded_upto, min(upto + 2, NSLOTS)), max(e.loaded_upto, min(upto + 2, NSLOTS))
    return sp, pool


def feed_sp(e, sp, span):
    tiles = {n: f for n, _, f in STREAM}

    def load(name, i, p, g, ihalf, ghalf):
        sp.wait_ge(e.w_split, g - 1)
        src = e.dram[name]
        sp.dma_start(e.raw[p][:, 0:tiles[name] * P],
                     src[i] if isinstance(i, int) else src[ds(i, 1)].rearrange("a p n -> p (a n)")
                     ).then_inc(e.w_landed[p], 16)

    slots(sp, *span, load)


def feed_pool(e, pool, span):
    tiles = {n: f for n, _, f in STREAM}

    def split(name, i, p, g, ihalf, ghalf):
        f = tiles[name] * P
        pool.wait_ge(e.w_landed[p], 16 * ghalf + 16)
        if not (isinstance(g, int) and g < 2):
            pool.wait_ge(e.slot_done, g - 1)
        e.nc.gpsimd.tensor_tensor(e.whi[p][:, 0:f], e.raw[p][:, 0:f], e.one_col[:, 0:1].to_broadcast([P, f]),
                                  ALU.mult).then_inc(e.w_hi, 1)
        pool.wait_ge(e.w_hi, g + 1)
        e.nc.gpsimd.tensor_tensor(e.wlo[p][:, 0:f], e.raw[p][:, 0:f], e.whi[p][:, 0:f].bitcast(F32),
                                  ALU.subtract).then_inc(e.w_split, 1)

    slots(pool, *span, split)


def pe_slot_begin(e, pe, g):
    pe.wait_ge(e.w_split, g + 1)
    if not (isinstance(g, int) and g < 2):
        pe.wait_ge(e.acc_free, g - 1)


def three_pass(e, out, wh, wl, xh, xl, first, last):
    e.nc.tensor.matmul(out, wh, xh, start=first, stop=False)
    e.nc.tensor.matmul(out, wh, xl, start=False, stop=False)
    return e.nc.tensor.matmul(out, wl, xh, start=False, stop=last)


def pe_feature_major(e, p, kt, ntile, xh, xl, ctx):
    done = None
    for n in range(ntile):
        for k in range(kt):
            at = (n * kt + k) * P
            done = three_pass(e, e.bank[2 * p + n][:, :], e.whi[p][:, at:at + P], e.wlo[p][:, at:at + P],
                              xh[:, k, 0:T], xl[:, k, 0:T], k == 0, k == kt - 1)
    if ctx:
        for n in range(ntile):
            for k in range(kt):
                at = (n * kt + k) * P
                done = three_pass(e, e.bank[4 + p][:, n * TC:(n + 1) * TC], e.whi[p][:, at:at + P],
                                  e.wlo[p][:, at:at + P], xh[:, k, T:W], xl[:, k, T:W], k == 0, k == kt - 1)
    return done


def pe_token_major(e, p, ncol, xh, xl, ctx):
    done = None
    for t in range(NCH + (NCC if ctx else 0)):
        bank = e.bank[2 * p + t // 2] if t < NCH else e.bank[4 + p]
        out = bank[:, (t % 2) * ncol:(t % 2 + 1) * ncol]
        for k in range(KT):
            col = slice(k * ncol, (k + 1) * ncol)
            tok = slice(t * P, (t + 1) * P)
            e.nc.tensor.matmul(out, xh[:, k, tok], e.whi[p][:, col], start=k == 0, stop=False)
            e.nc.tensor.matmul(out, xh[:, k, tok], e.wlo[p][:, col], start=False, stop=False)
            done = e.nc.tensor.matmul(out, xl[:, k, tok], e.whi[p][:, col], start=False, stop=k == KT - 1)
    return done


def parts_of(w):
    return [(slice(0, T), 0)] + ([(slice(T, W), 1)] if w == W else [])


def prologue(e):
    st = Stage(e, "ada")
    nc = e.nc
    ring = [st.sb(f"w{r}", [P, 2048], MAIN + 24576 + r * 8192) for r in range(4)]
    x = st.sb("x", [P, KT, W], MAIN)
    sc = st.sb("sc", [P, KT, 2], TMP)
    landed = [st.sem(f"landed{r}") for r in range(4)]
    params_in, x_in, used, silu, ones_set, chain = (
        st.sem(n) for n in ("params_in", "x_in", "used", "silu", "ones_set", "chain"))
    nada = ADA * KT // 2
    e.x0 = x
    with nc.Block() as block:
        @block.sync
        def _(sp):
            sp.dma_start(e.params[:, :], e.dram["params"]).then_inc(params_in, 16)
            sp.dma_start(e.ident[:, :], e.dram["ident"]).then_inc(params_in, 16)
            for r in range(4):
                sp.dma_start(ring[r][:, :], e.dram["w_ada"][r]).then_inc(landed[r], 16)
            for g in range(2):
                sp.dma_start(e.raw[g][:, :], e.dram["gu_a0"][g]).then_inc(e.w_landed[g], 16)
            with sp.Fori(1, nada // 4) as i:
                for r in range(4):
                    sp.wait_ge(used, 4 * i + r - 3)
                    sp.dma_start(ring[r][:, :], e.dram["w_ada"][ds(4 * i + r, 1)].rearrange("a p n -> p (a n)")
                                 ).then_inc(landed[r], 16)
            sp.dma_start(x[:, :, :], e.dram["x"]).then_inc(x_in, 16)
            sp.wait_ge(params_in, 32)
            sp.wait_ge(x_in, 16)

        @block.gpsimd
        def _(pool):
            pool.wait_ge(ones_set, 1)
            feed_pool(e, pool, (0, 2))

        @block.scalar
        def _(act):
            act.wait_ge(params_in, 32)
            for s, n in enumerate(("c", "c_ctx")):
                at = PARAM_AT[n]
                nc.scalar.activation(sc[:, :, s], e.params[:, at:at + KT], ACT.Silu).then_inc(silu, 1)

        @block.tensor
        def _(pe):
            pe.wait_ge(silu, 2)
            with pe.Fori(0, nada // 4) as i:
                for r in range(4):
                    pe.wait_ge(landed[r], 16 * i + 16)
                    for n in range(2):
                        for k in range(KT):
                            at = (n * KT + k) * P
                            last = nc.tensor.matmul(e.bank[0][:, ds((4 * i + r) * 4 + 2 * n, 2)],
                                                    ring[r][:, at:at + P], sc[:, k, :],
                                                    start=k == 0, stop=k == KT - 1)
                    last.then_inc(used, 1)

        @block.vector
        def _(dve):
            nc.vector.memset(e.one_col[:, :], 1.0)
            nc.vector.memset(e.eps[:, 0:1], EPS)
            nc.vector.memset(e.eps[:, 1:2], LN_EPS)
            nc.vector.memset(e.mean_ones[:, :], 1.0 / D)
            nc.vector.memset(e.ones[:, :], 1.0).then_inc(ones_set, 1)
            dve.wait_ge(used, nada)
            dve.wait_ge(params_in, 32)
            at = PARAM_AT["b_ada"]
            acc = e.bank[0][:, 0:ADA * KT * 2].rearrange("p (m s) -> p m s", s=2)
            for s in range(2):
                last = nc.vector.tensor_tensor(e.mods[:, :, s], acc[:, :, s], e.params[:, at:at + ADA * KT], ALU.add)
            last.then_inc(chain, 1)
            dve.wait_ge(chain, 1)
            for j in range(3):
                g_pre = PARAM_AT["norm_g"] + 2 * j * KT
                for s in range(2):
                    sc_at, gt_at = (3 * j + 1) * KT, (3 * j + 2) * KT
                    nc.vector.scalar_tensor_tensor(e.gs[:, j, :, s], e.mods[:, sc_at:sc_at + KT, s], 1.0,
                                                   e.params[:, g_pre:g_pre + KT], ALU.add, ALU.mult)
                    nc.vector.scalar_tensor_tensor(e.gg[:, j, :, s], e.mods[:, gt_at:gt_at + KT, s],
                                                   1.0 if j == 1 else 0.5,
                                                   e.params[:, g_pre + KT:g_pre + 2 * KT], ALU.mult, ALU.mult)
    st.close()


def rms_stats(e, st, w, x):
    nc = e.nc
    sq = [st.sb(f"sq{r}", [P, w], TMP + r * W * 4) for r in range(2)]
    acc = st.sb("acc", [P, w], TMP + 2 * W * 4)
    rstd = st.sb("rstd", [P, w], TMP + 3 * W * 4)
    squared, summed, mean_ready, std_ready, rstd_ready = (
        st.sem(n) for n in ("squared", "summed", "mean_ready", "std_ready", "rstd_ready"))

    def act_part(act):
        for k in range(KT):
            if k >= 2:
                act.wait_ge(summed, k - 1)
            nc.scalar.activation(sq[k % 2][:, :], x[:, k, :], ACT.Square).then_inc(squared, 1)
        act.wait_ge(mean_ready, 1)
        for c, s in parts_of(w):
            last = nc.scalar.activation(acc[:, c], e.bank[6 + s][:, 0:c.stop - c.start], ACT.Sqrt,
                                        bias=e.eps[:, 0:1])
        last.then_inc(std_ready, 1)

    def dve_part(dve):
        for k in range(KT):
            dve.wait_ge(squared, k + 1)
            if k == 0:
                nc.vector.tensor_copy(acc[:, :], sq[0][:, :]).then_inc(summed, 1)
            else:
                dve.wait_ge(summed, k)
                nc.vector.tensor_tensor(acc[:, :], acc[:, :], sq[k % 2][:, :], ALU.add).then_inc(summed, 1)
        dve.wait_ge(std_ready, 1)
        nc.vector.reciprocal(rstd[:, :], acc[:, :]).then_inc(rstd_ready, 1)
        dve.wait_ge(rstd_ready, 1)

    def pe_part(pe):
        pe.wait_ge(summed, KT)
        for c, s in parts_of(w):
            last = nc.tensor.matmul(e.bank[6 + s][:, 0:c.stop - c.start], e.mean_ones[:, :], acc[:, c],
                                    start=True, stop=True)
        last.then_inc(mean_ready, 1)

    return rstd, act_part, dve_part, pe_part


def pre_norm(e, name, j, w, x, uh, ul):
    st = Stage(e, name)
    nc = e.nc
    rstd, act_stats, dve_stats, pe_stats = rms_stats(e, st, w, x)
    t = [st.sb(f"t{r}", [P, w], TMP + r * W * 4) for r in range(2)]
    u = [st.sb(f"u{r}", [P, w], TMP + (2 if r == 0 else 4) * W * 4) for r in range(2)]
    scaled, u_ready, hi_ready, lo_ready = (st.sem(n) for n in ("scaled", "u_ready", "hi_ready", "lo_ready"))
    with nc.Block() as block:
        @block.tensor
        def _(pe):
            pe_stats(pe)

        @block.scalar
        def _(act):
            act_stats(act)
            for k in range(KT):
                act.wait_ge(scaled, k + 1)
                if k >= 2:
                    act.wait_ge(lo_ready, k - 1)
                for c, s in parts_of(w):
                    last = nc.scalar.activation(u[k % 2][:, c], t[k % 2][:, c], ACT.Identity,
                                                bias=e.mods[:, 3 * j * KT + k, s:s + 1])
                last.then_inc(u_ready, 1)
                act.wait_ge(u_ready, k + 1)
                nc.scalar.activation(uh[:, k, :], u[k % 2][:, :], ACT.Copy).then_inc(hi_ready, 1)

        @block.vector
        def _(dve):
            dve_stats(dve)

            def scale(k):
                if k >= 2:
                    dve.wait_ge(u_ready, k - 1)
                for c, s in parts_of(w):
                    last = nc.vector.scalar_tensor_tensor(t[k % 2][:, c], x[:, k, c], e.gs[:, j, k, s:s + 1],
                                                          rstd[:, c], ALU.mult, ALU.mult)
                last.then_inc(scaled, 1)

            scale(0)
            for k in range(KT):
                if k + 1 < KT:
                    scale(k + 1)
                dve.wait_ge(hi_ready, k + 1)
                nc.vector.tensor_tensor(ul[:, k, :], u[k % 2][:, :], uh[:, k, :].bitcast(F32),
                                        ALU.subtract).then_inc(lo_ready, 1)
    st.close()


def post_norm(e, name, j, w, y, res, out, load=None, store=None):
    st = Stage(e, name)
    nc = e.nc
    rstd, act_stats, dve_stats, pe_stats = rms_stats(e, st, w, y)
    t = [st.sb(f"t{r}", [P, w], TMP + r * W * 4) for r in range(2)]
    res_in, scaled, added, stored = (st.sem(n) for n in ("res_in", "scaled", "added", "stored"))
    with nc.Block() as block:
        @block.sync
        def _(sp):
            if load is not None:
                sp.dma_start(res[:, :, :], load).then_inc(res_in, 16)
            if store is not None:
                sp.wait_ge(added, KT)
                sp.dma_start(store, out[:, :, 0:T]).then_inc(stored, 16)
                sp.wait_ge(stored, 16)

        @block.tensor
        def _(pe):
            pe_stats(pe)

        @block.scalar
        def _(act):
            act_stats(act)

        @block.vector
        def _(dve):
            dve_stats(dve)
            if load is not None:
                dve.wait_ge(res_in, 16)
            for k in range(KT):
                for c, s in parts_of(w):
                    last = nc.vector.scalar_tensor_tensor(t[k % 2][:, c], y[:, k, c], e.gg[:, j, k, s:s + 1],
                                                          rstd[:, c], ALU.mult, ALU.mult)
                last.then_inc(scaled, 1)
                dve.wait_ge(scaled, k + 1)
                nc.vector.tensor_tensor(out[:, k, :], t[k % 2][:, :], res[:, k, :], ALU.add).then_inc(added, 1)
    st.close()


def tile_at(t, i):
    return t[:, i, :] if isinstance(i, int) else t[:, ds(i, 1), :].rearrange("p a w -> p (a w)")


def ffn(e, name, up, down, halves, w, htiles, uh, ul, y, hid_at, combine=None):
    st = Stage(e, name)
    nc = e.nc
    hh = st.sb("hh", [P, htiles, w], hid_at, F32R)
    hl = st.sb("hl", [P, htiles, w], hid_at + htiles * w * 4, F32R)
    sil = [st.sb(f"sil{r}", [P, w], TMP + r * W * 4) for r in range(2)]
    v = [st.sb(f"v{r}", [P, w], TMP + (2 + r) * W * 4) for r in range(2)]
    silu_ready, hi_ready, lo_ready, gated = (st.sem(n) for n in ("silu_ready", "hi_ready", "lo_ready", "gated"))
    ctx = w == W
    a, b = START[f"{up}{halves[0]}"][0], START[f"{down}{halves[-1]}"][1]
    sp_span, pool_span = feed_ahead(e, b)
    with nc.Block() as block:
        @block.sync
        def _(sp):
            feed_sp(e, sp, sp_span)

        @block.gpsimd
        def _(pool):
            feed_pool(e, pool, pool_span)

        @block.tensor
        def _(pe):
            for m, half in enumerate(halves):
                def up_slot(nm, i, p, g, ih, gh):
                    pe_slot_begin(e, pe, g)
                    pe_feature_major(e, p, KT, 2, uh, ul, ctx).then_inc(e.slot_done, 1)

                slots(pe, *START[f"{up}{half}"], up_slot)
                pe.wait_ge(lo_ready, htiles * (m + 1))

                def down_slot(nm, i, p, g, ih, gh):
                    pe_slot_begin(e, pe, g)
                    pe_feature_major(e, p, htiles, 1, hh, hl, ctx).then_inc(e.slot_done, 1)

                slots(pe, *START[f"{down}{half}"], down_slot)

        @block.scalar
        def _(act):
            for m, half in enumerate(halves):
                def silu_slot(nm, i, p, g, ih, gh):
                    act.wait_ge(e.slot_done, g + 1)
                    if not (isinstance(g, int) and g < 2):
                        act.wait_ge(e.acc_free, g - 1)
                    last = nc.scalar.activation(sil[p][:, 0:T], e.bank[2 * p][:, :], ACT.Silu)
                    if ctx:
                        last = nc.scalar.activation(sil[p][:, T:W], e.bank[4 + p][:, 0:TC], ACT.Silu)
                    last.then_inc(silu_ready, 1)
                    act.wait_ge(e.acc_free, g + 1)
                    nc.scalar.activation(tile_at(hh, i), v[p][:, :], ACT.Copy).then_inc(hi_ready, 1)

                slots(act, *START[f"{up}{half}"], silu_slot)

        @block.vector
        def _(dve):
            for m, half in enumerate(halves):
                def mul_slot(nm, i, p, g, ih, gh):
                    n = i + m * htiles
                    dve.wait_ge(silu_ready, n + 1)
                    if combine is not None:
                        nc.vector.tensor_tensor(sil[p][:, :], sil[p][:, :], tile_at(combine, ih), ALU.mult
                                                ).then_inc(gated, 1)
                        dve.wait_ge(gated, n + 1)
                    last = nc.vector.tensor_tensor(v[p][:, 0:T], sil[p][:, 0:T], e.bank[2 * p + 1][:, :], ALU.mult)
                    if ctx:
                        last = nc.vector.tensor_tensor(v[p][:, T:W], sil[p][:, T:W], e.bank[4 + p][:, TC:2 * TC],
                                                       ALU.mult)
                    last.then_inc(e.acc_free, 1)
                    dve.wait_ge(hi_ready, n + 1)
                    nc.vector.tensor_tensor(tile_at(hl, i), v[p][:, :], tile_at(hh, i).bitcast(F32), ALU.subtract
                                            ).then_inc(lo_ready, 1)

                slots(dve, *START[f"{up}{half}"], mul_slot)

                def out_slot(nm, i, p, g, ih, gh):
                    dve.wait_ge(e.slot_done, g + 1)
                    yv = tile_at(y, i)
                    pieces = [(yv[:, 0:T], e.bank[2 * p][:, :])]
                    if ctx:
                        pieces.append((yv[:, T:W], e.bank[4 + p][:, 0:TC]))
                    for dst, src in pieces:
                        if half == 0:
                            last = nc.vector.tensor_copy(dst, src)
                        else:
                            last = nc.vector.tensor_tensor(dst, dst, src, ALU.add)
                    last.then_inc(e.acc_free, 1)

                slots(dve, *START[f"{down}{half}"], out_slot)
    st.close()


def gemm(e, name, seg, pe_body, act_body=None, dve_body=None, act_end=None, dve_end=None, sp_end=None):
    a, b = START[seg]
    sp_span, pool_span = feed_ahead(e, b)
    with e.nc.Block() as block:
        @block.sync
        def _(sp):
            feed_sp(e, sp, sp_span)

        @block.gpsimd
        def _(pool):
            feed_pool(e, pool, pool_span)

        @block.tensor
        def _(pe):
            def body(nm, i, p, g, ih, gh):
                pe_slot_begin(e, pe, g)
                pe_body(p).then_inc(e.slot_done, 1)
            slots(pe, a, b, body)

        @block.scalar
        def _(act):
            if act_body is not None:
                slots(act, a, b, lambda nm, i, p, g, ih, gh: act_body(act, i, p, g))

        @block.vector
        def _(dve):
            if dve_body is not None:
                slots(dve, a, b, lambda nm, i, p, g, ih, gh: dve_body(dve, i, p, g))


def project_1(e, uh, ul, K, Q, V, XF, GR, bias_tok):
    st = Stage(e, "proj")
    nc = e.nc
    raw = [st.sb(f"raw{n}", [P, W], TMP + n * W * 4) for n in range(2)]
    con = [st.sb(f"con{n}", [P, W], TMP + (2 + n) * W * 4) for n in range(2)]
    bias_in, tap_done, silu_done, spilled = (st.sem(n) for n in ("bias_in", "tap_done", "silu_done", "spilled"))
    a, b = START["gates"][0], START["wxf"][1]
    conv_w, conv_b = PARAM_AT["conv_w"], PARAM_AT["conv_b"]

    def column(at, i, n):
        return e.params[:, at + 2 * i + n:at + 2 * i + n + 1] if isinstance(i, int) else \
            e.params[:, ds(at + n + 2 * i, 1)]

    sp_span, pool_span = feed_ahead(e, b)
    with nc.Block() as block:
        @block.sync
        def _(sp):
            sp.dma_start(bias_tok[:, :], e.dram["bias_tok"]).then_inc(bias_in, 16)
            sp.dma_start(e.dram["uh_s"], uh[:, :, 0:T].bitcast(F32)).then_inc(spilled, 16)
            sp.dma_start(e.dram["ul_s"], ul[:, :, 0:T].bitcast(F32)).then_inc(spilled, 16)
            feed_sp(e, sp, sp_span)
            sp.wait_ge(spilled, 32)

        @block.gpsimd
        def _(pool):
            feed_pool(e, pool, pool_span)

        @block.tensor
        def _(pe):
            def fm(ntile, ctx):
                def body(nm, i, p, g, ih, gh):
                    pe_slot_begin(e, pe, g)
                    pe_feature_major(e, p, KT, ntile, uh, ul, ctx).then_inc(e.slot_done, 1)
                return body

            def tm(ctx):
                def body(nm, i, p, g, ih, gh):
                    pe_slot_begin(e, pe, g)
                    pe_token_major(e, p, 256, uh, ul, ctx).then_inc(e.slot_done, 1)
                return body

            slots(pe, *START["gates"], fm(1, True))
            slots(pe, *START["wk"], fm(2, True))
            slots(pe, *START["wq"], fm(2, False))
            slots(pe, *START["wv"], tm(True))
            slots(pe, *START["wxf"], tm(False))

        @block.scalar
        def _(act):
            g0 = START["gates"][0]
            at = PARAM_AT["bgate"]
            act.wait_ge(e.slot_done, g0 + 1)
            nc.scalar.activation(GR[:, 0:T], e.bank[2 * (g0 % 2)][:, :], ACT.Identity, bias=e.params[:, at:at + 1])
            nc.scalar.activation(GR[:, T:W], e.bank[4 + g0 % 2][:, 0:TC], ACT.Identity,
                                 bias=e.params[:, at:at + 1]).then_inc(e.acc_free, 1)

            def rows(dst, w, bias_at, conv_at, m0):
                def body(nm, i, p, g, ih, gh):
                    act.wait_ge(e.slot_done, g + 1)
                    for n in range(2):
                        last = nc.scalar.activation(raw[n][:, 0:T], e.bank[2 * p + n][:, :], ACT.Identity,
                                                    bias=column(bias_at, i, n))
                        if w == W:
                            last = nc.scalar.activation(raw[n][:, T:W], e.bank[4 + p][:, n * TC:(n + 1) * TC],
                                                        ACT.Identity, bias=column(bias_at, i, n))
                    last.then_inc(e.acc_free, 1)
                    for n in range(2):
                        act.wait_ge(tap_done, 3 * m0 + 3 * n + 3 + 6 * i)
                        out = dst[:, 2 * i + n, 0:w] if isinstance(i, int) else \
                            dst[:, ds(n + 2 * i, 1), 0:w].rearrange("p a w -> p (a w)")
                        nc.scalar.activation(out, con[n][:, 0:w], ACT.Silu, bias=column(conv_at, i, n)
                                             ).then_inc(silu_done, 1)
                return body

            slots(act, *START["wk"], rows(K, W, PARAM_AT["bk"], conv_b + 8, 0))
            slots(act, *START["wq"], rows(Q, T, PARAM_AT["bq"], conv_b, 8))

        @block.vector
        def _(dve):
            def conv(w, conv_at, m0):
                def body(nm, i, p, g, ih, gh):
                    dve.wait_ge(e.acc_free, g + 1)
                    for n in range(2):
                        if m0:
                            dve.wait_ge(silu_done, m0 + n - 1 + 2 * i)
                        elif isinstance(i, int):
                            if i:
                                dve.wait_ge(silu_done, n - 1 + 2 * i)
                        tap = [column(conv_at + 16 * j, i, n) for j in range(3)]
                        nc.vector.tensor_scalar(con[n][:, 0:w], raw[n][:, 0:w], tap[1], None, ALU.mult
                                                ).then_inc(tap_done, 1)
                        dve.wait_ge(tap_done, 3 * m0 + 3 * n + 1 + 6 * i)
                        for c, _ in parts_of(w):
                            lo, hi = c.start, c.stop
                            last = nc.vector.scalar_tensor_tensor(con[n][:, lo + 1:hi], raw[n][:, lo:hi - 1], tap[0],
                                                                  con[n][:, lo + 1:hi], ALU.mult, ALU.add)
                        last.then_inc(tap_done, 1)
                        dve.wait_ge(tap_done, 3 * m0 + 3 * n + 2 + 6 * i)
                        for c, _ in parts_of(w):
                            lo, hi = c.start, c.stop
                            last = nc.vector.scalar_tensor_tensor(con[n][:, lo:hi - 1], raw[n][:, lo + 1:hi], tap[2],
                                                                  con[n][:, lo:hi - 1], ALU.mult, ALU.add)
                        last.then_inc(tap_done, 1)
                return body

            k0, k1 = START["wk"]
            slots(dve, k0, k0 + 1, conv(W, conv_w + 8, 0))
            slots(dve, k0 + 1, k1, conv(W, conv_w + 8, 0))
            slots(dve, *START["wq"], conv(T, conv_w, 8))
            dve.wait_ge(bias_in, 16)

            def add_bias(dst, bias_at, ntok):
                def body(nm, i, p, g, ih, gh):
                    dve.wait_ge(e.slot_done, g + 1)
                    for t in range(ntok):
                        bank = e.bank[2 * p + t // 2] if t < NCH else e.bank[4 + p]
                        cols = slice(256 * i, 256 * i + 256) if isinstance(i, int) else ds(256 * i, 256)
                        bcol = slice(bias_at + 256 * i, bias_at + 256 * i + 256) if isinstance(i, int) else \
                            ds(bias_at + 256 * i, 256)
                        last = nc.vector.tensor_tensor(dst[:, t, cols], bank[:, (t % 2) * 256:(t % 2 + 1) * 256],
                                                       bias_tok[:, bcol], ALU.add)
                    last.then_inc(e.acc_free, 1)
                return body

            slots(dve, *START["wv"], add_bias(V, 0, NCH + NCC))
            slots(dve, *START["wxf"], add_bias(XF, D, NCH))
    st.close()


STEPS = [[(T + P * j, None) for j in range(NCC)] + [(P * j, j) for j in range(NCH)],
         [(T + P * j, None) for j in reversed(range(NCC))] + [(P * j, j) for j in reversed(range(NCH))]]


def scan_rows(e, GR, B, LF, G, RT, MP, GC):
    st = Stage(e, "rows")
    nc = e.nc
    R = 36
    zero = st.sb("zero", [R, P], TMP)
    t1 = st.sb("t1", [R, W], TMP + 1024)
    t2 = st.sb("t2", [R, W], TMP + 1024 + W * 4)
    pre_ready, abs_ready, exp_ready, ln_ready, g_ready, gc_psum, chain = (
        st.sem(n) for n in ("pre_ready", "abs_ready", "exp_ready", "ln_ready", "g_ready", "gc_psum", "chain"))
    with nc.Block() as block:
        @block.sync
        def _(sp):
            sp.nop()

        @block.scalar
        def _(act):
            act.wait_ge(pre_ready, 1)
            nc.scalar.activation(t1[:, :], LF[:, :], ACT.Abs).then_inc(abs_ready, 1)
            act.wait_ge(abs_ready, 1)
            nc.scalar.activation(t2[:, :], t1[:, :], ACT.Exp, scale=-1.0).then_inc(exp_ready, 1)
            act.wait_ge(exp_ready, 1)
            nc.scalar.activation(t1[:, :], t2[:, :], ACT.Ln, bias=e.one_col[0:R, 0:1]).then_inc(ln_ready, 1)

        @block.tensor
        def _(pe):
            pe.wait_ge(g_ready, 1)
            for j in range(NCH + NCC):
                last = nc.tensor.matmul(e.bank[0][:, j * R:(j + 1) * R], G[0:R, j * P:(j + 1) * P],
                                        e.ident[0:R, 0:R], start=True, stop=True)
            last.then_inc(gc_psum, 1)

        @block.vector
        def _(dve):
            done = [0]

            def link(ins):
                done[0] += 1
                ins.then_inc(chain, 1)
                dve.wait_ge(chain, done[0])

            nc.vector.tensor_copy(LF[:, :], GR[64:64 + R, :]).then_inc(pre_ready, 1)
            nc.vector.memset(zero[:, :], 0.0)
            nc.vector.memset(MP[:, :], 0.0)
            link(nc.vector.memset(B[:, :], 0.0))
            dve.wait_ge(ln_ready, 1)
            link(nc.vector.scalar_tensor_tensor(LF[:, :], LF[:, :], 0.0, t1[:, :], ALU.min, ALU.subtract))
            cut = [[(slice(32 * d, 32 * d + MH), slice(c, c + P)) for c, _ in STEPS[d]] for d in range(2)]

            def walk(ap, d):
                return ap[:, ::-1] if d else ap

            for d in range(2):
                for r, c in cut[d]:
                    last = nc.vector.tensor_tensor_scan(walk(B[r, c], d), walk(zero[0:MH, :], d), walk(LF[r, c], d), 0.0,
                                                        ALU.add, ALU.add) if d == 0 else \
                        nc.vector.tensor_tensor_scan(walk(B[r, c], d), walk(zero[r, :], d), walk(LF[r, c], d), 0.0,
                                                     ALU.add, ALU.add)
            link(last)
            nc.vector.tensor_tensor(G[0:R, :], GR[0:R, :], B[:, :], ALU.subtract).then_inc(g_ready, 1)
            dve.wait_ge(g_ready, 1)
            for j in range(NCH + NCC):
                for d in range(2):
                    r, c = cut[d][j]
                    last = nc.vector.tensor_tensor_scan(walk(RT[r, 0, c], d), walk(G[r, c], d), walk(G[r, c], d),
                                                        MP[r, j:j + 1], ALU.max, ALU.max)
                link(last)
                for d in range(2):
                    r, c = cut[d][j]
                    end = c.start if d else c.stop - 1
                    last = nc.vector.tensor_tensor(MP[r, j + 1:j + 2], B[r, end:end + 1], RT[r, 0, end:end + 1], ALU.add)
                    nc.vector.tensor_scalar(RT[r, 1, c], RT[r, 0, c], MP[r, j:j + 1], -1.0, ALU.subtract, ALU.mult)
                    last = nc.vector.scalar_tensor_tensor(RT[r, 2, c], B[r, c], -1.0, RT[r, 0, c],
                                                          ALU.mult, ALU.subtract)
                link(last)
            dve.wait_ge(gc_psum, 1)
            nc.vector.tensor_copy(GC[:, :, :], e.bank[0][:, 0:(NCH + NCC) * R].rearrange("p (j r) -> p j r", r=R))
    st.close()


def scan(e, Q, K, V, C, HT, RT, GC, SEL, MASK):
    st = Stage(e, "scan")
    nc = e.nc
    NV = DH + P
    units = [(j, h, d) for j in range(NCC + NCH) for h in range(MH) for d in range(2)]
    lat = [u[0] >= NCC for u in units]
    upd = [u[0] < NCC + NCH - 1 for u in units]
    nlat = [sum(lat[:n]) for n in range(len(units) + 1)]
    nupd = [sum(upd[:n]) for n in range(len(units) + 1)]
    off = [TMP]

    def pair(n, cols):
        out = [st.sb(f"{n}{r}", [P, cols], off[0] + r * cols * 4) for r in range(2)]
        off[0] += 2 * cols * 4
        return out

    AE, W1, WM, SW, KW, QA, DEN, RD, WKS = (
        pair(n, c) for n, c in (("ae", 256), ("w1", P), ("wm", P), ("sw", P), ("kw", 256), ("qa", 256), ("den", P),
                                ("rd", P), ("wks", 8)))
    HTMP = pair("htmp", 256)
    assert off[0] <= MAIN
    sel_in, zeroed, a_ready, w1_ready, ae_ready, w_ready, sw_ready, wks_ready, kw_ready, qa_ready, num_ready, \
        upd_ready, c_ready, abs_ready, max_ready, rd_ready, mul_ready, h_ready = (
            st.sem(n) for n in ("sel_in", "zeroed", "a_ready", "w1_ready", "ae_ready", "w_ready", "sw_ready",
                                "wks_ready", "kw_ready", "qa_ready", "num_ready", "upd_ready", "c_ready", "abs_ready",
                                "max_ready", "rd_ready", "mul_ready", "h_ready"))

    def where(u):
        j, h, d = units[u]
        return j, h, d, STEPS[d][j][0], u % 2, (0 if d else P - 1)

    with nc.Block() as block:
        @block.sync
        def _(sp):
            sp.dma_start(SEL[:, :], e.dram["sel"]).then_inc(sel_in, 16)
            sp.dma_start(MASK[:, :], e.dram["scan_mask"]).then_inc(sel_in, 16)
            sp.wait_ge(sel_in, 32)

        @block.tensor
        def _(pe):
            def first(u):
                j, h, d, c, p, end = where(u)
                if u >= 2:
                    pe.wait_ge(kw_ready, u - 1)
                    pe.wait_ge(ae_ready, u - 1)
                if lat[u]:
                    for t in range(2):
                        nc.tensor.matmul(e.bank[p][:, 0:P], K[:, 2 * h + t, c:c + P], Q[:, 2 * h + t, c:c + P],
                                         start=t == 0, stop=t == 1)
                for t in range(2):
                    nc.tensor.transpose(e.bank[p][:, P + t * P:2 * P + t * P], K[:, 2 * h + t, c:c + P], e.ident[:, :])
                nc.tensor.matmul(e.bank[2 + p][:, 0:3 * P], SEL[32 * d:32 * d + MH, h * P:(h + 1) * P],
                                 RT[32 * d:32 * d + MH, :, c:c + P], start=True, stop=True).then_inc(a_ready, 1)

            def second(u):
                j, h, d, c, p, end = where(u)
                cs = C[2 * h + d]
                prev = u - 2 * MH
                if prev >= 0:
                    pe.wait_ge(c_ready, nupd[prev + 1])
                if lat[u]:
                    pe.wait_ge(sw_ready, nlat[u] + 1)
                    pe.wait_ge(qa_ready, nlat[u] + 1)
                    if nlat[u] >= 2:
                        pe.wait_ge(h_ready, nlat[u] - 1)
                    vt = c // P
                    for m in range(3):
                        out = e.bank[4 + p][:, m * P:(m + 1) * P]
                        for t in range(2):
                            nc.tensor.matmul(out, cs[:, t, m * P:(m + 1) * P], QA[p][:, t * P:(t + 1) * P],
                                             start=t == 0, stop=False)
                        vm = V[:, vt, h * DH + m * P:h * DH + (m + 1) * P] if m < 2 else e.ones[:, :]
                        last = nc.tensor.matmul(out, vm, SW[p][:, :], start=False, stop=True)
                    last.then_inc(num_ready, 1)
                if upd[u]:
                    pe.wait_ge(kw_ready, u + 1)
                    if nupd[u]:
                        pe.wait_ge(c_ready, nupd[u])
                    for t in range(2):
                        nc.tensor.matmul(e.bank[6 + t][:, 0:DH], KW[p][:, t * P:(t + 1) * P],
                                         V[:, c // P, h * DH:(h + 1) * DH], start=True, stop=True)
                        last = nc.tensor.matmul(e.bank[6 + t][:, DH:NV], KW[p][:, t * P:(t + 1) * P], e.ones[:, :],
                                                start=True, stop=True)
                    last.then_inc(upd_ready, 1)

            pe.wait_ge(sel_in, 32)
            first(0)
            for u in range(len(units)):
                if u + 1 < len(units):
                    first(u + 1)
                second(u)

        @block.scalar
        def _(act):
            def first(u):
                j, h, d, c, p, end = where(u)
                act.wait_ge(w1_ready, u + 1)
                if u >= 2:
                    act.wait_ge(c_ready, nupd[u - 1])
                    if nlat[u - 1]:
                        act.wait_ge(h_ready, nlat[u - 1])
                        act.wait_ge(max_ready, nlat[u - 1])
                nc.scalar.activation(AE[p][:, :], e.bank[2 + p][:, P:3 * P], ACT.Exp).then_inc(ae_ready, 1)
                if u >= 2:
                    act.wait_ge(wks_ready, u - 1)
                nc.scalar.activation(WM[p][:, :], W1[p][:, :], ACT.Exp, scale=-1.0).then_inc(w_ready, 1)
                act.wait_ge(wks_ready, u + 1)
                if u >= 2 and nupd[u - 1]:
                    act.wait_ge(upd_ready, nupd[u - 1])
                nc.scalar.activation(KW[p][:, :], e.bank[p][:, P:3 * P], ACT.Copy, scale=WKS[p][:, 0:1]
                                     ).then_inc(kw_ready, 1)

            def second(u):
                p = u % 2
                if lat[u]:
                    act.wait_ge(num_ready, nlat[u] + 1)
                    if nlat[u] >= 2:
                        act.wait_ge(max_ready, nlat[u] - 1)
                    nc.scalar.activation(DEN[p][:, :], e.bank[4 + p][:, DH:NV], ACT.Abs).then_inc(abs_ready, 1)

            first(0)
            for u in range(len(units)):
                if u + 1 < len(units):
                    first(u + 1)
                second(u)

        @block.vector
        def _(dve):
            for t in C[:-1]:
                nc.vector.memset(t[:, :, :], 0.0)
            nc.vector.memset(C[-1][:, :, :], 0.0).then_inc(zeroed, 1)
            dve.wait_ge(sel_in, 32)
            dve.wait_ge(zeroed, 1)

            def first(u):
                j, h, d, c, p, end = where(u)
                dve.wait_ge(a_ready, u + 1)
                if u >= 2:
                    dve.wait_ge(w_ready, u - 1)
                nc.vector.scalar_tensor_tensor(W1[p][:, :], e.bank[2 + p][:, 0:P], GC[:, c // P, 32 * d + h:32 * d + h + 1],
                                               MASK[:, d * P:(d + 1) * P], ALU.subtract, ALU.add).then_inc(w1_ready, 1)
                dve.wait_ge(w_ready, u + 1)
                if lat[u]:
                    if nlat[u] >= 2:
                        dve.wait_ge(num_ready, nlat[u] - 1)
                    nc.vector.scalar_tensor_tensor(SW[p][:, :], e.bank[p][:, 0:P], DH ** -0.5, WM[p][:, :],
                                                   ALU.mult, ALU.mult).then_inc(sw_ready, 1)
                if u >= 2:
                    dve.wait_ge(kw_ready, u - 1)
                nc.vector.tensor_scalar(WKS[p][:, 0:1], WM[p][:, end:end + 1], DH ** -0.5, None, ALU.mult
                                        ).then_inc(wks_ready, 1)
                if lat[u]:
                    dve.wait_ge(ae_ready, u + 1)
                    for t in range(2):
                        last = nc.vector.tensor_tensor(QA[p][:, t * P:(t + 1) * P], Q[:, 2 * h + t, c:c + P],
                                                       AE[p][:, 0:P], ALU.mult)
                    last.then_inc(qa_ready, 1)

            def second(u):
                j, h, d, c, p, end = where(u)
                cs = C[2 * h + d]
                if upd[u]:
                    dve.wait_ge(upd_ready, nupd[u] + 1)
                    dve.wait_ge(ae_ready, u + 1)
                    if lat[u]:
                        dve.wait_ge(num_ready, nlat[u] + 1)
                    if u >= 2 * MH:
                        dve.wait_ge(c_ready, nupd[u - 2 * MH + 1])
                    for t in range(2):
                        last = nc.vector.scalar_tensor_tensor(cs[:, t, :], cs[:, t, :], AE[p][:, end:end + 1],
                                                              e.bank[6 + t][:, 0:NV], ALU.mult, ALU.add)
                    last.then_inc(c_ready, 1)
                if lat[u]:
                    n = nlat[u]
                    dve.wait_ge(abs_ready, n + 1)
                    dve.wait_ge(ae_ready, u + 1)
                    nc.vector.tensor_tensor(DEN[p][:, :], DEN[p][:, :], AE[p][:, P:2 * P], ALU.max).then_inc(max_ready, 1)
                    dve.wait_ge(max_ready, n + 1)
                    nc.vector.reciprocal(RD[p][:, :], DEN[p][:, :]).then_inc(rd_ready, 1)
                    dve.wait_ge(rd_ready, n + 1)
                    dst = HT[:, 2 * h:2 * h + 2, c:c + P]
                    fresh = (d == 0) == (c < T // 2)
                    for t in range(2):
                        out = dst[:, t, :] if fresh else HTMP[p][:, t * P:(t + 1) * P]
                        last = nc.vector.tensor_tensor(out, e.bank[4 + p][:, t * P:(t + 1) * P], RD[p][:, :], ALU.mult)
                    if fresh:
                        last.then_inc(h_ready, 1)
                    else:
                        last.then_inc(mul_ready, 1)
                        dve.wait_ge(mul_ready, sum(1 for x in range(u + 1) if lat[x] and (units[x][2] == 0) != (
                            STEPS[units[x][2]][units[x][0]][0] < T // 2)))
                        nc.vector.tensor_tensor(dst, dst, HTMP[p][:, :].rearrange("p (t c) -> p t c", t=2), ALU.add
                                                ).then_inc(h_ready, 1)

            first(0)
            for u in range(len(units)):
                if u + 1 < len(units):
                    first(u + 1)
                second(u)
    st.close()


def fourier(e, XF, yh, yl, at, uh, ul):
    st = Stage(e, "four")
    nc = e.nc
    dft_t = st.sb("dft_t", [P, 2, NCH, T], at)
    dft_c = st.sb("dft_c", [P, 2, P], at + 49152)
    AB = st.sb("ab", [P, 2, 4, T], at + 16384)
    y = [st.sb(f"y{r}", [P, T], TMP + r * T * 4) for r in range(2)]
    const_in, ab_psum, ab_ready, y_psum, y_ready, hi_ready, lo_ready, u_in = (
        st.sem(n) for n in ("const_in", "ab_psum", "ab_ready", "y_psum", "y_ready", "hi_ready", "lo_ready", "u_in"))
    with nc.Block() as block:
        @block.sync
        def _(sp):
            sp.dma_start(dft_t[:, :, :, :], e.dram["dft_t"]).then_inc(const_in, 16)
            sp.dma_start(dft_c[:, :, :], e.dram["dft_c"]).then_inc(const_in, 16)
            sp.dma_start(uh[:, :, :].bitcast(F32), e.dram["uh_s"]).then_inc(u_in, 16)
            sp.dma_start(ul[:, :, :].bitcast(F32), e.dram["ul_s"]).then_inc(u_in, 16)
            sp.wait_ge(u_in, 32)

        @block.tensor
        def _(pe):
            pe.wait_ge(const_in, 32)
            for n in range(8):
                gc, s = n // 2, n % 2
                if n >= 2:
                    pe.wait_ge(ab_ready, n - 1)
                for t in range(NCH):
                    last = nc.tensor.matmul(e.bank[n % 2][:, :], XF[:, t, gc * P:(gc + 1) * P], dft_t[:, s, t, :],
                                            start=t == 0, stop=t == NCH - 1)
                last.then_inc(ab_psum, 1)
            for gc in range(4):
                pe.wait_ge(ab_ready, 2 * gc + 2)
                if gc >= 2:
                    pe.wait_ge(y_ready, gc - 1)
                for s in range(2):
                    last = nc.tensor.matmul(e.bank[2 + gc % 2][:, :], dft_c[:, s, :], AB[:, s, gc, :],
                                            start=s == 0, stop=s == 1)
                last.then_inc(y_psum, 1)

        @block.scalar
        def _(act):
            for n in range(8):
                act.wait_ge(ab_psum, n + 1)
                nc.scalar.activation(AB[:, n % 2, n // 2, :], e.bank[n % 2][:, :], ACT.Copy).then_inc(ab_ready, 1)
            for gc in range(4):
                act.wait_ge(y_ready, gc + 1)
                nc.scalar.activation(yh[:, gc, :], y[gc % 2][:, :], ACT.Copy).then_inc(hi_ready, 1)

        @block.vector
        def _(dve):
            for gc in range(4):
                dve.wait_ge(y_psum, gc + 1)
                nc.vector.tensor_copy(y[gc % 2][:, :], e.bank[2 + gc % 2][:, :]).then_inc(y_ready, 1)
                dve.wait_ge(hi_ready, gc + 1)
                nc.vector.tensor_tensor(yl[:, gc, :], y[gc % 2][:, :], yh[:, gc, :].bitcast(F32), ALU.subtract
                                        ).then_inc(lo_ready, 1)
    st.close()


def column_of(e, at, i, n):
    return e.params[:, at + 2 * i + n:at + 2 * i + n + 1] if isinstance(i, int) else e.params[:, ds(at + n + 2 * i, 1)]


def tile2(t, i, n):
    return t[:, 2 * i + n, :] if isinstance(i, int) else t[:, ds(n + 2 * i, 1), :].rearrange("p a w -> p (a w)")


def gemm_act(e, seg, xh, xl, out, func, bias=None):
    def act_body(act, i, p, g):
        act.wait_ge(e.slot_done, g + 1)
        for n in range(2):
            b = {} if bias is None else {"bias": column_of(e, PARAM_AT[bias], i, n)}
            last = e.nc.scalar.activation(tile2(out, i, n), e.bank[2 * p + n][:, :], func, **b)
        last.then_inc(e.acc_free, 1)

    gemm(e, seg, seg, lambda p: pe_feature_major(e, p, KT, 2, xh, xl, False), act_body=act_body)


def gemm_gate(e, seg, kt, xh, xl, gate):
    def dve_body(dve, i, p, g):
        dve.wait_ge(e.slot_done, g + 1)
        for n in range(2):
            t = tile2(gate, i, n)
            last = e.nc.vector.tensor_tensor(t, t, e.bank[2 * p + n][:, :], ALU.mult)
        last.then_inc(e.acc_free, 1)

    gemm(e, seg, seg, lambda p: pe_feature_major(e, p, kt, 2, xh, xl, False), dve_body=dve_body)


def gemm_gate_split(e, seg, xh, xl, gate, other, yh, yl):
    st = Stage(e, seg + "_s")
    nc = e.nc
    t = [st.sb(f"t{r}", [P, T], TMP + r * T * 4) for r in range(2)]
    v = [st.sb(f"v{r}", [P, T], TMP + (2 + r) * T * 4) for r in range(2)]
    v_ready, hi_ready, lo_ready = (st.sem(n) for n in ("v_ready", "hi_ready", "lo_ready"))

    def act_body(act, i, p, g):
        act.wait_ge(v_ready, 1 + i)
        for n in range(2):
            last = nc.scalar.activation(tile2(yh, i, n), v[n][:, :], ACT.Copy)
        last.then_inc(hi_ready, 1)

    def dve_body(dve, i, p, g):
        dve.wait_ge(e.slot_done, g + 1)
        for n in range(2):
            last = nc.vector.tensor_tensor(t[n][:, :], tile2(gate, i, n), e.bank[2 * p + n][:, :], ALU.mult)
        last.then_inc(e.acc_free, 1)
        dve.wait_ge(e.acc_free, g + 1)
        for n in range(2):
            last = nc.vector.tensor_tensor(v[n][:, :], t[n][:, :], tile2(other, i, n), ALU.add)
        last.then_inc(v_ready, 1)
        dve.wait_ge(hi_ready, 1 + i)
        for n in range(2):
            last = nc.vector.tensor_tensor(tile2(yl, i, n), v[n][:, :], tile2(yh, i, n).bitcast(F32), ALU.subtract)
        last.then_inc(lo_ready, 1)

    gemm(e, seg, seg, lambda p: pe_feature_major(e, p, KT, 2, xh, xl, False), act_body=act_body, dve_body=dve_body)
    st.close()


def gemm_copy(e, seg, xh, xl, out):
    def dve_body(dve, i, p, g):
        dve.wait_ge(e.slot_done, g + 1)
        for n in range(2):
            last = e.nc.vector.tensor_copy(tile2(out, i, n), e.bank[2 * p + n][:, :])
        last.then_inc(e.acc_free, 1)

    gemm(e, seg, seg, lambda p: pe_feature_major(e, p, KT, 2, xh, xl, False), dve_body=dve_body)


def head_norm(e, name, x, per, gain, gate, oh, ol):
    st = Stage(e, name)
    nc = e.nc
    sq, r, t, v = ([st.sb(f"{n}{b}", [P, T], TMP + (2 * m + b) * T * 4) for b in range(2)]
                   for m, n in enumerate(("sq", "r", "t", "v")))
    squared, mean_ready, std_ready, rstd_ready, t_ready, v_ready, hi_ready, lo_ready = (
        st.sem(n) for n in ("squared", "mean_ready", "std_ready", "rstd_ready", "t_ready", "v_ready", "hi_ready",
                            "lo_ready"))
    with nc.Block() as block:
        @block.tensor
        def _(pe):
            for k in range(KT):
                h = k // per
                pe.wait_ge(squared, k + 1)
                if h >= 2:
                    pe.wait_ge(std_ready, h - 1)
                last = nc.tensor.matmul(e.bank[h % 2][:, :], e.ones[:, :], sq[k % 2][:, :],
                                        start=k % per == 0, stop=k % per == per - 1)
                last.then_inc(mean_ready, 1)

        @block.scalar
        def _(act):
            def square(k):
                if k >= 2:
                    act.wait_ge(mean_ready, k - 1)
                nc.scalar.activation(sq[k % 2][:, :], x[:, k, :], ACT.Square).then_inc(squared, 1)

            def hi(k):
                act.wait_ge(v_ready, k + 1)
                nc.scalar.activation(oh[:, k, :], v[k % 2][:, :], ACT.Copy).then_inc(hi_ready, 1)

            for k in range(per):
                square(k)
            for h in range(KT // per):
                act.wait_ge(mean_ready, per * (h + 1))
                if h >= 2:
                    act.wait_ge(t_ready, per * (h - 1))
                nc.scalar.activation(r[h % 2][:, :], e.bank[h % 2][:, :], ACT.Sqrt, scale=1.0 / (per * P),
                                     bias=e.eps[:, 0:1]).then_inc(std_ready, 1)
                for k in range(per * (h + 1), min(per * (h + 2), KT)):
                    square(k)
                for k in range(per * h, per * (h + 1)):
                    hi(k)

        @block.vector
        def _(dve):
            for h in range(KT // per):
                dve.wait_ge(std_ready, h + 1)
                nc.vector.reciprocal(r[h % 2][:, :], r[h % 2][:, :]).then_inc(rstd_ready, 1)
                dve.wait_ge(rstd_ready, h + 1)
                for k in range(per * h, per * (h + 1)):
                    nc.vector.scalar_tensor_tensor(t[k % 2][:, :], x[:, k, :], gain(k), r[h % 2][:, :],
                                                   ALU.mult, ALU.mult).then_inc(t_ready, 1)
                    dve.wait_ge(t_ready, k + 1)
                    if k >= 2:
                        dve.wait_ge(hi_ready, k - 1)
                    nc.vector.tensor_tensor(v[k % 2][:, :], t[k % 2][:, :], gate[:, k, :], ALU.mult).then_inc(v_ready, 1)
                    dve.wait_ge(hi_ready, k + 1)
                    nc.vector.tensor_tensor(ol[:, k, :], v[k % 2][:, :], oh[:, k, :].bitcast(F32), ALU.subtract
                                            ).then_inc(lo_ready, 1)
    st.close()


def split_stage(e, name, x, xh, xl, store):
    st = Stage(e, name)
    nc = e.nc
    hi_ready, lo_ready, stored = (st.sem(n) for n in ("hi_ready", "lo_ready", "stored"))
    with nc.Block() as block:
        @block.sync
        def _(sp):
            sp.dma_start(store, x[:, :, :]).then_inc(stored, 16)
            sp.wait_ge(stored, 16)

        @block.scalar
        def _(act):
            for k in range(KT):
                nc.scalar.activation(xh[:, k, :], x[:, k, :], ACT.Copy).then_inc(hi_ready, 1)

        @block.vector
        def _(dve):
            for k in range(KT):
                dve.wait_ge(hi_ready, k + 1)
                nc.vector.tensor_tensor(xl[:, k, :], x[:, k, :], xh[:, k, :].bitcast(F32), ALU.subtract
                                        ).then_inc(lo_ready, 1)
    st.close()


def project_2(e, xh, xl, QKV, GR):
    st = Stage(e, "proj2")
    nc = e.nc
    raw = [st.sb(f"raw{n}", [P, T], TMP + n * T * 4) for n in range(2)]
    con = [st.sb(f"con{n}", [P, T], TMP + (2 + n) * T * 4) for n in range(2)]
    tap_done, silu_done, spilled = (st.sem(n) for n in ("tap_done", "silu_done", "spilled"))
    a, b = START["gates2"][0], START["wqkv2"][1]
    conv_w = PARAM_AT["conv_w_2"]
    sp_span, pool_span = feed_ahead(e, b)
    with nc.Block() as block:
        @block.sync
        def _(sp):
            sp.dma_start(e.dram["uh_s"], xh[:, :, :].bitcast(F32)).then_inc(spilled, 16)
            sp.dma_start(e.dram["ul_s"], xl[:, :, :].bitcast(F32)).then_inc(spilled, 16)
            feed_sp(e, sp, sp_span)
            sp.wait_ge(spilled, 32)

        @block.gpsimd
        def _(pool):
            feed_pool(e, pool, pool_span)

        @block.tensor
        def _(pe):
            def fm(ntile):
                def body(nm, i, p, g, ih, gh):
                    pe_slot_begin(e, pe, g)
                    pe_feature_major(e, p, KT, ntile, xh, xl, False).then_inc(e.slot_done, 1)
                return body

            slots(pe, *START["gates2"], fm(1))
            slots(pe, *START["wqkv2"], fm(2))

        @block.scalar
        def _(act):
            act.wait_ge(e.slot_done, a + 1)
            nc.scalar.activation(GR[:, :], e.bank[2 * (a % 2)][:, :], ACT.Copy).then_inc(e.acc_free, 1)

            def body(nm, i, p, g, ih, gh):
                act.wait_ge(e.slot_done, g + 1)
                for n in range(2):
                    last = nc.scalar.activation(raw[n][:, :], e.bank[2 * p + n][:, :], ACT.Copy)
                last.then_inc(e.acc_free, 1)
                for n in range(2):
                    act.wait_ge(tap_done, 4 * n + 4 + 8 * i)
                    nc.scalar.activation(tile2(QKV, i, n), con[n][:, :], ACT.Silu).then_inc(silu_done, 1)

            slots(act, *START["wqkv2"], body)

        @block.vector
        def _(dve):
            def body(nm, i, p, g, ih, gh):
                dve.wait_ge(e.acc_free, g + 1)
                for n in range(2):
                    if not (isinstance(i, int) and i == 0):
                        dve.wait_ge(silu_done, n - 1 + 2 * i)
                    tap = [column_of(e, conv_w + 24 * j, i, n) for j in range(4)]
                    nc.vector.tensor_scalar(con[n][:, :], raw[n][:, :], tap[3], None, ALU.mult).then_inc(tap_done, 1)
                    for back in range(1, 4):
                        dve.wait_ge(tap_done, 4 * n + back + 8 * i)
                        nc.vector.scalar_tensor_tensor(con[n][:, back:], raw[n][:, :T - back], tap[3 - back],
                                                       con[n][:, back:], ALU.mult, ALU.add).then_inc(tap_done, 1)

            g0, g1 = START["wqkv2"]
            slots(dve, g0, g0 + 1, body)
            slots(dve, g0 + 1, g1, body)
    st.close()


def l2_norm(e, QKV):
    st = Stage(e, "l2")
    nc = e.nc
    sq = [st.sb(f"sq{r}", [P, T], TMP + r * T * 4) for r in range(2)]
    r_ = [st.sb(f"r{r}", [P, T], TMP + (2 + r) * T * 4) for r in range(2)]
    squared, sum_ready, std_ready, rstd_ready, done = (
        st.sem(n) for n in ("squared", "sum_ready", "std_ready", "rstd_ready", "done"))
    n = 2 * DNH
    with nc.Block() as block:
        @block.tensor
        def _(pe):
            for k in range(n):
                pe.wait_ge(squared, k + 1)
                if k >= 2:
                    pe.wait_ge(std_ready, k - 1)
                nc.tensor.matmul(e.bank[k % 2][:, :], e.ones[:, :], sq[k % 2][:, :], start=True, stop=True
                                 ).then_inc(sum_ready, 1)

        @block.scalar
        def _(act):
            def square(k):
                if k >= 2:
                    act.wait_ge(sum_ready, k - 1)
                nc.scalar.activation(sq[k % 2][:, :], QKV[:, k, :], ACT.Square).then_inc(squared, 1)

            square(0)
            for k in range(n):
                if k + 1 < n:
                    square(k + 1)
                act.wait_ge(sum_ready, k + 1)
                if k >= 2:
                    act.wait_ge(done, k - 1)
                nc.scalar.activation(r_[k % 2][:, :], e.bank[k % 2][:, :], ACT.Sqrt, bias=e.eps[:, 0:1]
                                     ).then_inc(std_ready, 1)

        @block.vector
        def _(dve):
            for k in range(n):
                dve.wait_ge(std_ready, k + 1)
                nc.vector.reciprocal(r_[k % 2][:, :], r_[k % 2][:, :]).then_inc(rstd_ready, 1)
                dve.wait_ge(rstd_ready, k + 1)
                nc.vector.scalar_tensor_tensor(QKV[:, k, :], QKV[:, k, :], P ** -0.5 if k < DNH else 1.0, r_[k % 2][:, :],
                                               ALU.mult, ALU.mult).then_inc(done, 1)
    st.close()


def delta_rows(e, GR, R, SEL, QKV, QD, COL, GL):
    st = Stage(e, "drows")
    nc = e.nc
    H = DNH
    x, t1, t2, zero = (st.sb(n, [H, T], TMP + m * T * 4) for m, n in enumerate(("x", "t1", "t2", "zero")))
    eg = [st.sb(f"eg{b}", [P, T], TMP + (4 + b) * T * 4) for b in range(2)]
    ea = st.sb("ea", [H, 1], TMP + 6 * T * 4)
    sel_in, x_ready, abs_ready, exp_ready, ln_ready, act_ready, g_ready, eg_row, be_ready, kd_pre, kd_ready, col_psum, \
        col_ready, g_psum, eg_ready, qd_ready, chain = (st.sem(n) for n in (
            "sel_in", "x_ready", "abs_ready", "exp_ready", "ln_ready", "act_ready", "g_ready", "eg_row", "be_ready",
            "kd_pre", "kd_ready", "col_psum", "col_ready", "g_psum", "eg_ready", "qd_ready", "chain"))
    db, al = PARAM_AT["dt_bias"], PARAM_AT["a_log"]
    with nc.Block() as block:
        @block.sync
        def _(sp):
            sp.dma_start(SEL[:, :], e.dram["sel8"]).then_inc(sel_in, 16)
            sp.wait_ge(sel_in, 16)

        @block.scalar
        def _(act):
            nc.scalar.activation(x[:, :], GR[0:H, :], ACT.Identity, bias=e.params[0:H, db:db + 1]).then_inc(x_ready, 1)
            act.wait_ge(x_ready, 1)
            nc.scalar.activation(t1[:, :], x[:, :], ACT.Abs).then_inc(abs_ready, 1)
            act.wait_ge(abs_ready, 1)
            nc.scalar.activation(t2[:, :], t1[:, :], ACT.Exp, scale=-1.0).then_inc(exp_ready, 1)
            nc.scalar.activation(ea[:, :], e.params[0:H, al:al + 1], ACT.Exp)
            act.wait_ge(exp_ready, 1)
            nc.scalar.activation(t1[:, :], t2[:, :], ACT.Ln, bias=e.one_col[0:H, 0:1]).then_inc(ln_ready, 1)
            nc.scalar.activation(R[:, 1, :], GR[32:32 + H, :], ACT.Sigmoid).then_inc(act_ready, 1)
            act.wait_ge(g_ready, 1)
            nc.scalar.activation(t2[:, :], R[:, 0, :], ACT.Exp).then_inc(eg_row, 1)
            act.wait_ge(kd_pre, 1)
            nc.scalar.activation(R[:, 3, :], x[:, :], ACT.Exp).then_inc(kd_ready, 1)
            for h in range(H):
                act.wait_ge(g_psum, h + 1)
                if h >= 2:
                    act.wait_ge(qd_ready, h - 1)
                nc.scalar.activation(eg[h % 2][:, :], e.bank[2 + h % 2][:, :], ACT.Exp).then_inc(eg_ready, 1)

        @block.tensor
        def _(pe):
            pe.wait_ge(sel_in, 16)
            pe.wait_ge(g_ready, 1)
            for h in range(H):
                if h >= 2:
                    pe.wait_ge(eg_ready, h - 1)
                nc.tensor.matmul(e.bank[2 + h % 2][:, :], SEL[:, h * P:(h + 1) * P], R[:, 0, :], start=True, stop=True
                                 ).then_inc(g_psum, 1)
            pe.wait_ge(be_ready, 1)
            pe.wait_ge(kd_ready, 1)
            for c in range(NCH):
                for r in range(4):
                    at = (c * 4 + r) * H
                    last = nc.tensor.matmul(e.bank[0][:, at:at + H], R[:, r, c * P:(c + 1) * P], e.ident[0:H, 0:H],
                                            start=True, stop=True)
            last.then_inc(col_psum, 1)

        @block.vector
        def _(dve):
            done = [0]

            def link(ins):
                done[0] += 1
                ins.then_inc(chain, 1)
                dve.wait_ge(chain, done[0])

            link(nc.vector.memset(zero[:, :], 0.0))
            dve.wait_ge(ln_ready, 1)
            link(nc.vector.scalar_tensor_tensor(x[:, :], x[:, :], 0.0, t1[:, :], ALU.max, ALU.add))
            link(nc.vector.tensor_scalar(x[:, :], x[:, :], ea[:, 0:1], -1.0, ALU.mult, ALU.mult))
            for c in range(NCH):
                cc = slice(c * P, (c + 1) * P)
                last = nc.vector.tensor_tensor_scan(R[:, 0, cc], zero[:, cc], x[:, cc], 0.0, ALU.add, ALU.add)
            last.then_inc(g_ready, 1)
            dve.wait_ge(g_ready, 1)
            for c in range(NCH):
                cc = slice(c * P, (c + 1) * P)
                last = nc.vector.tensor_scalar(x[:, cc], R[:, 0, cc], R[:, 0, (c + 1) * P - 1:(c + 1) * P], -1.0,
                                               ALU.subtract, ALU.mult)
            last.then_inc(kd_pre, 1)
            dve.wait_ge(act_ready, 1)
            dve.wait_ge(eg_row, 1)
            nc.vector.tensor_tensor(R[:, 2, :], R[:, 1, :], t2[:, :], ALU.mult).then_inc(be_ready, 1)
            for h in range(H):
                dve.wait_ge(eg_ready, h + 1)
                nc.vector.tensor_copy(GL[:, h, :], eg[h % 2][:, P - 1:T:P])
                nc.vector.tensor_tensor(QD[:, h, :], QKV[:, h, :], eg[h % 2][:, :], ALU.mult).then_inc(qd_ready, 1)
            dve.wait_ge(col_psum, 1)
            nc.vector.tensor_copy(COL[:, :], e.bank[0][:, 0:NCH * 4 * H]).then_inc(col_ready, 1)
    st.close()


def delta(e, QKV, QD, R, SEL, COL, GL, LMASK, DMASK, at):
    st = Stage(e, "delta")
    nc = e.nc
    HW = 4 * P
    off = [at]

    def halves(n, area=None):
        if area is not None:
            return [st.sb(f"{n}{x}", [P, HW], area + x * HW * 4) for x in range(2)]
        out = [st.sb(f"{n}{x}", [P, HW], off[0] + x * HW * 4) for x in range(2)]
        off[0] += 2 * HW * 4
        return out

    N, QK, X, XT, PB, LM, KD, KBE, VB, S = (halves(n) for n in ("n", "qk", "x", "xt", "pb", "lm", "kd", "kbe", "vb",
                                                               "s"))
    DA, DB, EA, EB = (halves(n, TMP + m * 2 * HW * 4) for m, n in enumerate(("da", "db", "ea", "eb")))
    names = ("mask_in", "zeroed", "gram", "tok", "dec", "dec_exp", "qk_ready", "n_ready", "scaled", "l1", "x1", "xt_psum",
             "xt1", "lm_ready", "p_psum", "p_ready", "xy_psum", "x_ready", "uw_psum", "uw_ready", "ws_psum", "vn_ready",
             "o_psum", "o_ready", "s_ready")
    s = {n: st.sem(n) for n in names}
    LEVELS = 7

    def head(buf, n):
        return buf[:, n * P:(n + 1) * P]

    def col(c, r, h):
        return COL[:, (c * 4 + r) * DNH + h:(c * 4 + r) * DNH + h + 1]

    def mask(m):
        return LMASK[:, m * P:(m + 1) * P].unsqueeze(1).to_broadcast([P, 4, P])

    def four(buf):
        return buf[:, :].rearrange("p (h c) -> p h c", h=4)

    with nc.Block() as block:
        @block.sync
        def _(sp):
            sp.dma_start(LMASK[:, :], e.dram["level_mask"]).then_inc(s["mask_in"], 16)
            sp.dma_start(DMASK[:, :], e.dram["decay_mask"]).then_inc(s["mask_in"], 16)
            sp.wait_ge(s["mask_in"], 32)

        @block.tensor
        def _(pe):
            for c in range(NCH):
                cc = slice(c * P, (c + 1) * P)
                for x in range(2):
                    u = 2 * c + x
                    b = 3 * x
                    if c:
                        pe.wait_ge(s["o_ready"], u - 1)
                        pe.wait_ge(s["s_ready"], u - 1)
                    for n in range(4):
                        h = 4 * x + n
                        q, k = QKV[:, h, cc], QKV[:, DNH + h, cc]
                        nc.tensor.matmul(head(e.bank[b], n), k, k, start=True, stop=True)
                        nc.tensor.matmul(head(e.bank[b + 1], n), k, q, start=True, stop=True)
                        last = nc.tensor.matmul(head(e.bank[b + 2], n), SEL[:, h * P:(h + 1) * P], R[:, 0, cc],
                                                start=True, stop=True)
                    last.then_inc(s["gram"], 1)
                    if u:
                        pe.wait_ge(s["scaled"], u)
                    for n in range(4):
                        h = 4 * x + n
                        nc.tensor.transpose(head(e.bank[6], n), QKV[:, DNH + h, cc], e.ident[:, :])
                        last = nc.tensor.transpose(head(e.bank[7], n), QKV[:, 2 * DNH + h, cc], e.ident[:, :])
                    last.then_inc(s["tok"], 1)
                for x in range(2):
                    u = 2 * c + x
                    pe.wait_ge(s["x1"], u + 1)
                    for n in range(4):
                        last = nc.tensor.transpose(head(e.bank[3 * x], n), head(X[x], n), e.ident[:, :])
                    last.then_inc(s["xt_psum"], 1)
                for m in range(1, LEVELS):
                    for x in range(2):
                        step = (c * (LEVELS - 1) + m - 1) * 2 + x
                        pe.wait_ge(s["lm_ready"], step + 1)
                        if m == 1:
                            pe.wait_ge(s["xt1"], 2 * c + x + 1)
                        else:
                            pe.wait_ge(s["x_ready"], step - 1)
                        for n in range(4):
                            last = nc.tensor.matmul(head(e.bank[3 * x], n), head(LM[x], n), head(XT[x], n),
                                                    start=True, stop=True)
                        last.then_inc(s["p_psum"], 1)
                    for x in range(2):
                        step = (c * (LEVELS - 1) + m - 1) * 2 + x
                        pe.wait_ge(s["p_ready"], step + 1)
                        for n in range(4):
                            last = nc.tensor.matmul(head(e.bank[3 * x + 1], n), head(X[x], n), head(PB[x], n),
                                                    start=True, stop=True)
                            if m < LEVELS - 1:
                                last = nc.tensor.matmul(head(e.bank[3 * x + 2], n), head(PB[x], n), head(X[x], n),
                                                        start=True, stop=True)
                        last.then_inc(s["xy_psum"], 1)
                for x in range(2):
                    u = 2 * c + x
                    pe.wait_ge(s["x_ready"], (c + 1) * (LEVELS - 1) * 2 - 1 + x)
                    pe.wait_ge(s["scaled"], u + 1)
                    for n in range(4):
                        nc.tensor.matmul(head(e.bank[3 * x], n), head(XT[x], n), head(VB[x], n), start=True, stop=True)
                        last = nc.tensor.matmul(head(e.bank[3 * x + 1], n), head(KBE[x], n), head(XT[x], n),
                                                start=True, stop=True)
                    last.then_inc(s["uw_psum"], 1)
                for x in range(2):
                    u = 2 * c + x
                    pe.wait_ge(s["uw_ready"], u + 1)
                    if c:
                        pe.wait_ge(s["s_ready"], u - 1)
                    else:
                        pe.wait_ge(s["zeroed"], 1)
                    for n in range(4):
                        last = nc.tensor.matmul(head(e.bank[3 * x + 2], n), head(KBE[x], n), head(S[x], n),
                                                start=True, stop=True)
                    last.then_inc(s["ws_psum"], 1)
                for x in range(2):
                    u = 2 * c + x
                    pe.wait_ge(s["vn_ready"], u + 1)
                    pe.wait_ge(s["qk_ready"], u + 1)
                    for n in range(4):
                        nc.tensor.matmul(head(e.bank[3 * x], n), head(S[x], n), QD[:, 4 * x + n, cc],
                                         start=True, stop=False)
                        nc.tensor.matmul(head(e.bank[3 * x], n), head(PB[x], n), head(QK[x], n),
                                         start=False, stop=True)
                        last = nc.tensor.matmul(head(e.bank[3 * x + 1], n), head(KD[x], n), head(PB[x], n),
                                                start=True, stop=True)
                    last.then_inc(s["o_psum"], 1)

        @block.scalar
        def _(act):
            for c in range(NCH):
                for x in range(2):
                    u = 2 * c + x
                    act.wait_ge(s["dec"], u + 1)
                    nc.scalar.activation(EA[x][:, :], DA[x][:, :], ACT.Exp)
                    nc.scalar.activation(EB[x][:, :], DB[x][:, :], ACT.Exp, scale=-1.0).then_inc(s["dec_exp"], 1)
                    act.wait_ge(s["tok"], u + 1)
                    for n in range(4):
                        h = 4 * x + n
                        nc.scalar.activation(head(KD[x], n), head(e.bank[6], n), ACT.Copy, scale=col(c, 3, h))
                        nc.scalar.activation(head(KBE[x], n), head(e.bank[6], n), ACT.Copy, scale=col(c, 2, h))
                        last = nc.scalar.activation(head(VB[x], n), head(e.bank[7], n), ACT.Copy, scale=col(c, 1, h))
                    last.then_inc(s["scaled"], 1)
                for x in range(2):
                    act.wait_ge(s["xt_psum"], 2 * c + x + 1)
                    nc.scalar.activation(XT[x][:, :], e.bank[3 * x][:, :], ACT.Copy).then_inc(s["xt1"], 1)
                for m in range(1, LEVELS):
                    for x in range(2):
                        step = (c * (LEVELS - 1) + m - 1) * 2 + x
                        act.wait_ge(s["p_psum"], step + 1)
                        nc.scalar.activation(PB[x][:, :], e.bank[3 * x][:, :], ACT.Copy).then_inc(s["p_ready"], 1)
                for x in range(2):
                    act.wait_ge(s["uw_psum"], 2 * c + x + 1)
                    nc.scalar.activation(VB[x][:, :], e.bank[3 * x][:, :], ACT.Copy)
                    nc.scalar.activation(KBE[x][:, :], e.bank[3 * x + 1][:, :], ACT.Copy).then_inc(s["uw_ready"], 1)
                for x in range(2):
                    act.wait_ge(s["o_psum"], 2 * c + x + 1)
                    nc.scalar.activation(QKV[:, 2 * DNH + 4 * x:2 * DNH + 4 * x + 4, c * P:(c + 1) * P],
                                         four(e.bank[3 * x]), ACT.Copy).then_inc(s["o_ready"], 1)

        @block.vector
        def _(dve):
            nc.vector.memset(S[0][:, :], 0.0)
            nc.vector.memset(S[1][:, :], 0.0).then_inc(s["zeroed"], 1)
            dve.wait_ge(s["mask_in"], 32)
            dve.wait_ge(s["zeroed"], 1)
            for c in range(NCH):
                for x in range(2):
                    u = 2 * c + x
                    dve.wait_ge(s["gram"], u + 1)
                    for n in range(4):
                        h = 4 * x + n
                        nc.vector.scalar_tensor_tensor(head(DA[x], n), head(e.bank[3 * x + 2], n), col(c, 0, h),
                                                       DMASK[:, 0:P], ALU.subtract, ALU.add)
                        last = nc.vector.scalar_tensor_tensor(head(DB[x], n), head(e.bank[3 * x + 2], n), col(c, 0, h),
                                                              DMASK[:, P:2 * P], ALU.subtract, ALU.add)
                    last.then_inc(s["dec"], 1)
                    dve.wait_ge(s["dec_exp"], u + 1)
                    nc.vector.tensor_tensor(QK[x][:, :], e.bank[3 * x + 1][:, :], EA[x][:, :], ALU.mult
                                            ).then_inc(s["qk_ready"], 1)
                    for n in range(4):
                        last = nc.vector.scalar_tensor_tensor(head(N[x], n), head(e.bank[3 * x], n), col(c, 1, 4 * x + n),
                                                              head(EB[x], n), ALU.mult, ALU.mult)
                    last.then_inc(s["n_ready"], 1)
                    dve.wait_ge(s["n_ready"], u + 1)
                    nc.vector.tensor_tensor(four(LM[x]), four(N[x]), mask(0), ALU.mult).then_inc(s["l1"], 1)
                    dve.wait_ge(s["l1"], u + 1)
                    nc.vector.scalar_tensor_tensor(four(X[x]), four(LM[x]), -1.0,
                                                   e.ident[:, :].unsqueeze(1).to_broadcast([P, 4, P]),
                                                   ALU.mult, ALU.add).then_inc(s["x1"], 1)
                for x in range(2):
                    dve.wait_ge(s["x1"], 2 * c + x + 1)
                    nc.vector.tensor_tensor(four(LM[x]), four(N[x]), mask(1), ALU.mult).then_inc(s["lm_ready"], 1)
                for m in range(1, LEVELS):
                    for x in range(2):
                        step = (c * (LEVELS - 1) + m - 1) * 2 + x
                        dve.wait_ge(s["xy_psum"], step + 1)
                        if m + 1 < LEVELS:
                            nc.vector.tensor_tensor(four(LM[x]), four(N[x]), mask(m + 1), ALU.mult
                                                    ).then_inc(s["lm_ready"], 1)
                            nc.vector.tensor_tensor(X[x][:, :], X[x][:, :], e.bank[3 * x + 2][:, :], ALU.subtract)
                        nc.vector.tensor_tensor(XT[x][:, :], XT[x][:, :], e.bank[3 * x + 1][:, :], ALU.subtract
                                                ).then_inc(s["x_ready"], 1)
                for x in range(2):
                    u = 2 * c + x
                    dve.wait_ge(s["ws_psum"], u + 1)
                    dve.wait_ge(s["uw_ready"], u + 1)
                    nc.vector.tensor_tensor(PB[x][:, :], VB[x][:, :], e.bank[3 * x + 2][:, :], ALU.subtract
                                            ).then_inc(s["vn_ready"], 1)
                for x in range(2):
                    u = 2 * c + x
                    dve.wait_ge(s["o_psum"], u + 1)
                    for n in range(4):
                        last = nc.vector.scalar_tensor_tensor(head(S[x], n), head(S[x], n), GL[:, 4 * x + n, c:c + 1],
                                                              head(e.bank[3 * x + 1], n), ALU.mult, ALU.add)
                    last.then_inc(s["s_ready"], 1)
    st.close()


def reload(e, name, uh, ul):
    st = Stage(e, name)
    back = st.sem("back")
    with e.nc.Block() as block:
        @block.sync
        def _(sp):
            sp.dma_start(uh[:, :, :].bitcast(F32), e.dram["uh_s"]).then_inc(back, 16)
            sp.dma_start(ul[:, :, :].bitcast(F32), e.dram["ul_s"]).then_inc(back, 16)
            sp.wait_ge(back, 32)
    st.close()


def sgu_values(e, xh, xl, VT, LNP):
    st = Stage(e, "sguv")
    nc = e.nc
    stats = st.sb("stats", [P, NCH, 2, 6], TMP)
    mv = st.sb("mv", [P, NCH, 2], TMP + 256)
    rs = st.sb("rs", [P, NCH], TMP + 320)
    nrm = [st.sb(f"nrm{r}", [P, D], TMP + 1024 + r * D * 4) for r in range(2)]
    ln_in, gelu_done, var_ready, std_ready, chain = (st.sem(n) for n in ("ln_in", "gelu_done", "var_ready", "std_ready",
                                                                        "chain"))
    a, b = START["wv2"]
    sp_span, pool_span = feed_ahead(e, b)
    with nc.Block() as block:
        @block.sync
        def _(sp):
            sp.dma_start(LNP[:, :], e.dram["sgu_ln"]).then_inc(ln_in, 16)
            feed_sp(e, sp, sp_span)
            sp.wait_ge(ln_in, 16)

        @block.gpsimd
        def _(pool):
            feed_pool(e, pool, pool_span)

        @block.tensor
        def _(pe):
            def body(nm, i, p, g, ih, gh):
                pe_slot_begin(e, pe, g)
                pe_token_major(e, p, 256, xh, xl, False).then_inc(e.slot_done, 1)
            slots(pe, a, b, body)

        @block.scalar
        def _(act):
            def body(nm, i, p, g, ih, gh):
                act.wait_ge(e.slot_done, g + 1)
                cols = slice(256 * i, 256 * i + 256) if isinstance(i, int) else ds(256 * i, 256)
                for t in range(NCH):
                    last = nc.scalar.activation(VT[:, t, cols], e.bank[2 * p + t // 2][:, (t % 2) * 256:(t % 2 + 1) * 256],
                                                ACT.Gelu)
                last.then_inc(e.acc_free, 1)
            slots(act, a, b, body)
            act.wait_ge(var_ready, 1)
            nc.scalar.activation(rs[:, :], mv[:, :, 1], ACT.Sqrt, bias=e.eps[:, 1:2]).then_inc(std_ready, 1)

        @block.vector
        def _(dve):
            done = [0]

            def link(ins):
                done[0] += 1
                ins.then_inc(chain, 1)
                dve.wait_ge(chain, done[0])

            dve.wait_ge(e.acc_free, b)
            for t in range(NCH):
                for half in range(2):
                    last = nc.vector.bn_stats(stats[:, t, half, :], VT[:, t, half * 512:(half + 1) * 512])
            link(last)
            for t in range(NCH):
                last = nc.vector.bn_aggr(mv[:, t, :], stats[:, t, :, :].rearrange("p a b -> p (a b)"))
            last.then_inc(var_ready, 1)
            dve.wait_ge(std_ready, 1)
            link(nc.vector.reciprocal(rs[:, :], rs[:, :]))
            dve.wait_ge(ln_in, 16)
            for t in range(NCH):
                link(nc.vector.tensor_scalar(nrm[0][:, :], VT[:, t, :], mv[:, t, 0:1], rs[:, t:t + 1],
                                             ALU.subtract, ALU.mult))
                link(nc.vector.tensor_tensor(nrm[1][:, :], nrm[0][:, :], LNP[:, 0:D], ALU.mult))
                link(nc.vector.tensor_tensor(VT[:, t, :], nrm[1][:, :], LNP[:, D:2 * D], ALU.add))
    st.close()


def spatial(e, VT, UG, WS, SB, gh, gl):
    st = Stage(e, "spat")
    nc = e.nc
    G8 = D // P
    wm = st.sb("wm", [P, G8, P], TMP)
    msk = st.sb("msk", [P, P], TMP + 4096)
    t = [st.sb(f"t{r}", [P, T], TMP + 4608 + r * T * 4) for r in range(2)]
    v = [st.sb(f"v{r}", [P, T], TMP + 4608 + (2 + r) * T * 4) for r in range(2)]
    ws_in, w_ready, mixed, t_ready, v_ready, hi_ready, lo_ready = (
        st.sem(n) for n in ("ws_in", "w_ready", "mixed", "t_ready", "v_ready", "hi_ready", "lo_ready"))
    with nc.Block() as block:
        @block.sync
        def _(sp):
            sp.dma_start(WS[:, :, :], e.dram["spatial_w"]).then_inc(ws_in, 16)
            sp.dma_start(SB[:, :, :], e.dram["spatial_b"]).then_inc(ws_in, 16)
            sp.dma_start(msk[:, :], e.dram["causal"]).then_inc(ws_in, 16)
            sp.wait_ge(ws_in, 48)

        @block.tensor
        def _(pe):
            pe.wait_ge(w_ready, 1)
            for g in range(G8):
                if g >= 2:
                    pe.wait_ge(t_ready, g - 1)
                for c in range(NCH):
                    last = nc.tensor.matmul(e.bank[g % 2][:, c * P:(c + 1) * P], VT[:, c, g * P:(g + 1) * P],
                                            wm[:, g, :], start=True, stop=True)
                last.then_inc(mixed, 1)

        @block.scalar
        def _(act):
            for g in range(G8):
                act.wait_ge(v_ready, g + 1)
                nc.scalar.activation(gh[:, g, :], v[g % 2][:, :], ACT.Copy).then_inc(hi_ready, 1)

        @block.vector
        def _(dve):
            dve.wait_ge(ws_in, 48)
            nc.vector.tensor_tensor(wm[:, :, :], WS[:, :, :], msk[:, :].unsqueeze(1).to_broadcast([P, G8, P]),
                                    ALU.mult).then_inc(w_ready, 1)
            for g in range(G8):
                dve.wait_ge(mixed, g + 1)
                nc.vector.tensor_tensor(t[g % 2][:, :].rearrange("p (c t) -> p c t", c=NCH),
                                        e.bank[g % 2][:, :].rearrange("p (c t) -> p c t", c=NCH),
                                        SB[:, g, :].unsqueeze(1).to_broadcast([P, NCH, P]), ALU.add).then_inc(t_ready, 1)
                dve.wait_ge(t_ready, g + 1)
                if g >= 2:
                    dve.wait_ge(hi_ready, g - 1)
                nc.vector.tensor_tensor(v[g % 2][:, :], t[g % 2][:, :], UG[:, g, :], ALU.mult).then_inc(v_ready, 1)
                dve.wait_ge(hi_ready, g + 1)
                nc.vector.tensor_tensor(gl[:, g, :], v[g % 2][:, :], gh[:, g, :].bitcast(F32), ALU.subtract
                                        ).then_inc(lo_ready, 1)
    st.close()


def deep_norm(e, name, y, res, load, gain, shift, split=None, store=None):
    st = Stage(e, name)
    nc = e.nc
    sq, t = ([st.sb(f"{n}{r}", [P, T], TMP + (2 * m + r) * T * 4) for r in range(2)] for m, n in enumerate(("sq", "t")))
    acc, var, rstd = (st.sb(n, [P, T], TMP + (4 + m) * T * 4) for m, n in enumerate(("acc", "var", "rstd")))
    res_in, added, summed, mean_ready, centred, squared, sq_summed, var_ready, std_ready, rstd_ready, scaled, out_ready, \
        hi_ready, lo_ready, stored = (st.sem(n) for n in (
            "res_in", "added", "summed", "mean_ready", "centred", "squared", "sq_summed", "var_ready", "std_ready",
            "rstd_ready", "scaled", "out_ready", "hi_ready", "lo_ready", "stored"))
    g_at, b_at = PARAM_AT[gain], PARAM_AT[shift]
    with nc.Block() as block:
        @block.sync
        def _(sp):
            sp.dma_start(res[:, :, :], load).then_inc(res_in, 16)
            sp.wait_ge(out_ready, KT)
            sp.dma_start(store, y[:, :, :]).then_inc(stored, 16)
            sp.wait_ge(stored, 16)

        @block.tensor
        def _(pe):
            pe.wait_ge(summed, KT)
            nc.tensor.matmul(e.bank[6][:, :], e.mean_ones[:, :], acc[:, :], start=True, stop=True
                             ).then_inc(mean_ready, 1)
            pe.wait_ge(sq_summed, KT)
            nc.tensor.matmul(e.bank[7][:, :], e.mean_ones[:, :], var[:, :], start=True, stop=True
                             ).then_inc(var_ready, 1)

        @block.scalar
        def _(act):
            for k in range(KT):
                act.wait_ge(centred, k + 1)
                if k >= 2:
                    act.wait_ge(sq_summed, k - 1)
                nc.scalar.activation(sq[k % 2][:, :], y[:, k, :], ACT.Square).then_inc(squared, 1)
            act.wait_ge(var_ready, 1)
            nc.scalar.activation(rstd[:, :], e.bank[7][:, :], ACT.Sqrt, bias=e.eps[:, 1:2]).then_inc(std_ready, 1)
            for k in range(KT):
                act.wait_ge(scaled, k + 1)
                nc.scalar.activation(y[:, k, :], t[k % 2][:, :], ACT.Identity, bias=e.params[:, b_at + k:b_at + k + 1]
                                     ).then_inc(out_ready, 1)
                if split is not None:
                    act.wait_ge(out_ready, k + 1)
                    nc.scalar.activation(split[0][:, k, :], y[:, k, :], ACT.Copy).then_inc(hi_ready, 1)

        @block.vector
        def _(dve):
            dve.wait_ge(res_in, 16)
            for k in range(KT):
                nc.vector.scalar_tensor_tensor(y[:, k, :], res[:, k, :], ALPHA, y[:, k, :], ALU.mult, ALU.add
                                               ).then_inc(added, 1)
            for k in range(KT):
                dve.wait_ge(added, k + 1)
                if k == 0:
                    nc.vector.tensor_copy(acc[:, :], y[:, 0, :]).then_inc(summed, 1)
                else:
                    dve.wait_ge(summed, k)
                    nc.vector.tensor_tensor(acc[:, :], acc[:, :], y[:, k, :], ALU.add).then_inc(summed, 1)
            dve.wait_ge(mean_ready, 1)
            for k in range(KT):
                nc.vector.tensor_tensor(y[:, k, :], y[:, k, :], e.bank[6][:, :], ALU.subtract).then_inc(centred, 1)
            for k in range(KT):
                dve.wait_ge(squared, k + 1)
                if k == 0:
                    nc.vector.tensor_copy(var[:, :], sq[0][:, :]).then_inc(sq_summed, 1)
                else:
                    dve.wait_ge(sq_summed, k)
                    nc.vector.tensor_tensor(var[:, :], var[:, :], sq[k % 2][:, :], ALU.add).then_inc(sq_summed, 1)
            dve.wait_ge(std_ready, 1)
            nc.vector.reciprocal(rstd[:, :], rstd[:, :]).then_inc(rstd_ready, 1)
            dve.wait_ge(rstd_ready, 1)

            def scale(k):
                if k >= 2:
                    dve.wait_ge(out_ready, k - 1)
                nc.vector.scalar_tensor_tensor(t[k % 2][:, :], y[:, k, :], e.params[:, g_at + k:g_at + k + 1], rstd[:, :],
                                               ALU.mult, ALU.mult).then_inc(scaled, 1)

            scale(0)
            for k in range(KT):
                if k + 1 < KT:
                    scale(k + 1)
                if split is not None:
                    dve.wait_ge(hi_ready, k + 1)
                    nc.vector.tensor_tensor(split[1][:, k, :], y[:, k, :], split[0][:, k, :].bitcast(F32), ALU.subtract
                                            ).then_inc(lo_ready, 1)
    st.close()


def router(e, xh, xl, CR):
    st = Stage(e, "route")
    nc = e.nc
    a, b = START["router"]
    NG, EG = 4, NE // 4
    off = [TMP]

    def small(n, cols):
        t = st.sb(n, [P, NCH, cols], off[0])
        off[0] += (NCH * cols * 4 + 31) // 32 * 32
        return t

    RB, PRI = st.sb("rb", [P, 32], TMP + 8192), st.sb("pri", [P, 4], TMP + 8192 + 128)
    LG, EX, M1, EQ, MG, IN, TM, MA, MB, M2, ED, SM, GP, W1, W2, CI = (small(n, c) for n, c in (
        ("lg", 32), ("ex", 4), ("m1", 1), ("eq", 4), ("mg", 4), ("in", 4), ("tm", 4), ("ma", 4), ("mb", 4), ("m2", 1),
        ("ed", 1), ("sm", 1), ("gp", 1), ("w1", 1), ("w2", 1), ("ci", 4)))
    CW = small("cw", NE)
    rb_in, e1_pre, e1_ready, e2_pre, e2_ready, cw_ready, cr_psum, cr_ready, chain = (
        st.sem(n) for n in ("rb_in", "e1_pre", "e1_ready", "e2_pre", "e2_ready", "cw_ready", "cr_psum", "cr_ready", "chain"))
    AX = mybir.AxisListType.X
    sp_span, pool_span = feed_ahead(e, b)
    with nc.Block() as block:
        @block.sync
        def _(sp):
            sp.dma_start(RB[:, :], e.dram["router_b"]).then_inc(rb_in, 16)
            sp.dma_start(PRI[:, :], e.dram["priority"]).then_inc(rb_in, 16)
            feed_sp(e, sp, sp_span)
            sp.wait_ge(rb_in, 32)

        @block.gpsimd
        def _(pool):
            feed_pool(e, pool, pool_span)

        @block.tensor
        def _(pe):
            pe_slot_begin(e, pe, a)
            pe_token_major(e, a % 2, 32, xh, xl, False).then_inc(e.slot_done, 1)
            pe.wait_ge(cw_ready, 1)
            for t in range(NCH):
                last = nc.tensor.transpose(e.bank[6][0:NE, t * P:(t + 1) * P], CW[:, t, :], e.ident[:, :])
            last.then_inc(cr_psum, 1)

        @block.scalar
        def _(act):
            act.wait_ge(e1_pre, 1)
            nc.scalar.activation(EX[:, :, :], TM[:, :, :], ACT.Exp).then_inc(e1_ready, 1)
            act.wait_ge(e2_pre, 1)
            nc.scalar.activation(ED[:, :, :], SM[:, :, :], ACT.Exp).then_inc(e2_ready, 1)
            act.wait_ge(cr_psum, 1)
            nc.scalar.activation(CR[:, :], e.bank[6][0:NE, :], ACT.Copy).then_inc(cr_ready, 1)

        @block.vector
        def _(dve):
            done = [0]
            V = nc.vector

            def link(ins):
                done[0] += 1
                ins.then_inc(chain, 1)
                dve.wait_ge(chain, done[0])

            def wide(x, n=4):
                return x.to_broadcast([P, NCH, n])

            pri = PRI[:, :].unsqueeze(1).to_broadcast([P, NCH, 4])

            def first_max(out, logits, top):
                link(V.tensor_tensor(EQ[:, :, :], logits, wide(top[:, :, :]), ALU.is_equal))
                link(V.tensor_tensor(EQ[:, :, :], EQ[:, :, :], pri, ALU.mult))
                link(V.tensor_reduce(M2[:, :, :], EQ[:, :, :], AX, ALU.max))
                link(V.tensor_tensor(out[:, :, :], EQ[:, :, :], wide(M2[:, :, :]), ALU.is_equal))

            dve.wait_ge(e.slot_done, a + 1)
            dve.wait_ge(rb_in, 32)
            p = a % 2
            for t in range(NCH):
                last = V.tensor_tensor(LG[:, t, :], e.bank[2 * p + t // 2][:, (t % 2) * 32:(t % 2 + 1) * 32], RB[:, :],
                                       ALU.add)
            last.then_inc(e.acc_free, 1)
            dve.wait_ge(e.acc_free, a + 1)
            lg = LG[:, :, 0:NG]
            link(V.tensor_reduce(M1[:, :, :], lg, AX, ALU.max))
            V.tensor_tensor(TM[:, :, :], lg, wide(M1[:, :, :]), ALU.subtract).then_inc(e1_pre, 1)
            first_max(MG, lg, M1)
            dve.wait_ge(e1_ready, 1)
            link(V.tensor_reduce(GP[:, :, :], EX[:, :, :], AX, ALU.add))
            for n in range(NG):
                sub = LG[:, :, NG + EG * n:NG + EG * (n + 1)]
                link(V.tensor_tensor(TM[:, :, :] if n else IN[:, :, :], sub, wide(MG[:, :, n:n + 1]), ALU.mult))
                if n:
                    link(V.tensor_tensor(IN[:, :, :], IN[:, :, :], TM[:, :, :], ALU.add))
            link(V.tensor_reduce(M1[:, :, :], IN[:, :, :], AX, ALU.max))
            first_max(MA, IN[:, :, :], M1)
            link(V.scalar_tensor_tensor(IN[:, :, :], MA[:, :, :], -BIG, IN[:, :, :], ALU.mult, ALU.add))
            link(V.tensor_reduce(W2[:, :, :], IN[:, :, :], AX, ALU.max))
            first_max(MB, IN[:, :, :], W2)
            V.tensor_tensor(SM[:, :, :], W2[:, :, :], M1[:, :, :], ALU.subtract).then_inc(e2_pre, 1)
            dve.wait_ge(e2_ready, 1)
            link(V.scalar_tensor_tensor(W1[:, :, :], ED[:, :, :], 1.0, GP[:, :, :], ALU.add, ALU.mult))
            link(V.reciprocal(W1[:, :, :], W1[:, :, :]))
            link(V.tensor_tensor(W2[:, :, :], W1[:, :, :], ED[:, :, :], ALU.mult))
            link(V.tensor_tensor(CI[:, :, :], MA[:, :, :], wide(W1[:, :, :]), ALU.mult))
            link(V.tensor_tensor(TM[:, :, :], MB[:, :, :], wide(W2[:, :, :]), ALU.mult))
            link(V.tensor_tensor(CI[:, :, :], CI[:, :, :], TM[:, :, :], ALU.add))
            for n in range(NG):
                last = V.tensor_tensor(CW[:, :, EG * n:EG * (n + 1)], CI[:, :, :], wide(MG[:, :, n:n + 1]), ALU.mult)
            last.then_inc(cw_ready, 1)
    st.close()


def spread_experts(e, name, half, SEL, CR, CB):
    st = Stage(e, name)
    nc = e.nc
    n = NE // 2
    sel_in, psum, ready = (st.sem(x) for x in ("sel_in", "psum", "ready"))
    with nc.Block() as block:
        @block.sync
        def _(sp):
            if half == 0:
                sp.dma_start(SEL[:, :], e.dram["sel16"]).then_inc(sel_in, 16)
                sp.wait_ge(sel_in, 16)

        @block.tensor
        def _(pe):
            if half == 0:
                pe.wait_ge(sel_in, 16)
            for m in range(n):
                if m >= 2:
                    pe.wait_ge(ready, m - 1)
                x = half * n + m
                nc.tensor.matmul(e.bank[6 + m % 2][:, :], SEL[:, x * P:(x + 1) * P], CR[:, :], start=True, stop=True
                                 ).then_inc(psum, 1)

        @block.scalar
        def _(act):
            for m in range(n):
                act.wait_ge(psum, m + 1)
                nc.scalar.activation(CB[:, m, :], e.bank[6 + m % 2][:, :], ACT.Copy).then_inc(ready, 1)
    st.close()


def layout_stream(w, kt, ntile, order=None):
    k, n = w.shape
    v = w.reshape(k // P, P, n // P, P).transpose(2, 1, 0, 3)
    if order is not None:
        v = v[order]
    v = v.reshape(-1, ntile, P, kt, P).transpose(0, 2, 1, 3, 4)
    return np.ascontiguousarray(v.reshape(v.shape[0], P, ntile * kt * P))


def pack_params(p):
    cols = [np.asarray(p[n], np.float32).reshape(s, P).T for n, s in PARAM_SIZES]
    return np.ascontiguousarray(np.concatenate(cols, axis=1))


def pad_rows(groups, width=P):
    first = np.asarray(groups[0])
    out = np.zeros(first.shape[:-1] + (width,), np.float32)
    for g, v in enumerate(groups):
        out[..., 32 * g:32 * g + v.shape[-1]] = v
    return out


def feature_major(x):
    return np.ascontiguousarray(x.T.reshape(x.shape[1] // P, P, x.shape[0]).transpose(1, 0, 2))


def layout_token_major(w, ncol):
    k, n = w.shape
    v = w.reshape(k // P, P, n // ncol, ncol).transpose(2, 1, 0, 3)
    return np.ascontiguousarray(v.reshape(n // ncol, P, k // P * ncol))


def layout_inputs(i):
    g = {n: np.asarray(v) for n, v in i.items()}
    dram = {}
    x = np.concatenate([g["x"][0], g["ctx"][0]], axis=0)
    dram["x"] = feature_major(x)
    dram["ident"] = np.eye(P, dtype=np.float32)
    w_in, b_in = g["w_in"][0], g["b_in"][0]
    xf, q, k, v, o, gt, gf, gm = np.split(w_in, np.cumsum([512, 1024, 1024, 1024, 1024, 16, 1024]), axis=1)
    bxf, bq, bk, bv, bo, bgt, bgf, bgm = np.split(b_in, np.cumsum([512, 1024, 1024, 1024, 1024, 16, 1024]))
    order = (0, 2, 1, 3)
    dram["gates"] = layout_stream(pad_rows([gt[:, 4 * m:4 * m + 4] for m in order]), KT, 1)
    params = {
        "c": g["c"][0], "c_ctx": g["c_ctx"], "b_ada": g["b_ada"][0], "norm_g": g["norm_g"][0], "bk": bk, "bq": bq,
        "bgate": pad_rows([bgt[4 * m:4 * m + 4] for m in order]), "bo": bo, "bgf": bgf, "bgm": bgm,
        "conv_w": g["conv_w"][0], "conv_b": g["conv_b"][0], "head_g": g["head_g"][0],
        "conv_w_2": g["conv_w_2"][0], "dn_g": g["dn_norm_g_2"][0], "ln1_g": g["ln1_g_2"][0],
        "ln1_b": g["ln1_b_2"][0], "ln2_g": g["ln2_g_2"][0], "ln2_b": g["ln2_b_2"][0],
        "dt_bias": pad_rows([g["dt_bias_2"][0]]), "a_log": pad_rows([g["a_log_2"][0]]),
    }
    dram["params"] = pack_params(params)
    dram["w_ada"] = layout_stream(g["w_ada"][0], KT, 2)

    def pair(name, wa, wb, w2, half_tiles):
        n = half_tiles * P
        for h in range(2):
            ha, hb = (m[:, h * n:(h + 1) * n].reshape(D, half_tiles, P) for m in (wa, wb))
            both = np.stack([ha, hb], axis=2).reshape(D, 2 * n)
            dram[f"{name[0]}{h}"] = layout_stream(both, KT, 2)
            dram[f"{name[1]}{h}"] = layout_stream(w2[h * n:(h + 1) * n], half_tiles, 1)

    for s in "ab":
        w13 = g[f"w13_{s}"][0]
        pair((f"gu_{s}", f"dn_{s}"), w13[:, :FFH], w13[:, FFH:], g[f"w2_{s}"][0], HTILES)
    dram["wk"], dram["wq"] = layout_stream(k, KT, 2), layout_stream(q, KT, 2)
    dram["wv"], dram["wxf"] = layout_token_major(v, 256), layout_token_major(xf, 256)
    dram["wo"], dram["wgf"], dram["wgm"] = (layout_stream(m, KT, 2) for m in (o, gf, gm))
    dram["w_four"] = layout_stream(g["w_four"][0], 4, 2)
    dram["w_mproj"], dram["w_out"] = layout_stream(g["w_mproj"][0], KT, 2), layout_stream(g["w_out"][0], KT, 2)
    dram["bias_tok"] = np.ascontiguousarray(np.broadcast_to(np.concatenate([bv, bxf]), (P, D + 512)))
    w_in = g["w_in_2"][0]
    qkv, z, aa, bb, u2, v2, gd, gsg = np.split(w_in, np.cumsum([3072, 1024, 8, 8, 1024, 1024, 1024]), axis=1)
    dram["gates2"] = layout_stream(pad_rows([aa, bb]), KT, 1)
    for n, m in (("wqkv2", qkv), ("wz2", z), ("wgd2", gd), ("wu2", u2), ("wgs2", gsg), ("w_dn", g["w_dn_out_2"][0]),
                 ("w_sgu", g["w_sgu_out_2"][0]), ("w_out2", g["w_out_2"][0])):
        dram[n] = layout_stream(m, KT, 2)
    dram["wv2"] = layout_token_major(v2, 256)
    rw = np.concatenate([g["router_group_w_2"][0], g["router_expert_w_2"][0], np.zeros((D, 12), np.float32)], axis=1)
    dram["router"] = layout_token_major(rw, 32)
    rb = np.concatenate([g["router_group_b_2"][0], g["router_expert_b_2"][0], np.zeros(12, np.float32)])
    dram["router_b"] = np.ascontiguousarray(np.broadcast_to(rb, (P, 32)))
    dram["priority"] = np.ascontiguousarray(np.broadcast_to(np.arange(4, 0, -1, dtype=np.float32), (P, 4)))
    flat = lambda m: m.transpose(1, 0, 2).reshape(D, NE * EFF)
    pair(("e_up", "e_dn"), flat(g["expert_w_gate_2"][0]), flat(g["expert_w_up_2"][0]),
         g["expert_w_down_2"][0].reshape(NE * EFF, D), ETILES)
    dram["sgu_ln"] = np.ascontiguousarray(
        np.broadcast_to(np.concatenate([g["sgu_ln_g_2"][0], g["sgu_ln_b_2"][0]]), (P, 2 * D)))
    dram["spatial_w"] = np.ascontiguousarray(g["spatial_w_2"][0].transpose(2, 0, 1))
    dram["spatial_b"] = np.ascontiguousarray(np.broadcast_to(g["spatial_b_2"][0], (P, D // P, P)))
    ones_at = lambda n: np.ascontiguousarray(np.broadcast_to(np.eye(n, dtype=np.float32)[:, :, None], (n, n, P))
                                             ).reshape(n, n * P)
    dram["sel8"], dram["sel16"] = ones_at(DNH), ones_at(NE)
    row, colm = np.meshgrid(np.arange(P), np.arange(P), indexing="ij")
    dram["causal"] = (row <= colm).astype(np.float32)
    dram["level_mask"] = np.concatenate(
        [((row >> (m + 1)) == (colm >> (m + 1))) & ((row >> m) % 2 == 1) & ((colm >> m) % 2 == 0)
         for m in range(7)], axis=1).astype(np.float32)
    dram["decay_mask"] = np.concatenate([np.where(row <= colm, 0, -BIG), np.where(colm < row, 0, BIG)],
                                        axis=1).astype(np.float32)
    sel = np.zeros((36, MH, P), np.float32)
    for h in range(MH):
        sel[h, h] = sel[32 + h, h] = 1.0
    dram["sel"] = sel.reshape(36, MH * P)
    s, t = np.meshgrid(np.arange(P), np.arange(P), indexing="ij")
    dram["scan_mask"] = np.concatenate([np.where(s <= t, 0, BIG), np.where(s >= t, 0, BIG)], axis=1).astype(np.float32)
    dft = lambda n: np.exp(-2j * np.pi * np.outer(np.arange(n), np.arange(n)) / n) / np.sqrt(n)
    tok, ch = np.kron(dft(T // 64), dft(64)), dft(P)
    dram["dft_t"] = np.ascontiguousarray(
        np.stack([tok.real, tok.imag]).reshape(2, NCH, P, T).transpose(2, 0, 1, 3).astype(np.float32))
    dram["dft_c"] = np.ascontiguousarray(np.stack([ch.real, -ch.imag], axis=1).astype(np.float32))
    return dram


INTERNAL = [("h1", [P, KT, T]), ("uh_s", [P, KT, T]), ("ul_s", [P, KT, T]), ("h4", [P, KT, T])]


def setup(nc, dram):
    e = Env()
    e.nc, e.dram, e.cleared = nc, dram, []
    e.split_upto, e.loaded_upto = 2, 2
    at = lambda n, shape, off, dt=F32: nc.alloc_sbuf_tensor_at(n, shape, dt, offset=off)
    e.raw = [at(f"raw{p}", [P, 2048], RAW + p * 8192) for p in range(2)]
    e.whi = [at(f"whi{p}", [P, 2048], WHI + p * 8192, F32R) for p in range(2)]
    e.wlo = [at(f"wlo{p}", [P, 2048], WLO + p * 8192, F32R) for p in range(2)]
    off = [CONST]

    def resident(n, shape):
        t = at(n, shape, off[0])
        off[0] += (int(np.prod(shape[1:])) * 4 + 31) // 32 * 32
        assert off[0] <= TMP, (n, off[0] - TMP)
        return t

    e.params, e.mods = resident("params", [P, NPARAM]), resident("mods", [P, ADA * KT, 2])
    e.gs, e.gg = resident("gs", [P, 3, KT, 2]), resident("gg", [P, 3, KT, 2])
    e.ident, e.ones, e.mean_ones = (resident(n, [P, P]) for n in ("ident", "ones", "mean_ones"))
    e.one_col, e.eps = resident("one_col", [P, 1]), resident("eps", [P, 2])
    e.bank = [nc.alloc_psum_tensor(f"bank{b}", [P, 512], F32) for b in range(8)]
    e.w_landed = [nc.alloc_semaphore(f"w_landed{p}") for p in range(2)]
    e.w_hi, e.w_split, e.slot_done, e.acc_free = (
        nc.alloc_semaphore(n) for n in ("w_hi", "w_split", "slot_done", "acc_free"))
    return e


def program(nc, dram):
    e = setup(nc, dram)
    prologue(e)
    uh = nc.alloc_sbuf_tensor_at("uh_a", [P, KT, W], F32R, offset=MAIN + 24576)
    ul = nc.alloc_sbuf_tensor_at("ul_a", [P, KT, W], F32R, offset=MAIN + 49152)
    pre_norm(e, "n1", 0, W, e.x0, uh, ul)
    y = nc.alloc_sbuf_tensor_at("y_a", [P, KT, W], F32, offset=MAIN)
    ffn(e, "fa", "gu_a", "dn_a", (0, 1), W, HTILES, uh, ul, y, MAIN + 73728)
    xr = nc.alloc_sbuf_tensor_at("xr", [P, KT, W], F32, offset=MAIN + 24576)
    post_norm(e, "p1", 0, W, y, xr, y, load=dram["x"], store=dram["h1"])
    at = lambda n, shape, off, dt=F32: nc.alloc_sbuf_tensor_at(n, shape, dt, offset=MAIN + off)
    uh, ul = at("uh_m", [P, KT, W], 24576, F32R), at("ul_m", [P, KT, W], 49152, F32R)
    pre_norm(e, "n2", 1, W, y, uh, ul)
    K, V, Q = at("K", [P, KT, W], 74752), at("V", [P, NCH + NCC, D], 99328), at("Q", [P, KT, T], 123904)
    XF, bias_tok, GR = at("XF", [P, NCH, 512], 0), at("bias_tok", [P, D + 512], 8192), at("GR", [P, W], 14336)
    project_1(e, uh, ul, K, Q, V, XF, GR, bias_tok)
    B, LF, G = at("B", [36, W], 17408), at("LF", [36, W], 20480), at("G", [36, W], 8192)
    SEL, MASK = at("SEL", [36, MH * P], 11264), at("MASK", [P, 2 * P], 13312)
    C = [at(f"C{n}", [P, 2, DH + P], 24576 + n * 3072) for n in range(2 * MH)]
    RT, HT = at("RT", [36, 3, W], 49152), at("HT", [P, KT, T], 58368)
    GC, MP = at("GC", [P, NCH + NCC, 36], 140288), at("MP", [36, 8], 140288 + 896)
    scan_rows(e, GR, B, LF, G, RT, MP, GC)
    scan(e, Q, K, V, C, HT, RT, GC, SEL, MASK)
    uh, ul = at("uh_r", [P, KT, T], 24576, F32R), at("ul_r", [P, KT, T], 40960, F32R)
    yfh, yfl = at("yfh", [P, 4, T], 107520, F32R), at("yfl", [P, 4, T], 115712, F32R)
    fourier(e, XF, yfh, yfl, MAIN + 74752, uh, ul)
    O, GF, GM = at("O", [P, KT, T], 74752), at("GF", [P, KT, T], 91136), at("GM", [P, KT, T], 123904)
    gemm_act(e, "wo", uh, ul, O, ACT.Sigmoid, "bo")
    gemm_act(e, "wgf", uh, ul, GF, ACT.Sigmoid, "bgf")
    gemm_act(e, "wgm", uh, ul, GM, ACT.Sigmoid, "bgm")
    mh, ml = at("mh", [P, KT, T], 24576, F32R), at("ml", [P, KT, T], 40960, F32R)
    hg = PARAM_AT["head_g"]
    head_norm(e, "hn", HT, 2, lambda k: e.params[:, hg + k:hg + k + 1], O, mh, ml)
    gemm_gate(e, "w_four", 4, yfh, yfl, GF)
    yh, yl = at("yh", [P, KT, T], 58368, F32R), at("yl", [P, KT, T], 74752, F32R)
    gemm_gate_split(e, "w_mproj", mh, ml, GM, GF, yh, yl)
    Y1, XR = at("Y1", [P, KT, T], 91136), at("XR1", [P, KT, T], 107520)
    gemm_copy(e, "w_out", yh, yl, Y1)
    post_norm(e, "p2", 1, T, Y1, XR, Y1, load=dram["h1"])
    uh, ul = at("uh_b", [P, KT, T], 0, F32R), at("ul_b", [P, KT, T], 16384, F32R)
    pre_norm(e, "n3", 2, T, Y1, uh, ul)
    Y2 = at("Y2", [P, KT, T], 107520)
    ffn(e, "fb", "gu_b", "dn_b", (0, 1), T, HTILES, uh, ul, Y2, MAIN + 32768)
    post_norm(e, "p3", 2, T, Y2, Y1, Y2)
    xh, xl = at("xh", [P, KT, T], 0, F32R), at("xl", [P, KT, T], 16384, F32R)
    split_stage(e, "sp2", Y2, xh, xl, dram["h1"])
    QKV, GR2 = at("QKV", [P, 3 * DNH, T], 32768), at("GR2", [P, T], 81920)
    project_2(e, xh, xl, QKV, GR2)
    l2_norm(e, QKV)
    QD = at("QD", [P, DNH, T], 84480)
    R, SEL8 = at("R", [DNH, 4, T], 0), at("SEL8", [DNH, DNH * P], 8192)
    LMASK, DMASK = at("LMASK", [P, 7 * P], 12288), at("DMASK", [P, 2 * P], 15872)
    COL, GL = at("COL", [P, NCH * 4 * DNH], 16896), at("GL", [P, DNH, NCH], 17408)
    delta_rows(e, GR2, R, SEL8, QKV, QD, COL, GL)
    delta(e, QKV, QD, R, SEL8, COL, GL, LMASK, DMASK, MAIN + 100864)
    OT = QKV[:, 2 * DNH:3 * DNH, :]
    xh, xl = at("xh_r", [P, KT, T], 0, F32R), at("xl_r", [P, KT, T], 16384, F32R)
    reload(e, "rl2", xh, xl)
    Z, GD = at("Z", [P, KT, T], 32768), at("GD", [P, KT, T], 49152)
    gemm_act(e, "wz2", xh, xl, Z, ACT.Silu)
    gemm_act(e, "wgd2", xh, xl, GD, ACT.Sigmoid)
    mh, ml = at("oh", [P, KT, T], 81920, F32R), at("ol", [P, KT, T], 98304, F32R)
    dg = PARAM_AT["dn_g"]
    head_norm(e, "on", OT, 1, lambda k: e.params[:, dg:dg + 1], Z, mh, ml)
    gemm_gate(e, "w_dn", KT, mh, ml, GD)
    VT, LNP = at("VT", [P, NCH, D], 114688), at("LNP", [P, 2 * D], 65536)
    sgu_values(e, xh, xl, VT, LNP)
    UG = at("UG", [P, KT, T], 32768)
    gemm_act(e, "wu2", xh, xl, UG, ACT.Gelu)
    WS, SB = at("WS", [P, D // P, P], 73728), at("SB", [P, D // P, P], 77824)
    gh, gl = at("gh", [P, KT, T], 81920, F32R), at("gl", [P, KT, T], 98304, F32R)
    spatial(e, VT, UG, WS, SB, gh, gl)
    GS = at("GS", [P, KT, T], 114688)
    gemm_act(e, "wgs2", xh, xl, GS, ACT.Sigmoid)
    yh, yl = at("y2h", [P, KT, T], 0, F32R), at("y2l", [P, KT, T], 16384, F32R)
    gemm_gate_split(e, "w_sgu", gh, gl, GS, GD, yh, yl)
    MX, XR = at("MX", [P, KT, T], 65536), at("XR2", [P, KT, T], 81920)
    gemm_copy(e, "w_out2", yh, yl, MX)
    hh, hl = at("h4h", [P, KT, T], 0, F32R), at("h4l", [P, KT, T], 16384, F32R)
    deep_norm(e, "ln1", MX, XR, dram["h1"], "ln1_g", "ln1_b", split=(hh, hl), store=dram["h4"])
    SEL16, CR = at("SEL16", [NE, NE * P], 131072), at("CR", [NE, T], 139264)
    CB, Y3 = at("CB", [P, NE // 2, T], 114688), at("Y3", [P, KT, T], 98304)
    router(e, hh, hl, CR)
    spread_experts(e, "cb0", 0, SEL16, CR, CB)
    ffn(e, "m0", "e_up", "e_dn", (0,), T, ETILES, hh, hl, Y3, MAIN + 32768, combine=CB)
    spread_experts(e, "cb1", 1, SEL16, CR, CB)
    ffn(e, "m1", "e_up", "e_dn", (1,), T, ETILES, hh, hl, Y3, MAIN + 32768, combine=CB)
    XR = at("XR3", [P, KT, T], 32768)
    deep_norm(e, "ln2", Y3, XR, dram["h4"], "ln2_g", "ln2_b", store=dram["out"])


def kernel(**inputs):
    import concourse.bacc as bacc
    from concourse.bass_utils import run_bass_kernel_spmd

    nc = bacc.Bacc("TRN2", target_bir_lowering=False, num_devices=1)
    arrays = {f"{n}_dram": a for n, a in layout_inputs(inputs).items()}
    dram = {n[:-5]: nc.dram_tensor(n, a.shape, F32, kind="ExternalInput").ap() for n, a in arrays.items()}
    for n, shape in INTERNAL:
        dram[n] = nc.dram_tensor(f"{n}_scratch", shape, F32, kind="Internal").ap()
    dram["out"] = nc.dram_tensor("out_dram", [P, KT, T], F32, kind="ExternalOutput").ap()
    program(nc, dram)
    result = run_bass_kernel_spmd(nc, [arrays], core_ids=[0]).results[0]["out_dram"]
    return np.ascontiguousarray(np.asarray(result).transpose(2, 1, 0).reshape(1, T, D))
```

```python
import numpy as np
import concourse.bass as bass
from concourse import mybir

F32 = mybir.dt.float32
F32R = mybir.dt.float32r
ALU = mybir.AluOpType
ACT = mybir.ActivationFunctionType
ds = bass.ds

P = 128
D = 1024
KT = D // P
T = 512
TC = 256
W = T + TC
FFH = 2816
HTILES = FFH // P // 2
ADA = 9
MH = 4
DH = 256
NCH = T // P
NCC = TC // P
DNH = 8
NE = 16
EFF = 256
ETILES = NE * EFF // P // 2
EPS = 1e-6
LN_EPS = 1e-5
ALPHA = 2.0 ** 0.25
BIG = 1e30

BASE = 16512
RAW = BASE
WHI = RAW + 2 * 8192
WLO = WHI + 2 * 8192
CONST = WLO + 2 * 8192
TMP = CONST + 4608
MAIN = TMP + 5 * W * 4 + 1024
LIMIT = 229368

PARAM_SIZES = [("c", 8), ("c_ctx", 8), ("b_ada", 72), ("norm_g", 48), ("bk", 8), ("bq", 8), ("bgate", 1),
               ("bo", 8), ("bgf", 8), ("bgm", 8), ("conv_w", 48), ("conv_b", 16), ("head_g", 8),
               ("conv_w_2", 96), ("dn_g", 1), ("ln1_g", 8), ("ln1_b", 8), ("ln2_g", 8), ("ln2_b", 8),
               ("dt_bias", 1), ("a_log", 1)]
PARAM_AT = {}
_at = 0
for _n, _s in PARAM_SIZES:
    PARAM_AT[_n] = _at
    _at += _s
NPARAM = _at

STREAM = [("gu_a0", HTILES, 16), ("dn_a0", 8, HTILES), ("gu_a1", HTILES, 16), ("dn_a1", 8, HTILES),
          ("gates", 1, 8), ("wk", 4, 16), ("wq", 4, 16), ("wv", 4, 16), ("wxf", 2, 16),
          ("wo", 4, 16), ("wgf", 4, 16), ("wgm", 4, 16), ("w_four", 4, 8), ("w_mproj", 4, 16), ("w_out", 4, 16),
          ("gu_b0", HTILES, 16), ("dn_b0", 8, HTILES), ("gu_b1", HTILES, 16), ("dn_b1", 8, HTILES),
          ("gates2", 1, 8), ("wqkv2", 12, 16), ("wz2", 4, 16), ("wgd2", 4, 16), ("w_dn", 4, 16),
          ("wv2", 4, 16), ("wu2", 4, 16), ("wgs2", 4, 16), ("w_sgu", 4, 16), ("w_out2", 4, 16),
          ("router", 1, 2), ("e_up0", ETILES, 16), ("e_dn0", 8, ETILES), ("e_up1", ETILES, 16), ("e_dn1", 8, ETILES)]
START = {}
_at = 0
for _n, _s, _f in STREAM:
    START[_n] = (_at, _at + _s)
    _at += _s
NSLOTS = _at


class Env:
    pass


class Stage:

    def __init__(self, e, name):
        self.e, self.nc, self.name, self.used = e, e.nc, name, []

    def sem(self, name):
        s = self.nc.alloc_semaphore(f"{self.name}_{name}")
        self.used.append(s)
        return s

    def sb(self, name, shape, offset, dt=F32):
        size = int(np.prod(shape[1:])) * 4
        assert offset + size <= LIMIT, (self.name, name, offset + size - LIMIT)
        return self.nc.alloc_sbuf_tensor_at(f"{self.name}_{name}", shape, dt, offset=offset)

    def close(self):
        for s in self.used:
            self.nc.gpsimd.sem_clear(s)
        for s in self.e.cleared:
            self.nc.release_semaphore(s)
        self.e.cleared = self.used


def slots(eng, a, b, body, straight=False):
    at = 0
    for name, n, _ in STREAM:
        lo, hi = max(a, at), min(b, at + n)
        if lo < hi:
            while lo < min(2, hi):
                body(name, lo - at, lo % 2, lo, (lo - at) // 2, lo // 2)
                lo += 1
            pairs = (hi - lo) // 2 if hi - lo >= 4 and not straight else 0
            if pairs:
                with eng.Fori(0, pairs) as i:
                    for s in range(2):
                        body(name, lo - at + s + 2 * i, (lo + s) % 2, lo + s + 2 * i, (lo - at + s) // 2 + i,
                             (lo + s) // 2 + i)
            for g in range(lo + 2 * pairs, hi):
                body(name, g - at, g % 2, g, (g - at) // 2, g // 2)
        at += n


def feed_ahead(e, b, more=0):
    upto = min(b + 1 + more, NSLOTS)
    pool, e.split_upto = (e.split_upto, upto), max(e.split_upto, upto)
    sp, e.loaded_upto = (e.loaded_upto, min(upto + 2, NSLOTS)), max(e.loaded_upto, min(upto + 2, NSLOTS))
    return sp, pool


def feed_sp(e, sp, span):
    tiles = {n: f for n, _, f in STREAM}

    def load(name, i, p, g, ihalf, ghalf):
        sp.wait_ge(e.w_split, g - 1)
        src = e.dram[name]
        sp.dma_start(e.raw[p][:, 0:tiles[name] * P],
                     src[i] if isinstance(i, int) else src[ds(i, 1)].rearrange("a p n -> p (a n)")
                     ).then_inc(e.w_landed[p], 16)

    slots(sp, *span, load)


def feed_pool(e, pool, span):
    tiles = {n: f for n, _, f in STREAM}

    def split(name, i, p, g, ihalf, ghalf):
        f = tiles[name] * P
        pool.wait_ge(e.w_landed[p], 16 * ghalf + 16)
        if not (isinstance(g, int) and g < 2):
            pool.wait_ge(e.slot_done, g - 1)
        e.nc.gpsimd.tensor_tensor(e.whi[p][:, 0:f], e.raw[p][:, 0:f], e.one_col[:, 0:1].to_broadcast([P, f]),
                                  ALU.mult).then_inc(e.w_hi, 1)
        pool.wait_ge(e.w_hi, g + 1)
        e.nc.gpsimd.tensor_tensor(e.wlo[p][:, 0:f], e.raw[p][:, 0:f], e.whi[p][:, 0:f].bitcast(F32),
                                  ALU.subtract).then_inc(e.w_split, 1)

    slots(pool, *span, split)


def pe_slot_begin(e, pe, g):
    pe.wait_ge(e.w_split, g + 1)
    if not (isinstance(g, int) and g < 2):
        pe.wait_ge(e.acc_free, g - 1)


def three_pass(e, out, wh, wl, xh, xl, first, last):
    e.nc.tensor.matmul(out, wh, xh, start=first, stop=False)
    e.nc.tensor.matmul(out, wh, xl, start=False, stop=False)
    return e.nc.tensor.matmul(out, wl, xh, start=False, stop=last)


def pe_feature_major(e, p, kt, ntile, xh, xl, ctx, between=None, ready=None):
    done = None
    order = [(n, k) for k in range(kt) for n in range(ntile)] if ready is not None else \
        [(n, k) for n in range(ntile) for k in range(kt)]
    for n, k in order:
        if between is not None and (n, k) == (ntile - 1, 0):
            between()
        if ready is not None and n == 0:
            ready(k)
        at = (n * kt + k) * P
        done = three_pass(e, e.bank[2 * p + n][:, :], e.whi[p][:, at:at + P], e.wlo[p][:, at:at + P],
                          xh[:, k, 0:T], xl[:, k, 0:T], k == 0, k == kt - 1)
    if ctx:
        for n in range(ntile):
            for k in range(kt):
                at = (n * kt + k) * P
                done = three_pass(e, e.bank[4 + p][:, n * TC:(n + 1) * TC], e.whi[p][:, at:at + P],
                                  e.wlo[p][:, at:at + P], xh[:, k, T:W], xl[:, k, T:W], k == 0, k == kt - 1)
    return done


def pe_token_major(e, p, ncol, xh, xl, ctx):
    done = None
    for t in range(NCH + (NCC if ctx else 0)):
        bank = e.bank[2 * p + t // 2] if t < NCH else e.bank[4 + p]
        out = bank[:, (t % 2) * ncol:(t % 2 + 1) * ncol]
        for k in range(KT):
            col = slice(k * ncol, (k + 1) * ncol)
            tok = slice(t * P, (t + 1) * P)
            e.nc.tensor.matmul(out, xh[:, k, tok], e.whi[p][:, col], start=k == 0, stop=False)
            e.nc.tensor.matmul(out, xh[:, k, tok], e.wlo[p][:, col], start=False, stop=False)
            done = e.nc.tensor.matmul(out, xl[:, k, tok], e.whi[p][:, col], start=False, stop=k == KT - 1)
    return done


def parts_of(w):
    return [(slice(0, T), 0)] + ([(slice(T, W), 1)] if w == W else [])


def prologue(e):
    st = Stage(e, "ada")
    nc = e.nc
    ring = [st.sb(f"w{r}", [P, KT * 512], MAIN + 24576 + r * 16384) for r in range(3)]
    rows = st.sb("rows", [2, ADA * D], MAIN + 73728)
    spread = st.sb("spread", [ADA * KT, 2, P], MAIN + 110592)
    sc = st.sb("sc", [P, KT, 2], MAIN + 111616)
    x = st.sb("x", [P, KT, W], MAIN)
    landed = [st.sem(f"landed{r}") for r in range(3)]
    params_in, x_in, used, copied, spread_in, turned, silu, ones_set, consts_set, chain = (
        st.sem(n) for n in ("params_in", "x_in", "used", "copied", "spread_in", "turned", "silu", "ones_set",
                            "consts_set", "chain"))
    nada = ADA * D // 512
    e.x0 = x
    e.rstd0, act_stats, dve_stats, pe_stats = rms_stats(e, st, W, x)
    with nc.Block() as block:
        @block.sync
        def _(sp):
            sp.dma_start(e.params[:, :], e.dram["params"]).then_inc(params_in, 16)
            sp.dma_start(e.ident[:, :], e.dram["ident"]).then_inc(params_in, 16)
            for r in range(3):
                sp.dma_start(ring[r][:, :], e.dram["w_ada"][r]).then_inc(landed[r], 16)
            with sp.Fori(1, nada // 3) as i:
                for r in range(3):
                    sp.wait_ge(used, 3 * i + r - 2)
                    sp.dma_start(ring[r][:, :], e.dram["w_ada"][ds(3 * i + r, 1)].rearrange("a p n -> p (a n)")
                                 ).then_inc(landed[r], 16)
            sp.dma_start(x[:, :, :], e.dram["x"]).then_inc(x_in, 16)
            for g in range(2):
                sp.dma_start(e.raw[g][:, :], e.dram["gu_a0"][g]).then_inc(e.w_landed[g], 16)
            sp.wait_ge(copied, nada)
            for s in range(2):
                sp.dma_start(spread[:, s, :], rows[s:s + 1, :].rearrange("a (m n) -> a m n", n=P)
                             ).then_inc(spread_in, 16)
            sp.wait_ge(params_in, 32)

        @block.gpsimd
        def _(pool):
            pool.wait_ge(ones_set, 1)
            feed_pool(e, pool, (0, 2))

        @block.scalar
        def _(act):
            act.wait_ge(params_in, 32)
            for s, n in enumerate(("c", "c_ctx")):
                at = PARAM_AT[n]
                nc.scalar.activation(sc[:, :, s], e.params[:, at:at + KT], ACT.Silu).then_inc(silu, 1)
            act.wait_ge(consts_set, 1)
            act.wait_ge(x_in, 16)
            act_stats(act)

        @block.tensor
        def _(pe):
            def product(g, r, bank):
                for k in range(KT):
                    last = nc.tensor.matmul(e.bank[bank][0:2, :], sc[:, k, :], ring[r][:, k * 512:(k + 1) * 512],
                                            start=k == 0, stop=k == KT - 1)
                last.then_inc(used, 1)

            pe.wait_ge(silu, 2)
            for r in range(3):
                pe.wait_ge(landed[r], 16)
                product(r, r, r)
            with pe.Fori(1, nada // 3) as i:
                for r in range(3):
                    pe.wait_ge(landed[r], 16 * i + 16)
                    pe.wait_ge(copied, 3 * i + r - 2)
                    product(3 * i + r, r, r)
            pe_stats(pe)
            pe.wait_ge(spread_in, 32)
            pe.wait_ge(params_in, 32)
            for s in range(2):
                last = nc.tensor.matmul(e.bank[3][:, s * ADA * KT:(s + 1) * ADA * KT], spread[:, s, :],
                                        e.ident[0:ADA * KT, 0:ADA * KT], start=True, stop=True)
            last.then_inc(turned, 1)

        @block.vector
        def _(dve):
            nc.vector.memset(e.one_col[:, :], 1.0).then_inc(ones_set, 1)
            nc.vector.memset(e.eps[:, 0:1], EPS)
            nc.vector.memset(e.eps[:, 1:2], LN_EPS)
            nc.vector.memset(e.mean_ones[:, :], 1.0 / D)
            nc.vector.memset(e.ones[:, :], 1.0).then_inc(consts_set, 1)
            with dve.Fori(0, nada // 3) as i:
                for r in range(3):
                    dve.wait_ge(used, 3 * i + r + 1)
                    nc.vector.tensor_copy(rows[:, ds((3 * i + r) * 512, 512)], e.bank[r][0:2, :]).then_inc(copied, 1)
            dve_stats(dve)
            dve.wait_ge(turned, 1)
            at = PARAM_AT["b_ada"]
            for s in range(2):
                last = nc.vector.tensor_tensor(e.mods[:, :, s], e.bank[3][:, s * ADA * KT:(s + 1) * ADA * KT],
                                               e.params[:, at:at + ADA * KT], ALU.add)
            last.then_inc(chain, 1)
            dve.wait_ge(chain, 1)
            for j in range(3):
                g_pre = PARAM_AT["norm_g"] + 2 * j * KT
                for s in range(2):
                    sc_at, gt_at = (3 * j + 1) * KT, (3 * j + 2) * KT
                    nc.vector.scalar_tensor_tensor(e.gs[:, j, :, s], e.mods[:, sc_at:sc_at + KT, s], 1.0,
                                                   e.params[:, g_pre:g_pre + KT], ALU.add, ALU.mult)
                    nc.vector.scalar_tensor_tensor(e.gg[:, j, :, s], e.mods[:, gt_at:gt_at + KT, s],
                                                   1.0 if j == 1 else 0.5,
                                                   e.params[:, g_pre + KT:g_pre + 2 * KT], ALU.mult, ALU.mult)
    st.close()


def rms_stats(e, st, w, x):
    nc = e.nc
    sq = [st.sb(f"sq{r}", [P, w], TMP + r * W * 4) for r in range(2)]
    acc = st.sb("acc", [P, w], TMP + 2 * W * 4)
    rstd = st.sb("rstd", [P, w], TMP + 4 * W * 4)
    squared, summed, mean_ready, std_ready, rstd_ready = (
        st.sem(n) for n in ("squared", "summed", "mean_ready", "std_ready", "rstd_ready"))

    def act_part(act):
        for k in range(KT):
            if k >= 2:
                act.wait_ge(summed, k - 1)
            nc.scalar.activation(sq[k % 2][:, :], x[:, k, :], ACT.Square).then_inc(squared, 1)
        act.wait_ge(mean_ready, 1)
        for c, s in parts_of(w):
            last = nc.scalar.activation(acc[:, c], e.bank[6 + s][:, 0:c.stop - c.start], ACT.Sqrt,
                                        bias=e.eps[:, 0:1])
        last.then_inc(std_ready, 1)

    def dve_part(dve):
        for k in range(KT):
            dve.wait_ge(squared, k + 1)
            if k == 0:
                nc.vector.tensor_copy(acc[:, :], sq[0][:, :]).then_inc(summed, 1)
            else:
                dve.wait_ge(summed, k)
                nc.vector.tensor_tensor(acc[:, :], acc[:, :], sq[k % 2][:, :], ALU.add).then_inc(summed, 1)
        dve.wait_ge(std_ready, 1)
        nc.vector.reciprocal(rstd[:, :], acc[:, :]).then_inc(rstd_ready, 1)
        dve.wait_ge(rstd_ready, 1)

    def pe_part(pe):
        pe.wait_ge(summed, KT)
        for c, s in parts_of(w):
            last = nc.tensor.matmul(e.bank[6 + s][:, 0:c.stop - c.start], e.mean_ones[:, :], acc[:, c],
                                    start=True, stop=True)
        last.then_inc(mean_ready, 1)

    return rstd, act_part, dve_part, pe_part


class RunningSum:

    def __init__(self, e, st, w, squares):
        self.e, self.squares = e, squares
        if squares:
            self.sq = [st.sb(f"run_sq{r}", [P, w], TMP + r * W * 4) for r in range(2)]
            self.squared = st.sem("run_squared")
        self.acc = st.sb("run_acc", [P, w], TMP + 4 * W * 4)
        self.summed = st.sem("run_summed")

    def dve_start(self, dve):
        self.e.nc.vector.memset(self.acc[:, :], 0.0).then_inc(self.summed, 1)

    def act(self, act, y, i, p, g):
        if self.squares:
            act.wait_ge(self.e.acc_free, g + 1)
            self.e.nc.scalar.activation(self.sq[p][:, :], y, ACT.Square).then_inc(self.squared, 1)

    def dve(self, dve, y, i, p, g):
        if self.squares:
            dve.wait_ge(self.squared, i + 1)
        else:
            dve.wait_ge(self.e.acc_free, g + 1)
        dve.wait_ge(self.summed, i + 1)
        self.e.nc.vector.tensor_tensor(self.acc[:, :], self.acc[:, :], self.sq[p][:, :] if self.squares else y, ALU.add
                                       ).then_inc(self.summed, 1)


class NormFront:

    def __init__(self, e, name, w, y, uh, ul, acc=None, post=None, pre=None, rstd=None, store=None):
        self.e, self.st, self.w, self.y, self.uh, self.ul = e, Stage(e, name), w, y, uh, ul
        self.acc, self.post, self.pre, self.store = acc, post, pre, store
        self.t = [self.st.sb(f"t{r}", [P, w], TMP + r * W * 4) for r in range(2)]
        self.sq = [self.st.sb(f"sq{r}", [P, w], TMP + (2 + r) * W * 4) for r in range(2)]
        self.ring = self.t + self.sq
        self.r = rstd if rstd is not None else self.st.sb("r", [P, w], TMP + 4 * W * 4)
        self.mean_ready, self.std_ready, self.rstd_ready, self.scaled, self.added, self.squared, self.sq_summed, \
            self.normed, self.hi_ready, self.lo_ready, self.stored = (self.st.sem(n) for n in (
                "mean_ready", "std_ready", "rstd_ready", "scaled", "added", "squared", "sq_summed", "normed",
                "hi_ready", "lo_ready", "stored"))

    def sp(self, sp):
        if self.store is not None:
            sp.wait_ge(self.added, KT)
            sp.dma_start(self.store, self.y[:, :, 0:T]).then_inc(self.stored, 16)
            sp.wait_ge(self.stored, 16)

    def pe(self, pe):
        nc, e = self.e.nc, self.e
        if self.post is None:
            return
        for c, s in parts_of(self.w):
            last = nc.tensor.matmul(e.bank[6 + s][:, 0:c.stop - c.start], e.mean_ones[:, :], self.acc[:, c],
                                    start=True, stop=True)
        last.then_inc(self.mean_ready, 1)
        if self.pre is not None:
            pe.wait_ge(self.std_ready, 1)
            for k in range(KT):
                pe.wait_ge(self.squared, k + 1)
                for c, s in parts_of(self.w):
                    last = nc.tensor.matmul(e.bank[6 + s][:, 0:c.stop - c.start], e.mean_ones[:, :],
                                            self.sq[k % 2][:, c], start=k == 0, stop=k == KT - 1)
                last.then_inc(self.sq_summed, 1)

    def act(self, act):
        nc, e = self.e.nc, self.e

        def root():
            for c, s in parts_of(self.w):
                last = nc.scalar.activation(self.r[:, c], e.bank[6 + s][:, 0:c.stop - c.start], ACT.Sqrt,
                                            bias=e.eps[:, 0:1])
            last.then_inc(self.std_ready, 1)

        if self.post is not None:
            act.wait_ge(self.mean_ready, 1)
            root()
            for k in range(KT):
                act.wait_ge(self.added, k + 1)
                if self.pre is None:
                    nc.scalar.activation(self.uh[:, k, :], self.y[:, k, :], ACT.Copy).then_inc(self.hi_ready, 1)
                else:
                    if k >= 2:
                        act.wait_ge(self.sq_summed, k - 1)
                    nc.scalar.activation(self.sq[k % 2][:, :], self.y[:, k, :], ACT.Square).then_inc(self.squared, 1)
            if self.pre is not None:
                act.wait_ge(self.sq_summed, KT)
                root()
        if self.pre is not None:
            for k in range(KT):
                act.wait_ge(self.normed, k + 1)
                for c, s in parts_of(self.w):
                    last = nc.scalar.activation(self.uh[:, k, c], self.ring[k % 4][:, c], ACT.Identity,
                                                bias=e.mods[:, 3 * self.pre * KT + k, s:s + 1])
                last.then_inc(self.hi_ready, 1)

    def dve(self, dve):
        nc, e, y, t = self.e.nc, self.e, self.y, self.t

        def scale(k, gain, j, done, t):
            for c, s in parts_of(self.w):
                last = nc.vector.scalar_tensor_tensor(t[k % len(t)][:, c], y[:, k, c], gain[:, j, k, s:s + 1], self.r[:, c],
                                                      ALU.mult, ALU.mult)
            last.then_inc(done, 1)

        def invert(n):
            dve.wait_ge(self.std_ready, n)
            nc.vector.reciprocal(self.r[:, :], self.r[:, :]).then_inc(self.rstd_ready, 1)
            dve.wait_ge(self.rstd_ready, n)

        if self.post is not None:
            j, res = self.post
            invert(1)
            scale(0, e.gg, j, self.scaled, t)
            for k in range(KT):
                if k + 1 < KT:
                    if k:
                        dve.wait_ge(self.added, k)
                    scale(k + 1, e.gg, j, self.scaled, t)
                dve.wait_ge(self.scaled, k + 1)
                nc.vector.tensor_tensor(y[:, k, :], t[k % 2][:, :], res[:, k, :], ALU.add).then_inc(self.added, 1)
                if self.pre is None and k:
                    self.lo_of_out(dve, k - 1)
            if self.pre is None:
                self.lo_of_out(dve, KT - 1)
            else:
                invert(2)
        if self.pre is not None:
            ring = self.ring
            scale(0, e.gs, self.pre, self.normed, ring)
            for k in range(KT):
                if k + 1 < KT:
                    scale(k + 1, e.gs, self.pre, self.normed, ring)
                dve.wait_ge(self.hi_ready, k + 1)
                for c, s in parts_of(self.w):
                    last = nc.vector.scalar_tensor_tensor(self.ul[:, k, c], ring[k % 4][:, c],
                                                          e.mods[:, 3 * self.pre * KT + k, s:s + 1],
                                                          self.uh[:, k, c].bitcast(F32), ALU.add, ALU.subtract)
                last.then_inc(self.lo_ready, 1)

    def lo_of_out(self, dve, k):
        dve.wait_ge(self.hi_ready, k + 1)
        self.e.nc.vector.tensor_tensor(self.ul[:, k, :], self.y[:, k, :], self.uh[:, k, :].bitcast(F32), ALU.subtract
                                       ).then_inc(self.lo_ready, 1)


def tile_at(t, i):
    return t[:, i, :] if isinstance(i, int) else t[:, ds(i, 1), :].rearrange("p a w -> p (a w)")


def ffn(e, name, up, down, w, htiles, uh, ul, y, hid_at, squares=True, front=None, late_load=None, combine=None,
        base=None, route=None):
    st = Stage(e, name)
    nc = e.nc
    hh = st.sb("hh", [P, htiles, w], hid_at, F32R)
    hl = st.sb("hl", [P, htiles, w], hid_at + htiles * w * 4, F32R)
    sil = [st.sb(f"sil{r}", [P, w], TMP + r * W * 4) for r in range(2)]
    v = [st.sb(f"v{r}", [P, w], TMP + (2 + r) * W * 4) for r in range(2)]
    silu_ready, hi_ready, lo_ready, gated, row_ready, spread, loaded = (
        st.sem(n) for n in ("silu_ready", "hi_ready", "lo_ready", "gated", "row_ready", "spread", "loaded"))
    running = RunningSum(e, st, w, squares)
    ctx = w == W
    a, b = START[f"{up}0"][0], START[f"{down}1"][1]
    sp_span, pool_span = feed_ahead(e, b)
    if route is not None:
        route_sp, route_pe, route_pe_rows, route_act, route_dve, rows_ready, route_stages = route
    with nc.Block() as block:
        @block.sync
        def _(sp):
            if front is not None:
                front.sp(sp)
            if route is not None:
                route_sp(sp)
            feed_sp(e, sp, sp_span)
            if late_load is not None:
                sp.wait_ge(e.slot_done, START[f"{up}1"][1])
                sp.dma_start(late_load[0][:, :, :], late_load[1]).then_inc(loaded, 16)
                sp.wait_ge(loaded, 16)

        @block.gpsimd
        def _(pool):
            feed_pool(e, pool, pool_span)

        @block.tensor
        def _(pe):
            if front is not None:
                front.pe(pe)
            if route is not None:
                route_pe(pe)
            for half in range(2):
                def up_slot(nm, i, p, g, ih, gh, ready=None, spreads=True):
                    def spread_expert():
                        pe.wait_ge(row_ready, half * htiles // 2 + ih + 1)
                        nc.tensor.matmul(e.bank[6][:, 0:w], e.ones[0:NE, :], combine[1][:, :], start=True, stop=True
                                         ).then_inc(spread, 1)

                    first_of_expert = combine is not None and spreads and p == a % 2
                    pe_slot_begin(e, pe, g)
                    pe_feature_major(e, p, KT, 2, uh, ul, ctx, between=spread_expert if first_of_expert else None,
                                     ready=ready).then_inc(e.slot_done, 1)

                g0, g1 = START[f"{up}{half}"]
                if front is not None and half == 0:
                    slots(pe, g0, g0 + 1, lambda *s: up_slot(*s, ready=lambda k: pe.wait_ge(front.lo_ready, k + 1)))
                    slots(pe, g0 + 1, g1, up_slot)
                elif route is not None and half == 0:
                    slots(pe, g0, g0 + 2, lambda *s: up_slot(*s, spreads=False))
                    route_pe_rows(pe)
                    pe.wait_ge(row_ready, 1)
                    nc.tensor.matmul(e.bank[6][:, 0:w], e.ones[0:NE, :], combine[1][:, :], start=True, stop=True
                                     ).then_inc(spread, 1)
                    slots(pe, g0 + 2, g1, up_slot)
                else:
                    slots(pe, g0, g1, up_slot)

                def down_slot(nm, i, p, g, ih, gh, ready=None):
                    pe_slot_begin(e, pe, g)
                    pe_feature_major(e, p, htiles, 1, hh, hl, ctx, ready=ready).then_inc(e.slot_done, 1)

                d0, d1 = START[f"{down}{half}"]
                slots(pe, d0, d0 + 1, lambda *s: down_slot(*s, ready=lambda k: pe.wait_ge(lo_ready, htiles * half + k + 1)))
                slots(pe, d0 + 1, d1, down_slot)

        @block.scalar
        def _(act):
            if front is not None:
                front.act(act)
            if route is not None:
                route_act(act)
            for half in range(2):
                def silu_slot(nm, i, p, g, ih, gh):
                    act.wait_ge(e.slot_done, g + 1)
                    if not (isinstance(g, int) and g < 2):
                        act.wait_ge(e.acc_free, g - 1)
                    last = nc.scalar.activation(sil[p][:, 0:T], e.bank[2 * p][:, :], ACT.Silu)
                    if ctx:
                        last = nc.scalar.activation(sil[p][:, T:W], e.bank[4 + p][:, 0:TC], ACT.Silu)
                    last.then_inc(silu_ready, 1)
                    act.wait_ge(e.acc_free, g + 1)
                    nc.scalar.activation(tile_at(hh, i), v[p][:, :], ACT.Copy).then_inc(hi_ready, 1)

                slots(act, *START[f"{up}{half}"], silu_slot)
            slots(act, *START[f"{down}1"], lambda nm, i, p, g, ih, gh: running.act(act, tile_at(y, i), i, p, g))

        @block.vector
        def _(dve):
            if front is not None:
                front.dve(dve)
                dve.wait_ge(e.slot_done, a + 1)
            if route is not None:
                route_dve(dve)
                dve.wait_ge(rows_ready, 1)
            running.dve_start(dve)

            def lone_row(x):
                one = e.ident[0:NE, x:x + 1] if isinstance(x, int) else e.ident[0:NE, ds(x, 1)]
                nc.vector.tensor_scalar(combine[1][:, :], combine[0][:, :], one, None, ALU.mult).then_inc(row_ready, 1)

            if combine is not None:
                lone_row(0)
            for half in range(2):
                def mul_slot(nm, i, p, g, ih, gh):
                    n = i + half * htiles
                    dve.wait_ge(silu_ready, n + 1)
                    if combine is not None:
                        dve.wait_ge(spread, ih + half * htiles // 2 + 1)
                        nc.vector.tensor_tensor(sil[p][:, :], sil[p][:, :], e.bank[6][:, 0:w], ALU.mult
                                                ).then_inc(gated, 1)
                        dve.wait_ge(gated, n + 1)
                    last = nc.vector.tensor_tensor(v[p][:, 0:T], sil[p][:, 0:T], e.bank[2 * p + 1][:, :], ALU.mult)
                    if ctx:
                        last = nc.vector.tensor_tensor(v[p][:, T:W], sil[p][:, T:W], e.bank[4 + p][:, TC:2 * TC],
                                                       ALU.mult)
                    last.then_inc(e.acc_free, 1)
                    dve.wait_ge(hi_ready, n + 1)
                    nc.vector.tensor_tensor(tile_at(hl, i), v[p][:, :], tile_at(hh, i).bitcast(F32), ALU.subtract
                                            ).then_inc(lo_ready, 1)
                    if combine is not None and p != a % 2:
                        lone_row(half * htiles // 2 + ih + 1)

                slots(dve, *START[f"{up}{half}"], mul_slot)

                def out_slot(nm, i, p, g, ih, gh):
                    dve.wait_ge(e.slot_done, g + 1)
                    yv = tile_at(y, i)
                    pieces = [(yv[:, 0:T], e.bank[2 * p][:, :])]
                    if ctx:
                        pieces.append((yv[:, T:W], e.bank[4 + p][:, 0:TC]))
                    for dst, src in pieces:
                        if half == 1:
                            last = nc.vector.tensor_tensor(dst, dst, src, ALU.add)
                        elif base is not None:
                            last = nc.vector.scalar_tensor_tensor(dst, tile_at(base, i), ALPHA, src, ALU.mult, ALU.add)
                        else:
                            last = nc.vector.tensor_copy(dst, src)
                    last.then_inc(e.acc_free, 1)
                    if half == 1:
                        running.dve(dve, yv, i, p, g)

                slots(dve, *START[f"{down}{half}"], out_slot)
    if front is not None:
        front.st.close()
    if route is not None:
        for r in route_stages:
            r.close()
    st.close()
    return running.acc


class Product:

    def __init__(self, seg, pe_body, act_body=None, dve_body=None, ready=None, act_start=None, dve_start=None,
                 sp_start=None, sp_end=None, stages=(), straight=False):
        self.straight = straight
        self.seg, self.pe_body, self.act_body, self.dve_body, self.ready = seg, pe_body, act_body, dve_body, ready
        self.act_start, self.dve_start, self.sp_start, self.sp_end, self.stages = (
            act_start, dve_start, sp_start, sp_end, stages)


def products(e, runs):
    sp_span, pool_span = feed_ahead(e, START[runs[-1].seg][1])
    with e.nc.Block() as block:
        @block.sync
        def _(sp):
            fed = sp_span[0]
            for r in runs:
                if r.sp_start is not None:
                    upto = max(fed, min(START[r.seg][0] + 2, sp_span[1])) if r is not runs[0] else fed
                    feed_sp(e, sp, (fed, upto))
                    fed = upto
                    r.sp_start(sp)
            feed_sp(e, sp, (fed, sp_span[1]))
            for r in runs:
                if r.sp_end is not None:
                    r.sp_end(sp)

        @block.gpsimd
        def _(pool):
            feed_pool(e, pool, pool_span)

        @block.tensor
        def _(pe):
            for r in runs:
                def body(nm, i, p, g, ih, gh, ready=None):
                    pe_slot_begin(e, pe, g)
                    r.pe_body(pe, p, i, ready).then_inc(e.slot_done, 1)

                a, b = START[r.seg]
                if r.ready is not None:
                    slots(pe, a, a + 1, lambda *s: body(*s, ready=lambda k: r.ready(pe, k)))
                    a += 1
                slots(pe, a, b, body, r.straight)

        @block.scalar
        def _(act):
            for r in runs:
                if r.act_start is not None:
                    r.act_start(act)
                if r.act_body is not None:
                    slots(act, *START[r.seg], lambda nm, i, p, g, ih, gh: r.act_body(act, i, p, g),
                          r.straight)

        @block.vector
        def _(dve):
            for r in runs:
                if r.dve_start is not None:
                    r.dve_start(dve)
                if r.dve_body is not None:
                    slots(dve, *START[r.seg], lambda nm, i, p, g, ih, gh: r.dve_body(dve, i, p, g),
                          r.straight)
    for r in runs:
        for st in r.stages:
            st.close()


def project_1(e, uh, ul, K, Q, V, XF, GR, bias_tok, front):
    st = Stage(e, "proj")
    nc = e.nc
    raw = [st.sb(f"raw{n}", [P, W], TMP + n * W * 4) for n in range(2)]
    con = [st.sb(f"con{n}", [P, W], TMP + (2 + n) * W * 4) for n in range(2)]
    bias_in, tap_done, silu_done, spilled = (st.sem(n) for n in ("bias_in", "tap_done", "silu_done", "spilled"))
    a, b = START["gates"][0], START["wxf"][1]
    conv_w, conv_b = PARAM_AT["conv_w"], PARAM_AT["conv_b"]

    def column(at, i, n):
        return e.params[:, at + 2 * i + n:at + 2 * i + n + 1] if isinstance(i, int) else \
            e.params[:, ds(at + n + 2 * i, 1)]

    sp_span, pool_span = feed_ahead(e, b)
    with nc.Block() as block:
        @block.sync
        def _(sp):
            front.sp(sp)
            sp.wait_ge(front.lo_ready, KT)
            sp.dma_start(bias_tok[:, :], e.dram["bias_tok"]).then_inc(bias_in, 16)
            sp.dma_start(e.dram["uh_s"], uh[:, :, 0:T].bitcast(F32)).then_inc(spilled, 16)
            sp.dma_start(e.dram["ul_s"], ul[:, :, 0:T].bitcast(F32)).then_inc(spilled, 16)
            feed_sp(e, sp, sp_span)
            sp.wait_ge(spilled, 32)

        @block.gpsimd
        def _(pool):
            feed_pool(e, pool, pool_span)

        @block.tensor
        def _(pe):
            front.pe(pe)

            def fm(ntile, ctx, ready=None):
                def body(nm, i, p, g, ih, gh):
                    pe_slot_begin(e, pe, g)
                    pe_feature_major(e, p, KT, ntile, uh, ul, ctx, ready=ready).then_inc(e.slot_done, 1)
                return body

            def tm(ctx):
                def body(nm, i, p, g, ih, gh):
                    pe_slot_begin(e, pe, g)
                    pe_token_major(e, p, 256, uh, ul, ctx).then_inc(e.slot_done, 1)
                return body

            slots(pe, *START["gates"], fm(1, True, ready=lambda k: pe.wait_ge(front.lo_ready, k + 1)))
            slots(pe, *START["wk"], fm(2, True))
            slots(pe, *START["wq"], fm(2, False))
            slots(pe, *START["wv"], tm(True))
            slots(pe, *START["wxf"], tm(False))

        @block.scalar
        def _(act):
            g0 = START["gates"][0]
            at = PARAM_AT["bgate"]
            front.act(act)
            act.wait_ge(e.slot_done, g0 + 1)
            act.wait_ge(front.stored, 16)
            nc.scalar.activation(GR[:, 0:T], e.bank[2 * (g0 % 2)][:, :], ACT.Identity, bias=e.params[:, at:at + 1])
            nc.scalar.activation(GR[:, T:W], e.bank[4 + g0 % 2][:, 0:TC], ACT.Identity,
                                 bias=e.params[:, at:at + 1]).then_inc(e.acc_free, 1)

            def rows(dst, w, bias_at, conv_at, m0):
                def body(nm, i, p, g, ih, gh):
                    act.wait_ge(e.slot_done, g + 1)
                    for n in range(2):
                        last = nc.scalar.activation(raw[n][:, 0:T], e.bank[2 * p + n][:, :], ACT.Identity,
                                                    bias=column(bias_at, i, n))
                        if w == W:
                            last = nc.scalar.activation(raw[n][:, T:W], e.bank[4 + p][:, n * TC:(n + 1) * TC],
                                                        ACT.Identity, bias=column(bias_at, i, n))
                    last.then_inc(e.acc_free, 1)
                    for n in range(2):
                        act.wait_ge(tap_done, 3 * m0 + 3 * n + 3 + 6 * i)
                        out = dst[:, 2 * i + n, 0:w] if isinstance(i, int) else \
                            dst[:, ds(n + 2 * i, 1), 0:w].rearrange("p a w -> p (a w)")
                        nc.scalar.activation(out, con[n][:, 0:w], ACT.Silu, bias=column(conv_at, i, n)
                                             ).then_inc(silu_done, 1)
                return body

            slots(act, *START["wk"], rows(K, W, PARAM_AT["bk"], conv_b + 8, 0))
            slots(act, *START["wq"], rows(Q, T, PARAM_AT["bq"], conv_b, 8))

        @block.vector
        def _(dve):
            front.dve(dve)

            def conv(w, conv_at, m0):
                def body(nm, i, p, g, ih, gh):
                    dve.wait_ge(e.acc_free, g + 1)
                    for n in range(2):
                        if m0:
                            dve.wait_ge(silu_done, m0 + n - 1 + 2 * i)
                        elif isinstance(i, int):
                            if i:
                                dve.wait_ge(silu_done, n - 1 + 2 * i)
                        tap = [column(conv_at + 16 * j, i, n) for j in range(3)]
                        nc.vector.tensor_scalar(con[n][:, 0:w], raw[n][:, 0:w], tap[1], None, ALU.mult
                                                ).then_inc(tap_done, 1)
                        dve.wait_ge(tap_done, 3 * m0 + 3 * n + 1 + 6 * i)
                        for c, _ in parts_of(w):
                            lo, hi = c.start, c.stop
                            last = nc.vector.scalar_tensor_tensor(con[n][:, lo + 1:hi], raw[n][:, lo:hi - 1], tap[0],
                                                                  con[n][:, lo + 1:hi], ALU.mult, ALU.add)
                        last.then_inc(tap_done, 1)
                        dve.wait_ge(tap_done, 3 * m0 + 3 * n + 2 + 6 * i)
                        for c, _ in parts_of(w):
                            lo, hi = c.start, c.stop
                            last = nc.vector.scalar_tensor_tensor(con[n][:, lo:hi - 1], raw[n][:, lo + 1:hi], tap[2],
                                                                  con[n][:, lo:hi - 1], ALU.mult, ALU.add)
                        last.then_inc(tap_done, 1)
                return body

            k0, k1 = START["wk"]
            slots(dve, k0, k0 + 1, conv(W, conv_w + 8, 0))
            slots(dve, k0 + 1, k1, conv(W, conv_w + 8, 0))
            slots(dve, *START["wq"], conv(T, conv_w, 8))
            dve.wait_ge(bias_in, 16)

            def add_bias(dst, bias_at, ntok):
                def body(nm, i, p, g, ih, gh):
                    dve.wait_ge(e.slot_done, g + 1)
                    for t in range(ntok):
                        bank = e.bank[2 * p + t // 2] if t < NCH else e.bank[4 + p]
                        cols = slice(256 * i, 256 * i + 256) if isinstance(i, int) else ds(256 * i, 256)
                        bcol = slice(bias_at + 256 * i, bias_at + 256 * i + 256) if isinstance(i, int) else \
                            ds(bias_at + 256 * i, 256)
                        last = nc.vector.tensor_tensor(dst[:, t, cols], bank[:, (t % 2) * 256:(t % 2 + 1) * 256],
                                                       bias_tok[:, bcol], ALU.add)
                    last.then_inc(e.acc_free, 1)
                return body

            slots(dve, *START["wv"], add_bias(V, 0, NCH + NCC))
            slots(dve, *START["wxf"], add_bias(XF, D, NCH))
    front.st.close()
    st.close()


STEPS = [[(T + P * j, None) for j in range(NCC)] + [(P * j, j) for j in range(NCH)],
         [(T + P * j, None) for j in reversed(range(NCC))] + [(P * j, j) for j in reversed(range(NCH))]]


def scan_rows(e, GR, B, LF, G, RT, MP, GC):
    st = Stage(e, "rows")
    nc = e.nc
    R = 36
    zero = st.sb("zero", [R, P], TMP)
    t1 = st.sb("t1", [R, W], TMP + 1024)
    t2 = st.sb("t2", [R, W], TMP + 1024 + W * 4)
    pre_ready, abs_ready, exp_ready, ln_ready, g_ready, gc_psum, chain = (
        st.sem(n) for n in ("pre_ready", "abs_ready", "exp_ready", "ln_ready", "g_ready", "gc_psum", "chain"))
    with nc.Block() as block:
        @block.sync
        def _(sp):
            sp.nop()

        @block.scalar
        def _(act):
            act.wait_ge(pre_ready, 1)
            nc.scalar.activation(t1[:, :], LF[:, :], ACT.Abs).then_inc(abs_ready, 1)
            act.wait_ge(abs_ready, 1)
            nc.scalar.activation(t2[:, :], t1[:, :], ACT.Exp, scale=-1.0).then_inc(exp_ready, 1)
            act.wait_ge(exp_ready, 1)
            nc.scalar.activation(t1[:, :], t2[:, :], ACT.Ln, bias=e.one_col[0:R, 0:1]).then_inc(ln_ready, 1)

        @block.tensor
        def _(pe):
            pe.wait_ge(g_ready, 1)
            for j in range(NCH + NCC):
                last = nc.tensor.matmul(e.bank[0][:, j * R:(j + 1) * R], G[0:R, j * P:(j + 1) * P],
                                        e.ident[0:R, 0:R], start=True, stop=True)
            last.then_inc(gc_psum, 1)

        @block.vector
        def _(dve):
            done = [0]

            def link(ins):
                done[0] += 1
                ins.then_inc(chain, 1)
                dve.wait_ge(chain, done[0])

            nc.vector.tensor_copy(LF[:, :], GR[64:64 + R, :]).then_inc(pre_ready, 1)
            nc.vector.memset(zero[:, :], 0.0)
            nc.vector.memset(MP[:, :], 0.0)
            link(nc.vector.memset(B[:, :], 0.0))
            dve.wait_ge(ln_ready, 1)
            link(nc.vector.scalar_tensor_tensor(LF[:, :], LF[:, :], 0.0, t1[:, :], ALU.min, ALU.subtract))
            cut = [[(slice(32 * d, 32 * d + MH), slice(c, c + P)) for c, _ in STEPS[d]] for d in range(2)]

            def walk(ap, d):
                return ap[:, ::-1] if d else ap

            for d in range(2):
                for r, c in cut[d]:
                    last = nc.vector.tensor_tensor_scan(walk(B[r, c], d), walk(zero[0:MH, :], d), walk(LF[r, c], d), 0.0,
                                                        ALU.add, ALU.add) if d == 0 else \
                        nc.vector.tensor_tensor_scan(walk(B[r, c], d), walk(zero[r, :], d), walk(LF[r, c], d), 0.0,
                                                     ALU.add, ALU.add)
            link(last)
            nc.vector.tensor_tensor(G[0:R, :], GR[0:R, :], B[:, :], ALU.subtract).then_inc(g_ready, 1)
            dve.wait_ge(g_ready, 1)
            for j in range(NCH + NCC):
                for d in range(2):
                    r, c = cut[d][j]
                    last = nc.vector.tensor_tensor_scan(walk(RT[r, 0, c], d), walk(G[r, c], d), walk(G[r, c], d),
                                                        MP[r, j:j + 1], ALU.max, ALU.max)
                link(last)
                for d in range(2):
                    r, c = cut[d][j]
                    end = c.start if d else c.stop - 1
                    last = nc.vector.tensor_tensor(MP[r, j + 1:j + 2], B[r, end:end + 1], RT[r, 0, end:end + 1], ALU.add)
                    nc.vector.tensor_scalar(RT[r, 1, c], RT[r, 0, c], MP[r, j:j + 1], -1.0, ALU.subtract, ALU.mult)
                    last = nc.vector.scalar_tensor_tensor(RT[r, 2, c], B[r, c], -1.0, RT[r, 0, c],
                                                          ALU.mult, ALU.subtract)
                link(last)
            dve.wait_ge(gc_psum, 1)
            nc.vector.tensor_copy(GC[:, :, :], e.bank[0][:, 0:(NCH + NCC) * R].rearrange("p (j r) -> p j r", r=R))
    st.close()


def scan(e, Q, K, V, C, HT, RT, GC, SEL, MASK):
    st = Stage(e, "scan")
    nc = e.nc
    NV = DH + P
    units = [(j, h, d) for j in range(NCC + NCH) for h in range(MH) for d in range(2)]
    lat = [u[0] >= NCC for u in units]
    upd = [u[0] < NCC + NCH - 1 for u in units]
    nlat = [sum(lat[:n]) for n in range(len(units) + 1)]
    nupd = [sum(upd[:n]) for n in range(len(units) + 1)]
    off = [TMP]

    def pair(n, cols):
        out = [st.sb(f"{n}{r}", [P, cols], off[0] + r * cols * 4) for r in range(2)]
        off[0] += 2 * cols * 4
        return out

    AE, W1, WM, SW, KW, QA, DEN, RD, WKS = (
        pair(n, c) for n, c in (("ae", 256), ("w1", P), ("wm", P), ("sw", P), ("kw", 256), ("qa", 256), ("den", P),
                                ("rd", P), ("wks", 8)))
    HTMP = pair("htmp", 256)
    assert off[0] <= MAIN
    sel_in, zeroed, a_ready, w1_ready, ae_ready, w_ready, sw_ready, wks_ready, kw_ready, qa_ready, num_ready, \
        upd_ready, c_ready, abs_ready, max_ready, rd_ready, mul_ready, h_ready = (
            st.sem(n) for n in ("sel_in", "zeroed", "a_ready", "w1_ready", "ae_ready", "w_ready", "sw_ready",
                                "wks_ready", "kw_ready", "qa_ready", "num_ready", "upd_ready", "c_ready", "abs_ready",
                                "max_ready", "rd_ready", "mul_ready", "h_ready"))

    def where(u):
        j, h, d = units[u]
        return j, h, d, STEPS[d][j][0], u % 2, (0 if d else P - 1)

    with nc.Block() as block:
        @block.sync
        def _(sp):
            sp.dma_start(SEL[:, :], e.dram["sel"]).then_inc(sel_in, 16)
            sp.dma_start(MASK[:, :], e.dram["scan_mask"]).then_inc(sel_in, 16)
            sp.wait_ge(sel_in, 32)

        @block.tensor
        def _(pe):
            def first(u):
                j, h, d, c, p, end = where(u)
                if u >= 2:
                    pe.wait_ge(kw_ready, u - 1)
                    pe.wait_ge(ae_ready, u - 1)
                if lat[u]:
                    for t in range(2):
                        nc.tensor.matmul(e.bank[p][:, 0:P], K[:, 2 * h + t, c:c + P], Q[:, 2 * h + t, c:c + P],
                                         start=t == 0, stop=t == 1)
                for t in range(2):
                    nc.tensor.transpose(e.bank[p][:, P + t * P:2 * P + t * P], K[:, 2 * h + t, c:c + P], e.ident[:, :])
                nc.tensor.matmul(e.bank[2 + p][:, 0:3 * P], SEL[32 * d:32 * d + MH, h * P:(h + 1) * P],
                                 RT[32 * d:32 * d + MH, :, c:c + P], start=True, stop=True).then_inc(a_ready, 1)

            def second(u):
                j, h, d, c, p, end = where(u)
                cs = C[2 * h + d]
                prev = u - 2 * MH
                if prev >= 0:
                    pe.wait_ge(c_ready, nupd[prev + 1])
                if lat[u]:
                    pe.wait_ge(sw_ready, nlat[u] + 1)
                    pe.wait_ge(qa_ready, nlat[u] + 1)
                    if nlat[u] >= 2:
                        pe.wait_ge(h_ready, nlat[u] - 1)
                    vt = c // P
                    for m in range(3):
                        out = e.bank[4 + p][:, m * P:(m + 1) * P]
                        for t in range(2):
                            nc.tensor.matmul(out, cs[:, t, m * P:(m + 1) * P], QA[p][:, t * P:(t + 1) * P],
                                             start=t == 0, stop=False)
                        vm = V[:, vt, h * DH + m * P:h * DH + (m + 1) * P] if m < 2 else e.ones[:, :]
                        last = nc.tensor.matmul(out, vm, SW[p][:, :], start=False, stop=True)
                    last.then_inc(num_ready, 1)
                if upd[u]:
                    pe.wait_ge(kw_ready, u + 1)
                    if nupd[u]:
                        pe.wait_ge(c_ready, nupd[u])
                    for t in range(2):
                        nc.tensor.matmul(e.bank[6 + t][:, 0:DH], KW[p][:, t * P:(t + 1) * P],
                                         V[:, c // P, h * DH:(h + 1) * DH], start=True, stop=True)
                        last = nc.tensor.matmul(e.bank[6 + t][:, DH:NV], KW[p][:, t * P:(t + 1) * P], e.ones[:, :],
                                                start=True, stop=True)
                    last.then_inc(upd_ready, 1)

            pe.wait_ge(sel_in, 32)
            first(0)
            for u in range(len(units)):
                if u + 1 < len(units):
                    first(u + 1)
                second(u)

        @block.scalar
        def _(act):
            def first(u):
                j, h, d, c, p, end = where(u)
                act.wait_ge(w1_ready, u + 1)
                if u >= 2:
                    act.wait_ge(c_ready, nupd[u - 1])
                    if nlat[u - 1]:
                        act.wait_ge(h_ready, nlat[u - 1])
                        act.wait_ge(max_ready, nlat[u - 1])
                nc.scalar.activation(AE[p][:, :], e.bank[2 + p][:, P:3 * P], ACT.Exp).then_inc(ae_ready, 1)
                if u >= 2:
                    act.wait_ge(wks_ready, u - 1)
                nc.scalar.activation(WM[p][:, :], W1[p][:, :], ACT.Exp, scale=-1.0).then_inc(w_ready, 1)
                act.wait_ge(wks_ready, u + 1)
                if u >= 2 and nupd[u - 1]:
                    act.wait_ge(upd_ready, nupd[u - 1])
                nc.scalar.activation(KW[p][:, :], e.bank[p][:, P:3 * P], ACT.Copy, scale=WKS[p][:, 0:1]
                                     ).then_inc(kw_ready, 1)

            def second(u):
                p = u % 2
                if lat[u]:
                    act.wait_ge(num_ready, nlat[u] + 1)
                    if nlat[u] >= 2:
                        act.wait_ge(max_ready, nlat[u] - 1)
                    nc.scalar.activation(DEN[p][:, :], e.bank[4 + p][:, DH:NV], ACT.Abs).then_inc(abs_ready, 1)

            first(0)
            for u in range(len(units)):
                if u + 1 < len(units):
                    first(u + 1)
                second(u)

        @block.vector
        def _(dve):
            for t in C[:-1]:
                nc.vector.memset(t[:, :, :], 0.0)
            nc.vector.memset(C[-1][:, :, :], 0.0).then_inc(zeroed, 1)
            dve.wait_ge(sel_in, 32)
            dve.wait_ge(zeroed, 1)

            def first(u):
                j, h, d, c, p, end = where(u)
                dve.wait_ge(a_ready, u + 1)
                if u >= 2:
                    dve.wait_ge(w_ready, u - 1)
                nc.vector.scalar_tensor_tensor(W1[p][:, :], e.bank[2 + p][:, 0:P], GC[:, c // P, 32 * d + h:32 * d + h + 1],
                                               MASK[:, d * P:(d + 1) * P], ALU.subtract, ALU.add).then_inc(w1_ready, 1)
                dve.wait_ge(w_ready, u + 1)
                if lat[u]:
                    if nlat[u] >= 2:
                        dve.wait_ge(num_ready, nlat[u] - 1)
                    nc.vector.scalar_tensor_tensor(SW[p][:, :], e.bank[p][:, 0:P], DH ** -0.5, WM[p][:, :],
                                                   ALU.mult, ALU.mult).then_inc(sw_ready, 1)
                if u >= 2:
                    dve.wait_ge(kw_ready, u - 1)
                nc.vector.tensor_scalar(WKS[p][:, 0:1], WM[p][:, end:end + 1], DH ** -0.5, None, ALU.mult
                                        ).then_inc(wks_ready, 1)
                if lat[u]:
                    dve.wait_ge(ae_ready, u + 1)
                    for t in range(2):
                        last = nc.vector.tensor_tensor(QA[p][:, t * P:(t + 1) * P], Q[:, 2 * h + t, c:c + P],
                                                       AE[p][:, 0:P], ALU.mult)
                    last.then_inc(qa_ready, 1)

            def second(u):
                j, h, d, c, p, end = where(u)
                cs = C[2 * h + d]
                if upd[u]:
                    dve.wait_ge(upd_ready, nupd[u] + 1)
                    dve.wait_ge(ae_ready, u + 1)
                    if lat[u]:
                        dve.wait_ge(num_ready, nlat[u] + 1)
                    if u >= 2 * MH:
                        dve.wait_ge(c_ready, nupd[u - 2 * MH + 1])
                    for t in range(2):
                        last = nc.vector.scalar_tensor_tensor(cs[:, t, :], cs[:, t, :], AE[p][:, end:end + 1],
                                                              e.bank[6 + t][:, 0:NV], ALU.mult, ALU.add)
                    last.then_inc(c_ready, 1)
                if lat[u]:
                    n = nlat[u]
                    dve.wait_ge(abs_ready, n + 1)
                    dve.wait_ge(ae_ready, u + 1)
                    nc.vector.tensor_tensor(DEN[p][:, :], DEN[p][:, :], AE[p][:, P:2 * P], ALU.max).then_inc(max_ready, 1)
                    dve.wait_ge(max_ready, n + 1)
                    nc.vector.reciprocal(RD[p][:, :], DEN[p][:, :]).then_inc(rd_ready, 1)
                    dve.wait_ge(rd_ready, n + 1)
                    dst = HT[:, 2 * h:2 * h + 2, c:c + P]
                    fresh = (d == 0) == (c < T // 2)
                    for t in range(2):
                        out = dst[:, t, :] if fresh else HTMP[p][:, t * P:(t + 1) * P]
                        last = nc.vector.tensor_tensor(out, e.bank[4 + p][:, t * P:(t + 1) * P], RD[p][:, :], ALU.mult)
                    if fresh:
                        last.then_inc(h_ready, 1)
                    else:
                        last.then_inc(mul_ready, 1)
                        dve.wait_ge(mul_ready, sum(1 for x in range(u + 1) if lat[x] and (units[x][2] == 0) != (
                            STEPS[units[x][2]][units[x][0]][0] < T // 2)))
                        nc.vector.tensor_tensor(dst, dst, HTMP[p][:, :].rearrange("p (t c) -> p t c", t=2), ALU.add
                                                ).then_inc(h_ready, 1)

            first(0)
            for u in range(len(units)):
                if u + 1 < len(units):
                    first(u + 1)
                second(u)
    st.close()


def fourier(e, XF, yh, yl, at, uh, ul):
    st = Stage(e, "four")
    nc = e.nc
    dft_t = st.sb("dft_t", [P, 2, NCH, T], at)
    dft_c = st.sb("dft_c", [P, 2, P], at + 49152)
    AB = st.sb("ab", [P, 2, 4, T], at + 16384)
    y = [st.sb(f"y{r}", [P, T], TMP + r * T * 4) for r in range(2)]
    const_in, ab_psum, ab_ready, y_psum, y_ready, hi_ready, lo_ready, u_in = (
        st.sem(n) for n in ("const_in", "ab_psum", "ab_ready", "y_psum", "y_ready", "hi_ready", "lo_ready", "u_in"))
    dft_in = [st.sem(f"dft_in{s}") for s in range(2)]
    with nc.Block() as block:
        @block.sync
        def _(sp):
            for s in range(2):
                sp.dma_start(dft_t[:, s, :, :], e.dram["dft_t"][:, s]).then_inc(dft_in[s], 16)
            sp.dma_start(dft_c[:, :, :], e.dram["dft_c"]).then_inc(const_in, 16)
            sp.dma_start(uh[:, :, :].bitcast(F32), e.dram["uh_s"]).then_inc(u_in, 16)
            sp.dma_start(ul[:, :, :].bitcast(F32), e.dram["ul_s"]).then_inc(u_in, 16)
            sp.wait_ge(u_in, 32)

        @block.tensor
        def _(pe):
            for n in range(8):
                gc, s = n % 4, n // 4
                pe.wait_ge(dft_in[s], 16)
                if n >= 2:
                    pe.wait_ge(ab_ready, n - 1)
                for t in range(NCH):
                    last = nc.tensor.matmul(e.bank[n % 2][:, :], XF[:, t, gc * P:(gc + 1) * P], dft_t[:, s, t, :],
                                            start=t == 0, stop=t == NCH - 1)
                last.then_inc(ab_psum, 1)
            for gc in range(4):
                pe.wait_ge(const_in, 16)
                pe.wait_ge(ab_ready, gc + 5)
                if gc >= 2:
                    pe.wait_ge(y_ready, gc - 1)
                for s in range(2):
                    last = nc.tensor.matmul(e.bank[2 + gc % 2][:, :], dft_c[:, s, :], AB[:, s, gc, :],
                                            start=s == 0, stop=s == 1)
                last.then_inc(y_psum, 1)

        @block.scalar
        def _(act):
            for n in range(8):
                act.wait_ge(ab_psum, n + 1)
                nc.scalar.activation(AB[:, n // 4, n % 4, :], e.bank[n % 2][:, :], ACT.Copy).then_inc(ab_ready, 1)
            for gc in range(4):
                act.wait_ge(y_ready, gc + 1)
                nc.scalar.activation(yh[:, gc, :], y[gc % 2][:, :], ACT.Copy).then_inc(hi_ready, 1)

        @block.vector
        def _(dve):
            for gc in range(4):
                dve.wait_ge(y_psum, gc + 1)
                nc.vector.tensor_copy(y[gc % 2][:, :], e.bank[2 + gc % 2][:, :]).then_inc(y_ready, 1)
                dve.wait_ge(hi_ready, gc + 1)
                nc.vector.tensor_tensor(yl[:, gc, :], y[gc % 2][:, :], yh[:, gc, :].bitcast(F32), ALU.subtract
                                        ).then_inc(lo_ready, 1)
    st.close()


def column_of(e, at, i, n):
    return e.params[:, at + 2 * i + n:at + 2 * i + n + 1] if isinstance(i, int) else e.params[:, ds(at + n + 2 * i, 1)]


def tile2(t, i, n):
    return t[:, 2 * i + n, :] if isinstance(i, int) else t[:, ds(n + 2 * i, 1), :].rearrange("p a w -> p (a w)")


class HeadNorm:

    def __init__(self, e, name, x, per, gain, gate, oh, ol):
        self.e, self.st = e, Stage(e, name)
        self.x, self.per, self.gain, self.gate, self.oh, self.ol = x, per, gain, gate, oh, ol
        self.sq, self.r, self.t, self.v = ([self.st.sb(f"{n}{b}", [P, T], TMP + (2 * m + b) * T * 4) for b in range(2)]
                                           for m, n in enumerate(("sq", "r", "t", "v")))
        self.squared, self.mean_ready, self.std_ready, self.rstd_ready, self.t_ready, self.v_ready, self.hi_ready, \
            self.lo_ready = (self.st.sem(n) for n in ("squared", "mean_ready", "std_ready", "rstd_ready", "t_ready",
                                                      "v_ready", "hi_ready", "lo_ready"))

    def dve_start(self, dve):
        pass

    def pe(self, pe, i):
        e = self.e
        for n in range(2):
            pe.wait_ge(self.squared, 2 * i + n + 1)
            h = n // self.per
            e.nc.tensor.matmul(e.bank[6 + h][:, :], e.ones[:, :], self.sq[n][:, :], start=n % self.per == 0,
                               stop=n % self.per == self.per - 1).then_inc(self.mean_ready, 1)

    def act(self, act, i):
        e, nc = self.e, self.e.nc
        for n in range(2):
            nc.scalar.activation(self.sq[n][:, :], tile2(self.x, i, n), ACT.Square).then_inc(self.squared, 1)
        for h in range(2 // self.per):
            act.wait_ge(self.mean_ready, 2 * i + (h + 1) * self.per)
            nc.scalar.activation(self.r[h][:, :], e.bank[6 + h][:, :], ACT.Sqrt, scale=1.0 / (self.per * P),
                                 bias=e.eps[:, 0:1]).then_inc(self.std_ready, 1)
        for n in range(2):
            act.wait_ge(self.v_ready, 2 * i + n + 1)
            nc.scalar.activation(tile2(self.oh, i, n), self.v[n][:, :], ACT.Copy).then_inc(self.hi_ready, 1)

    def dve(self, dve, i):
        nc, heads = self.e.nc, 2 // self.per
        for h in range(heads):
            dve.wait_ge(self.std_ready, heads * i + h + 1)
            nc.vector.reciprocal(self.r[h][:, :], self.r[h][:, :]).then_inc(self.rstd_ready, 1)
        for n in range(2):
            h = n // self.per
            dve.wait_ge(self.rstd_ready, heads * i + h + 1)
            nc.vector.scalar_tensor_tensor(self.t[n][:, :], tile2(self.x, i, n), self.gain(i, n), self.r[h][:, :],
                                           ALU.mult, ALU.mult).then_inc(self.t_ready, 1)
        for n in range(2):
            dve.wait_ge(self.t_ready, 2 * i + n + 1)
            nc.vector.tensor_tensor(self.v[n][:, :], self.t[n][:, :], tile2(self.gate, i, n), ALU.mult
                                    ).then_inc(self.v_ready, 1)
        for n in range(2):
            dve.wait_ge(self.hi_ready, 2 * i + n + 1)
            nc.vector.tensor_tensor(tile2(self.ol, i, n), self.v[n][:, :], tile2(self.oh, i, n).bitcast(F32),
                                    ALU.subtract).then_inc(self.lo_ready, 1)


def product_act(e, seg, xh, xl, out, func, bias=None, norm=None, norm_ready=None, **more):
    def pe_body(pe, p, i, ready):
        return pe_feature_major(e, p, KT, 2, xh, xl, False, between=norm and (lambda: norm.pe(pe, i)), ready=ready)

    def act_body(act, i, p, g):
        if norm is not None:
            norm.act(act, i)
        act.wait_ge(e.slot_done, g + 1)
        for n in range(2):
            b = {} if bias is None else {"bias": column_of(e, PARAM_AT[bias], i, n)}
            last = e.nc.scalar.activation(tile2(out, i, n), e.bank[2 * p + n][:, :], func, **b)
        last.then_inc(e.acc_free, 1)

    def start(eng):
        eng.wait_ge(e.acc_free, norm_ready)

    def dve_start(dve):
        start(dve)
        norm.dve_start(dve)

    if norm is not None:
        more = dict(act_start=start, dve_start=dve_start, dve_body=lambda dve, i, p, g: norm.dve(dve, i),
                    stages=(norm.st,), **more)
    return Product(seg, pe_body, act_body, **more)


def product_gate(e, seg, kt, xh, xl, gate, ready=None):
    def dve_start(dve):
        dve.wait_ge(e.acc_free, START[seg][0])

    def dve_body(dve, i, p, g):
        dve.wait_ge(e.slot_done, g + 1)
        for n in range(2):
            t = tile2(gate, i, n)
            last = e.nc.vector.tensor_tensor(t, t, e.bank[2 * p + n][:, :], ALU.mult)
        last.then_inc(e.acc_free, 1)

    return Product(seg, lambda pe, p, i, ready: pe_feature_major(e, p, kt, 2, xh, xl, False, ready=ready),
                   dve_body=dve_body, dve_start=dve_start, ready=ready)


def product_gate_split(e, seg, xh, xl, gate, other, yh, yl, ready=None):
    st = Stage(e, seg + "_s")
    nc = e.nc
    t = [st.sb(f"t{r}", [P, T], TMP + r * T * 4) for r in range(2)]
    v = [st.sb(f"v{r}", [P, T], TMP + (2 + r) * T * 4) for r in range(2)]
    v_ready, hi_ready, lo_ready = (st.sem(n) for n in ("v_ready", "hi_ready", "lo_ready"))

    def dve_start(dve):
        dve.wait_ge(e.acc_free, START[seg][0])

    def act_body(act, i, p, g):
        act.wait_ge(v_ready, 1 + i)
        for n in range(2):
            last = nc.scalar.activation(tile2(yh, i, n), v[n][:, :], ACT.Copy)
        last.then_inc(hi_ready, 1)

    def dve_body(dve, i, p, g):
        dve.wait_ge(e.slot_done, g + 1)
        for n in range(2):
            last = nc.vector.tensor_tensor(t[n][:, :], tile2(gate, i, n), e.bank[2 * p + n][:, :], ALU.mult)
        last.then_inc(e.acc_free, 1)
        dve.wait_ge(e.acc_free, g + 1)
        for n in range(2):
            last = nc.vector.tensor_tensor(v[n][:, :], t[n][:, :], tile2(other, i, n), ALU.add)
        last.then_inc(v_ready, 1)
        dve.wait_ge(hi_ready, 1 + i)
        for n in range(2):
            last = nc.vector.tensor_tensor(tile2(yl, i, n), v[n][:, :], tile2(yh, i, n).bitcast(F32), ALU.subtract)
        last.then_inc(lo_ready, 1)

    run = Product(seg, lambda pe, p, i, ready: pe_feature_major(e, p, KT, 2, xh, xl, False, ready=ready),
                  act_body=act_body, dve_body=dve_body, dve_start=dve_start, ready=ready, stages=(st,))
    return run, lambda eng, k: eng.wait_ge(lo_ready, k // 2 + 1)


def product_out(e, seg, xh, xl, out, res, res_src, res_after, squares, ready):
    st = Stage(e, seg)
    res_in = st.sem("res_in")
    running = RunningSum(e, st, T, squares)

    def sp_start(sp):
        sp.wait_ge(e.slot_done, res_after)
        sp.dma_start(res[:, :, :], res_src).then_inc(res_in, 16)

    def sp_end(sp):
        sp.wait_ge(res_in, 16)

    def act_body(act, i, p, g):
        for n in range(2):
            running.act(act, tile2(out, i, n), 2 * i + n, n, g)

    def dve_start(dve):
        ready(dve, KT - 1)
        running.dve_start(dve)
        if not squares:
            dve.wait_ge(res_in, 16)

    def dve_body(dve, i, p, g):
        dve.wait_ge(e.slot_done, g + 1)
        for n in range(2):
            if squares:
                last = e.nc.vector.tensor_copy(tile2(out, i, n), e.bank[2 * p + n][:, :])
            else:
                last = e.nc.vector.scalar_tensor_tensor(tile2(out, i, n), tile2(res, i, n), ALPHA,
                                                        e.bank[2 * p + n][:, :], ALU.mult, ALU.add)
        last.then_inc(e.acc_free, 1)
        for n in range(2):
            running.dve(dve, tile2(out, i, n), 2 * i + n, n, g)

    return Product(seg, lambda pe, p, i, ready: pe_feature_major(e, p, KT, 2, xh, xl, False, ready=ready),
                   act_body=act_body, dve_body=dve_body, sp_start=sp_start, sp_end=sp_end, dve_start=dve_start,
                   ready=ready, stages=(st,)), running.acc


class DeltaRows:

    def __init__(self, e, GR, R, SEL, QKV, QD, COL, GL, at):
        self.e, self.st, self.GR, self.R, self.SEL, self.QKV, self.QD, self.COL, self.GL = (
            e, Stage(e, "drows"), GR, R, SEL, QKV, QD, COL, GL)
        self.x, self.t1, self.t2, self.zero = (self.st.sb(n, [DNH, T], at + m * T * 4)
                                               for m, n in enumerate(("x", "t1", "t2", "zero")))
        self.eg = [self.st.sb(f"eg{b}", [P, T], at + (4 + b) * T * 4) for b in range(2)]
        self.ea = self.st.sb("ea", [DNH, 1], at + 6 * T * 4)
        self.sel_in, self.x_ready, self.abs_ready, self.exp_ready, self.ln_ready, self.act_ready, self.g_ready, \
            self.eg_row, self.be_ready, self.kd_pre, self.kd_ready, self.col_psum, self.col_ready, self.g_psum, \
            self.eg_ready, self.qd_ready, self.chain = (self.st.sem(n) for n in (
                "sel_in", "x_ready", "abs_ready", "exp_ready", "ln_ready", "act_ready", "g_ready", "eg_row",
                "be_ready", "kd_pre", "kd_ready", "col_psum", "col_ready", "g_psum", "eg_ready", "qd_ready", "chain"))

    def sp(self, sp):
        sp.dma_start(self.SEL[:, :], self.e.dram["sel8"]).then_inc(self.sel_in, 16)

    def act_rows(self, act):
        nc, e, R, x, t1, t2, H = self.e.nc, self.e, self.R, self.x, self.t1, self.t2, DNH
        db, al = PARAM_AT["dt_bias"], PARAM_AT["a_log"]
        act.wait_ge(self.sel_in, 16)
        nc.scalar.activation(x[:, :], self.GR[0:H, :], ACT.Identity, bias=e.params[0:H, db:db + 1]
                             ).then_inc(self.x_ready, 1)
        act.wait_ge(self.x_ready, 1)
        nc.scalar.activation(t1[:, :], x[:, :], ACT.Abs).then_inc(self.abs_ready, 1)
        act.wait_ge(self.abs_ready, 1)
        nc.scalar.activation(t2[:, :], t1[:, :], ACT.Exp, scale=-1.0).then_inc(self.exp_ready, 1)
        nc.scalar.activation(self.ea[:, :], e.params[0:H, al:al + 1], ACT.Exp)
        act.wait_ge(self.exp_ready, 1)
        nc.scalar.activation(t1[:, :], t2[:, :], ACT.Ln, bias=e.one_col[0:H, 0:1]).then_inc(self.ln_ready, 1)
        nc.scalar.activation(R[:, 1, :], self.GR[32:32 + H, :], ACT.Sigmoid).then_inc(self.act_ready, 1)
        act.wait_ge(self.g_ready, 1)
        nc.scalar.activation(t2[:, :], R[:, 0, :], ACT.Exp).then_inc(self.eg_row, 1)
        act.wait_ge(self.kd_pre, 1)
        nc.scalar.activation(R[:, 3, :], x[:, :], ACT.Exp).then_inc(self.kd_ready, 1)

    def dve_rows(self, dve):
        nc, R, x, t1, zero = self.e.nc, self.R, self.x, self.t1, self.zero
        done = [0]

        def link(ins):
            done[0] += 1
            ins.then_inc(self.chain, 1)
            dve.wait_ge(self.chain, done[0])

        dve.wait_ge(self.sel_in, 16)
        link(nc.vector.memset(zero[:, :], 0.0))
        dve.wait_ge(self.ln_ready, 1)
        link(nc.vector.scalar_tensor_tensor(x[:, :], x[:, :], 0.0, t1[:, :], ALU.max, ALU.add))
        link(nc.vector.tensor_scalar(x[:, :], x[:, :], self.ea[:, 0:1], -1.0, ALU.mult, ALU.mult))
        for c in range(NCH):
            cc = slice(c * P, (c + 1) * P)
            last = nc.vector.tensor_tensor_scan(R[:, 0, cc], zero[:, cc], x[:, cc], 0.0, ALU.add, ALU.add)
        last.then_inc(self.g_ready, 1)
        dve.wait_ge(self.g_ready, 1)
        for c in range(NCH):
            cc = slice(c * P, (c + 1) * P)
            last = nc.vector.tensor_scalar(x[:, cc], R[:, 0, cc], R[:, 0, (c + 1) * P - 1:(c + 1) * P], -1.0,
                                           ALU.subtract, ALU.mult)
        last.then_inc(self.kd_pre, 1)
        dve.wait_ge(self.act_ready, 1)
        dve.wait_ge(self.eg_row, 1)
        nc.vector.tensor_tensor(R[:, 2, :], R[:, 1, :], self.t2[:, :], ALU.mult).then_inc(self.be_ready, 1)

    def pe_heads(self, pe, half):
        pe.wait_ge(self.sel_in, 16)
        pe.wait_ge(self.g_ready, 1)
        for h in range(4 * half, 4 * half + 4):
            if h >= 4:
                pe.wait_ge(self.eg_ready, h - 3)
            self.e.nc.tensor.matmul(self.e.bank[4 + h % 4][:, :], self.SEL[:, h * P:(h + 1) * P], self.R[:, 0, :],
                                    start=True, stop=True).then_inc(self.g_psum, 1)

    def act_heads(self, act, half):
        for h in range(4 * half, 4 * half + 4):
            act.wait_ge(self.g_psum, h + 1)
            if h >= 2:
                act.wait_ge(self.qd_ready, h - 1)
            self.e.nc.scalar.activation(self.eg[h % 2][:, :], self.e.bank[4 + h % 4][:, :], ACT.Exp
                                        ).then_inc(self.eg_ready, 1)

    def dve_heads(self, dve, half):
        nc, eg = self.e.nc, self.eg
        for h in range(4 * half, 4 * half + 4):
            dve.wait_ge(self.eg_ready, h + 1)
            nc.vector.tensor_copy(self.GL[:, h, :], eg[h % 2][:, P - 1:T:P])
            nc.vector.tensor_tensor(self.QD[:, h, :], self.QKV[:, h, :], eg[h % 2][:, :], ALU.mult
                                    ).then_inc(self.qd_ready, 1)

    def pe_columns(self, pe):
        e, H = self.e, DNH
        pe.wait_ge(self.be_ready, 1)
        pe.wait_ge(self.kd_ready, 1)
        pe.wait_ge(self.eg_ready, H)
        for c in range(NCH):
            for r in range(4):
                at = (c * 4 + r) * H
                last = e.nc.tensor.matmul(e.bank[4][:, at:at + H], self.R[:, r, c * P:(c + 1) * P], e.ident[0:H, 0:H],
                                          start=True, stop=True)
        last.then_inc(self.col_psum, 1)

    def dve_columns(self, dve):
        dve.wait_ge(self.col_psum, 1)
        self.e.nc.vector.tensor_copy(self.COL[:, :], self.e.bank[4][:, 0:NCH * 4 * DNH]).then_inc(self.col_ready, 1)


def project_2(e, xh, xl, QKV, GR, front, rows):
    st = Stage(e, "proj2")
    nc = e.nc
    raw = [st.sb(f"raw{n}", [P, T], TMP + n * T * 4) for n in range(2)]
    con = [st.sb(f"con{n}", [P, T], TMP + (2 + n) * T * 4) for n in range(2)]
    sq = [st.sb(f"sq{n}", [P, T], TMP + (4 + n) * T * 4) for n in range(2)]
    norm = [st.sb(f"norm{n}", [P, T], TMP + (6 + n) * T * 4) for n in range(2)]
    tap_done, silu_done, spilled, squared, sum_ready, norm_ready, inv_ready, normed = (
        st.sem(n) for n in ("tap_done", "silu_done", "spilled", "squared", "sum_ready", "norm_ready", "inv_ready",
                            "normed"))
    a, b = START["gates2"][0], START["wqkv2"][1]
    g0, g1 = START["wqkv2"]
    q_span, k_span = (g0 + 1, g0 + 1 + DNH // 2), (g0 + 1 + DNH // 2, g0 + 1 + DNH)
    conv_w = PARAM_AT["conv_w_2"]
    sp_span, pool_span = feed_ahead(e, b)
    with nc.Block() as block:
        @block.sync
        def _(sp):
            front.sp(sp)
            sp.wait_ge(front.lo_ready, KT)
            rows.sp(sp)
            sp.dma_start(e.dram["uh_s"], xh[:, :, :].bitcast(F32)).then_inc(spilled, 16)
            sp.dma_start(e.dram["ul_s"], xl[:, :, :].bitcast(F32)).then_inc(spilled, 16)
            feed_sp(e, sp, sp_span)
            sp.wait_ge(spilled, 32)

        @block.gpsimd
        def _(pool):
            feed_pool(e, pool, pool_span)

        @block.tensor
        def _(pe):
            front.pe(pe)

            def fm(ntile, ready=None):
                def body(nm, i, p, g, ih, gh):
                    pe_slot_begin(e, pe, g)
                    pe_feature_major(e, p, KT, ntile, xh, xl, False, ready=ready).then_inc(e.slot_done, 1)
                return body

            def with_norm(nm, i, p, g, ih, gh):
                fm(2)(nm, i, p, g, ih, gh)
                for n in range(2):
                    pe.wait_ge(squared, 2 * i + n - 1)
                    nc.tensor.matmul(e.bank[6 + n][:, :], e.ones[:, :], sq[n][:, :], start=True, stop=True
                                     ).then_inc(sum_ready, 1)

            slots(pe, *START["gates2"], fm(1, ready=lambda k: pe.wait_ge(front.lo_ready, k + 1)))
            slots(pe, g0, g0 + 1, fm(2))
            slots(pe, q_span[0], k_span[1], with_norm)
            slots(pe, k_span[1], k_span[1] + 1, fm(2))
            pe.wait_ge(norm_ready, 2 * DNH)
            rows.pe_heads(pe, 0)
            slots(pe, k_span[1] + 1, k_span[1] + 2, fm(2))
            rows.pe_heads(pe, 1)
            slots(pe, k_span[1] + 2, g1, fm(2))
            rows.pe_columns(pe)

        @block.scalar
        def _(act):
            front.act(act)
            act.wait_ge(e.slot_done, a + 1)
            nc.scalar.activation(GR[:, :], e.bank[2 * (a % 2)][:, :], ACT.Copy).then_inc(e.acc_free, 1)

            def body(nm, i, p, g, ih, gh):
                act.wait_ge(e.slot_done, g + 1)
                for n in range(2):
                    last = nc.scalar.activation(raw[n][:, :], e.bank[2 * p + n][:, :], ACT.Copy)
                last.then_inc(e.acc_free, 1)
                for n in range(2):
                    act.wait_ge(tap_done, 4 * n + 4 + 8 * i)
                    nc.scalar.activation(tile2(QKV, i, n), con[n][:, :], ACT.Silu).then_inc(silu_done, 1)

            def with_norm(nm, i, p, g, ih, gh):
                for n in range(2):
                    nc.scalar.activation(sq[n][:, :], tile2(QKV, i - 1, n), ACT.Square).then_inc(squared, 1)
                body(nm, i, p, g, ih, gh)
                act.wait_ge(silu_done, 2 * i + 2)
                for n in range(2):
                    act.wait_ge(sum_ready, 2 * i + n - 1)
                    nc.scalar.activation(norm[n][:, :], e.bank[6 + n][:, :], ACT.Sqrt, bias=e.eps[:, 0:1]
                                         ).then_inc(norm_ready, 1)

            act.wait_ge(e.acc_free, a + 1)
            rows.act_rows(act)
            slots(act, g0, g0 + 1, body)
            act.wait_ge(silu_done, 2)
            slots(act, q_span[0], k_span[1], with_norm)
            slots(act, k_span[1], k_span[1] + 1, body)
            rows.act_heads(act, 0)
            slots(act, k_span[1] + 1, k_span[1] + 2, body)
            rows.act_heads(act, 1)
            slots(act, k_span[1] + 2, g1, body)

        @block.vector
        def _(dve):
            front.dve(dve)

            def body(nm, i, p, g, ih, gh):
                dve.wait_ge(e.acc_free, g + 1)
                for n in range(2):
                    if not (isinstance(i, int) and i == 0):
                        dve.wait_ge(silu_done, n - 1 + 2 * i)
                    tap = [column_of(e, conv_w + 24 * j, i, n) for j in range(4)]
                    nc.vector.tensor_scalar(con[n][:, :], raw[n][:, :], tap[3], None, ALU.mult).then_inc(tap_done, 1)
                    for back in range(1, 4):
                        dve.wait_ge(tap_done, 4 * n + back + 8 * i)
                        nc.vector.scalar_tensor_tensor(con[n][:, back:], raw[n][:, :T - back], tap[3 - back],
                                                       con[n][:, back:], ALU.mult, ALU.add).then_inc(tap_done, 1)

            def with_norm(scale):
                def both(nm, i, p, g, ih, gh):
                    body(nm, i, p, g, ih, gh)
                    for n in range(2):
                        dve.wait_ge(norm_ready, 2 * i + n - 1)
                        nc.vector.reciprocal(norm[n][:, :], norm[n][:, :]).then_inc(inv_ready, 1)
                    for n in range(2):
                        dve.wait_ge(inv_ready, 2 * i + n - 1)
                        nc.vector.scalar_tensor_tensor(tile2(QKV, i - 1, n), tile2(QKV, i - 1, n), scale,
                                                       norm[n][:, :], ALU.mult, ALU.mult).then_inc(normed, 1)
                return both

            rows.dve_rows(dve)
            slots(dve, g0, g0 + 1, body)
            slots(dve, *q_span, with_norm(P ** -0.5))
            slots(dve, *k_span, with_norm(1.0))
            slots(dve, k_span[1], k_span[1] + 1, body)
            rows.dve_heads(dve, 0)
            slots(dve, k_span[1] + 1, k_span[1] + 2, body)
            rows.dve_heads(dve, 1)
            slots(dve, k_span[1] + 2, g1, body)
            rows.dve_columns(dve)
    front.st.close()
    rows.st.close()
    st.close()


def delta(e, QKV, QD, R, SEL, COL, GL, LMASK, DMASK, at, at2):
    st = Stage(e, "delta")
    nc = e.nc
    HW = 4 * P
    off = [at]

    def halves(n, area=None):
        if area is not None:
            return [st.sb(f"{n}{x}", [P, HW], area + x * HW * 4) for x in range(2)]
        out = [st.sb(f"{n}{x}", [P, HW], off[0] + x * HW * 4) for x in range(2)]
        off[0] += 2 * HW * 4
        return out

    N, QK, X, XT, PB, LM, KD, KBE = (halves(n) for n in ("n", "qk", "x", "xt", "pb", "lm", "kd", "kbe"))
    off[0] = at2
    VB, S = halves("vb"), halves("s")
    DA, DB, EA, EB = (halves(n, TMP + m * 2 * HW * 4) for m, n in enumerate(("da", "db", "ea", "eb")))
    names = ("mask_in", "zeroed", "gram", "tok", "dec", "dec_exp", "qk_ready", "n_ready", "scaled", "l1", "x1", "xt_psum",
             "xt1", "lm_ready", "p_psum", "p_ready", "xy_psum", "x_ready", "uw_psum", "uw_ready", "ws_psum", "vn_ready",
             "o_psum", "o_ready", "s_ready")
    s = {n: st.sem(n) for n in names}
    LEVELS = 7

    def head(buf, n):
        return buf[:, n * P:(n + 1) * P]

    def col(c, r, h):
        return COL[:, (c * 4 + r) * DNH + h:(c * 4 + r) * DNH + h + 1]

    def mask(m):
        return LMASK[:, m * P:(m + 1) * P].unsqueeze(1).to_broadcast([P, 4, P])

    def four(buf):
        return buf[:, :].rearrange("p (h c) -> p h c", h=4)

    with nc.Block() as block:
        @block.sync
        def _(sp):
            sp.dma_start(LMASK[:, :], e.dram["level_mask"]).then_inc(s["mask_in"], 16)
            sp.dma_start(DMASK[:, :], e.dram["decay_mask"]).then_inc(s["mask_in"], 16)
            sp.wait_ge(s["mask_in"], 32)

        @block.tensor
        def _(pe):
            for c in range(NCH):
                cc = slice(c * P, (c + 1) * P)
                for x in range(2):
                    u = 2 * c + x
                    b = 3 * x
                    if c:
                        pe.wait_ge(s["o_ready"], u - 1)
                        pe.wait_ge(s["s_ready"], u - 1)
                    for n in range(4):
                        h = 4 * x + n
                        q, k = QKV[:, h, cc], QKV[:, DNH + h, cc]
                        nc.tensor.matmul(head(e.bank[b], n), k, k, start=True, stop=True)
                        nc.tensor.matmul(head(e.bank[b + 1], n), k, q, start=True, stop=True)
                        last = nc.tensor.matmul(head(e.bank[b + 2], n), SEL[:, h * P:(h + 1) * P], R[:, 0, cc],
                                                start=True, stop=True)
                    last.then_inc(s["gram"], 1)
                    if u:
                        pe.wait_ge(s["scaled"], u)
                    for n in range(4):
                        h = 4 * x + n
                        nc.tensor.transpose(head(e.bank[6], n), QKV[:, DNH + h, cc], e.ident[:, :])
                        last = nc.tensor.transpose(head(e.bank[7], n), QKV[:, 2 * DNH + h, cc], e.ident[:, :])
                    last.then_inc(s["tok"], 1)
                for x in range(2):
                    u = 2 * c + x
                    pe.wait_ge(s["x1"], u + 1)
                    for n in range(4):
                        last = nc.tensor.transpose(head(e.bank[3 * x], n), head(X[x], n), e.ident[:, :])
                    last.then_inc(s["xt_psum"], 1)
                for m in range(1, LEVELS):
                    for x in range(2):
                        step = (c * (LEVELS - 1) + m - 1) * 2 + x
                        pe.wait_ge(s["lm_ready"], step + 1)
                        if m == 1:
                            pe.wait_ge(s["xt1"], 2 * c + x + 1)
                        else:
                            pe.wait_ge(s["x_ready"], step - 1)
                        for n in range(4):
                            last = nc.tensor.matmul(head(e.bank[3 * x], n), head(LM[x], n), head(XT[x], n),
                                                    start=True, stop=True)
                        last.then_inc(s["p_psum"], 1)
                    for x in range(2):
                        step = (c * (LEVELS - 1) + m - 1) * 2 + x
                        pe.wait_ge(s["p_ready"], step + 1)
                        for n in range(4):
                            last = nc.tensor.matmul(head(e.bank[3 * x + 1], n), head(X[x], n), head(PB[x], n),
                                                    start=True, stop=True)
                            if m < LEVELS - 1:
                                last = nc.tensor.matmul(head(e.bank[3 * x + 2], n), head(PB[x], n), head(X[x], n),
                                                        start=True, stop=True)
                        last.then_inc(s["xy_psum"], 1)
                for x in range(2):
                    u = 2 * c + x
                    pe.wait_ge(s["x_ready"], (c + 1) * (LEVELS - 1) * 2 - 1 + x)
                    pe.wait_ge(s["scaled"], u + 1)
                    for n in range(4):
                        nc.tensor.matmul(head(e.bank[3 * x], n), head(XT[x], n), head(VB[x], n), start=True, stop=True)
                        last = nc.tensor.matmul(head(e.bank[3 * x + 1], n), head(KBE[x], n), head(XT[x], n),
                                                start=True, stop=True)
                    last.then_inc(s["uw_psum"], 1)
                for x in range(2):
                    u = 2 * c + x
                    pe.wait_ge(s["uw_ready"], u + 1)
                    if c:
                        pe.wait_ge(s["s_ready"], u - 1)
                    else:
                        pe.wait_ge(s["zeroed"], 1)
                    for n in range(4):
                        last = nc.tensor.matmul(head(e.bank[3 * x + 2], n), head(KBE[x], n), head(S[x], n),
                                                start=True, stop=True)
                    last.then_inc(s["ws_psum"], 1)
                for x in range(2):
                    u = 2 * c + x
                    pe.wait_ge(s["vn_ready"], u + 1)
                    pe.wait_ge(s["qk_ready"], u + 1)
                    for n in range(4):
                        nc.tensor.matmul(head(e.bank[3 * x], n), head(S[x], n), QD[:, 4 * x + n, cc],
                                         start=True, stop=False)
                        nc.tensor.matmul(head(e.bank[3 * x], n), head(PB[x], n), head(QK[x], n),
                                         start=False, stop=True)
                        last = nc.tensor.matmul(head(e.bank[3 * x + 1], n), head(KD[x], n), head(PB[x], n),
                                                start=True, stop=True)
                    last.then_inc(s["o_psum"], 1)

        @block.scalar
        def _(act):
            for c in range(NCH):
                for x in range(2):
                    u = 2 * c + x
                    act.wait_ge(s["dec"], u + 1)
                    nc.scalar.activation(EA[x][:, :], DA[x][:, :], ACT.Exp)
                    nc.scalar.activation(EB[x][:, :], DB[x][:, :], ACT.Exp, scale=-1.0).then_inc(s["dec_exp"], 1)
                    act.wait_ge(s["tok"], u + 1)
                    for n in range(4):
                        h = 4 * x + n
                        nc.scalar.activation(head(KD[x], n), head(e.bank[6], n), ACT.Copy, scale=col(c, 3, h))
                        nc.scalar.activation(head(KBE[x], n), head(e.bank[6], n), ACT.Copy, scale=col(c, 2, h))
                        last = nc.scalar.activation(head(VB[x], n), head(e.bank[7], n), ACT.Copy, scale=col(c, 1, h))
                    last.then_inc(s["scaled"], 1)
                for x in range(2):
                    act.wait_ge(s["xt_psum"], 2 * c + x + 1)
                    nc.scalar.activation(XT[x][:, :], e.bank[3 * x][:, :], ACT.Copy).then_inc(s["xt1"], 1)
                for m in range(1, LEVELS):
                    for x in range(2):
                        step = (c * (LEVELS - 1) + m - 1) * 2 + x
                        act.wait_ge(s["p_psum"], step + 1)
                        nc.scalar.activation(PB[x][:, :], e.bank[3 * x][:, :], ACT.Copy).then_inc(s["p_ready"], 1)
                for x in range(2):
                    act.wait_ge(s["uw_psum"], 2 * c + x + 1)
                    nc.scalar.activation(VB[x][:, :], e.bank[3 * x][:, :], ACT.Copy)
                    nc.scalar.activation(KBE[x][:, :], e.bank[3 * x + 1][:, :], ACT.Copy).then_inc(s["uw_ready"], 1)
                for x in range(2):
                    act.wait_ge(s["o_psum"], 2 * c + x + 1)
                    nc.scalar.activation(QKV[:, 2 * DNH + 4 * x:2 * DNH + 4 * x + 4, c * P:(c + 1) * P],
                                         four(e.bank[3 * x]), ACT.Copy).then_inc(s["o_ready"], 1)

        @block.vector
        def _(dve):
            nc.vector.memset(S[0][:, :], 0.0)
            nc.vector.memset(S[1][:, :], 0.0).then_inc(s["zeroed"], 1)
            dve.wait_ge(s["mask_in"], 32)
            dve.wait_ge(s["zeroed"], 1)
            for c in range(NCH):
                for x in range(2):
                    u = 2 * c + x
                    dve.wait_ge(s["gram"], u + 1)
                    for n in range(4):
                        h = 4 * x + n
                        nc.vector.scalar_tensor_tensor(head(DA[x], n), head(e.bank[3 * x + 2], n), col(c, 0, h),
                                                       DMASK[:, 0:P], ALU.subtract, ALU.add)
                        last = nc.vector.scalar_tensor_tensor(head(DB[x], n), head(e.bank[3 * x + 2], n), col(c, 0, h),
                                                              DMASK[:, P:2 * P], ALU.subtract, ALU.add)
                    last.then_inc(s["dec"], 1)
                    dve.wait_ge(s["dec_exp"], u + 1)
                    nc.vector.tensor_tensor(QK[x][:, :], e.bank[3 * x + 1][:, :], EA[x][:, :], ALU.mult
                                            ).then_inc(s["qk_ready"], 1)
                    for n in range(4):
                        last = nc.vector.scalar_tensor_tensor(head(N[x], n), head(e.bank[3 * x], n), col(c, 1, 4 * x + n),
                                                              head(EB[x], n), ALU.mult, ALU.mult)
                    last.then_inc(s["n_ready"], 1)
                    dve.wait_ge(s["n_ready"], u + 1)
                    nc.vector.tensor_tensor(four(LM[x]), four(N[x]), mask(0), ALU.mult).then_inc(s["l1"], 1)
                    dve.wait_ge(s["l1"], u + 1)
                    nc.vector.scalar_tensor_tensor(four(X[x]), four(LM[x]), -1.0,
                                                   e.ident[:, :].unsqueeze(1).to_broadcast([P, 4, P]),
                                                   ALU.mult, ALU.add).then_inc(s["x1"], 1)
                for x in range(2):
                    dve.wait_ge(s["x1"], 2 * c + x + 1)
                    nc.vector.tensor_tensor(four(LM[x]), four(N[x]), mask(1), ALU.mult).then_inc(s["lm_ready"], 1)
                for m in range(1, LEVELS):
                    for x in range(2):
                        step = (c * (LEVELS - 1) + m - 1) * 2 + x
                        dve.wait_ge(s["xy_psum"], step + 1)
                        if m + 1 < LEVELS:
                            nc.vector.tensor_tensor(four(LM[x]), four(N[x]), mask(m + 1), ALU.mult
                                                    ).then_inc(s["lm_ready"], 1)
                            nc.vector.tensor_tensor(X[x][:, :], X[x][:, :], e.bank[3 * x + 2][:, :], ALU.subtract)
                        nc.vector.tensor_tensor(XT[x][:, :], XT[x][:, :], e.bank[3 * x + 1][:, :], ALU.subtract
                                                ).then_inc(s["x_ready"], 1)
                for x in range(2):
                    u = 2 * c + x
                    dve.wait_ge(s["ws_psum"], u + 1)
                    dve.wait_ge(s["uw_ready"], u + 1)
                    nc.vector.tensor_tensor(PB[x][:, :], VB[x][:, :], e.bank[3 * x + 2][:, :], ALU.subtract
                                            ).then_inc(s["vn_ready"], 1)
                for x in range(2):
                    u = 2 * c + x
                    dve.wait_ge(s["o_psum"], u + 1)
                    for n in range(4):
                        last = nc.vector.scalar_tensor_tensor(head(S[x], n), head(S[x], n), GL[:, 4 * x + n, c:c + 1],
                                                              head(e.bank[3 * x + 1], n), ALU.mult, ALU.add)
                    last.then_inc(s["s_ready"], 1)
    st.close()


def sgu_project(e, xh, xl, VT, LNP, UG):
    st = Stage(e, "sguv")
    nc = e.nc
    stats = st.sb("stats", [P, NCH, 2, 6], TMP)
    mv = st.sb("mv", [P, NCH, 2], TMP + 256)
    rs = st.sb("rs", [P, NCH], TMP + 320)
    nrm = [st.sb(f"nrm{r}", [P, D], TMP + 1024 + r * D * 4) for r in range(2)]
    ln_in, gelu_done, var_ready, std_ready, chain = (st.sem(n) for n in ("ln_in", "gelu_done", "var_ready", "std_ready",
                                                                        "chain"))
    a, b = START["wv2"]
    u_slots = START["wu2"]
    sp_span, pool_span = feed_ahead(e, u_slots[1])
    with nc.Block() as block:
        @block.sync
        def _(sp):
            sp.dma_start(LNP[:, :], e.dram["sgu_ln"]).then_inc(ln_in, 16)
            feed_sp(e, sp, sp_span)
            sp.wait_ge(ln_in, 16)

        @block.gpsimd
        def _(pool):
            feed_pool(e, pool, pool_span)

        @block.tensor
        def _(pe):
            def body(nm, i, p, g, ih, gh):
                pe_slot_begin(e, pe, g)
                pe_token_major(e, p, 256, xh, xl, False).then_inc(e.slot_done, 1)

            def u_body(nm, i, p, g, ih, gh):
                pe_slot_begin(e, pe, g)
                pe_feature_major(e, p, KT, 2, xh, xl, False).then_inc(e.slot_done, 1)

            slots(pe, a, b, body)
            slots(pe, *u_slots, u_body)

        @block.scalar
        def _(act):
            def body(nm, i, p, g, ih, gh):
                act.wait_ge(e.slot_done, g + 1)
                cols = slice(256 * i, 256 * i + 256) if isinstance(i, int) else ds(256 * i, 256)
                for t in range(NCH):
                    last = nc.scalar.activation(VT[:, t, cols], e.bank[2 * p + t // 2][:, (t % 2) * 256:(t % 2 + 1) * 256],
                                                ACT.Gelu)
                last.then_inc(e.acc_free, 1)
            slots(act, a, b, body)
            act.wait_ge(var_ready, 1)
            nc.scalar.activation(rs[:, :], mv[:, :, 1], ACT.Sqrt, bias=e.eps[:, 1:2]).then_inc(std_ready, 1)

            def u_body(nm, i, p, g, ih, gh):
                act.wait_ge(e.slot_done, g + 1)
                for n in range(2):
                    last = nc.scalar.activation(tile2(UG, i, n), e.bank[2 * p + n][:, :], ACT.Gelu)
                last.then_inc(e.acc_free, 1)
            slots(act, *u_slots, u_body)

        @block.vector
        def _(dve):
            done = [0]

            def link(ins):
                done[0] += 1
                ins.then_inc(chain, 1)
                dve.wait_ge(chain, done[0])

            dve.wait_ge(e.acc_free, b)
            for t in range(NCH):
                for half in range(2):
                    last = nc.vector.bn_stats(stats[:, t, half, :], VT[:, t, half * 512:(half + 1) * 512])
            link(last)
            for t in range(NCH):
                last = nc.vector.bn_aggr(mv[:, t, :], stats[:, t, :, :].rearrange("p a b -> p (a b)"))
            last.then_inc(var_ready, 1)
            dve.wait_ge(std_ready, 1)
            link(nc.vector.reciprocal(rs[:, :], rs[:, :]))
            dve.wait_ge(ln_in, 16)
            for t in range(NCH):
                link(nc.vector.tensor_scalar(nrm[0][:, :], VT[:, t, :], mv[:, t, 0:1], rs[:, t:t + 1],
                                             ALU.subtract, ALU.mult))
                link(nc.vector.tensor_tensor(nrm[1][:, :], nrm[0][:, :], LNP[:, 0:D], ALU.mult))
                link(nc.vector.tensor_tensor(VT[:, t, :], nrm[1][:, :], LNP[:, D:2 * D], ALU.add))
    st.close()


class Spatial:

    def __init__(self, e, VT, UG, WS, SB, gh, gl):
        self.e, self.st = e, Stage(e, "spat")
        self.VT, self.UG, self.WS, self.SB, self.gh, self.gl = VT, UG, WS, SB, gh, gl
        self.wm = self.st.sb("wm", [P, D // P, P], TMP)
        self.msk = self.st.sb("msk", [P, P], TMP + 4096)
        self.t = [self.st.sb(f"t{r}", [P, T], TMP + 4608 + r * T * 4) for r in range(2)]
        self.v = [self.st.sb(f"v{r}", [P, T], TMP + 4608 + (2 + r) * T * 4) for r in range(2)]
        self.ws_in, self.w_ready, self.mixed, self.t_ready, self.v_ready, self.hi_ready, self.lo_ready = (
            self.st.sem(n) for n in ("ws_in", "w_ready", "mixed", "t_ready", "v_ready", "hi_ready", "lo_ready"))

    def sp(self, sp):
        for t, n in ((self.WS, "spatial_w"), (self.SB, "spatial_b")):
            sp.dma_start(t[:, :, :], self.e.dram[n]).then_inc(self.ws_in, 16)
        sp.dma_start(self.msk[:, :], self.e.dram["causal"]).then_inc(self.ws_in, 16)

    def sp_end(self, sp):
        sp.wait_ge(self.ws_in, 48)

    def dve_start(self, dve):
        dve.wait_ge(self.ws_in, 48)
        self.e.nc.vector.tensor_tensor(self.wm[:, :, :], self.WS[:, :, :],
                                       self.msk[:, :].unsqueeze(1).to_broadcast([P, D // P, P]), ALU.mult
                                       ).then_inc(self.w_ready, 1)

    def pe(self, pe, i):
        pe.wait_ge(self.w_ready, 1)
        for n in range(2):
            g = 2 * i + n
            if i:
                pe.wait_ge(self.t_ready, g - 1)
            for c in range(NCH):
                last = self.e.nc.tensor.matmul(self.e.bank[6 + n][:, c * P:(c + 1) * P],
                                               self.VT[:, c, g * P:(g + 1) * P], self.wm[:, g, :],
                                               start=True, stop=True)
            last.then_inc(self.mixed, 1)

    def act(self, act, i):
        for n in range(2):
            act.wait_ge(self.v_ready, 2 * i + n + 1)
            self.e.nc.scalar.activation(self.gh[:, 2 * i + n, :], self.v[n][:, :], ACT.Copy
                                        ).then_inc(self.hi_ready, 1)

    def dve(self, dve, i):
        nc = self.e.nc
        for n in range(2):
            g = 2 * i + n
            dve.wait_ge(self.mixed, g + 1)
            nc.vector.tensor_tensor(self.t[n][:, :].rearrange("p (c t) -> p c t", c=NCH),
                                    self.e.bank[6 + n][:, :].rearrange("p (c t) -> p c t", c=NCH),
                                    self.SB[:, g, :].unsqueeze(1).to_broadcast([P, NCH, P]), ALU.add
                                    ).then_inc(self.t_ready, 1)
        for n in range(2):
            g = 2 * i + n
            dve.wait_ge(self.t_ready, g + 1)
            nc.vector.tensor_tensor(self.v[n][:, :], self.t[n][:, :], self.UG[:, g, :], ALU.mult
                                    ).then_inc(self.v_ready, 1)
        for n in range(2):
            g = 2 * i + n
            dve.wait_ge(self.hi_ready, g + 1)
            nc.vector.tensor_tensor(self.gl[:, g, :], self.v[n][:, :], self.gh[:, g, :].bitcast(F32), ALU.subtract
                                    ).then_inc(self.lo_ready, 1)


class DeepNorm:

    def __init__(self, e, name, y, acc, gain, shift, split=None, store=None):
        self.e, self.st, self.y, self.acc, self.split, self.store = e, Stage(e, name), y, acc, split, store
        self.gain, self.shift = PARAM_AT[gain], PARAM_AT[shift]
        self.t = [self.st.sb(f"t{r}", [P, T], TMP + r * W * 4) for r in range(2)]
        self.sq = [self.st.sb(f"sq{r}", [P, T], TMP + (2 + r) * W * 4) for r in range(2)]
        self.ring = self.t + self.sq
        self.r = self.st.sb("r", [P, T], TMP + 4 * W * 4)
        self.mean_ready, self.centred, self.squared, self.sq_summed, self.std_ready, self.rstd_ready, self.scaled, \
            self.out_ready, self.hi_ready, self.lo_ready, self.stored = (self.st.sem(n) for n in (
                "mean_ready", "centred", "squared", "sq_summed", "std_ready", "rstd_ready", "scaled", "out_ready",
                "hi_ready", "lo_ready", "stored"))

    def sp(self, sp):
        if self.store is not None:
            for k in range(0, KT, 2):
                sp.wait_ge(self.out_ready, k + 2)
                sp.dma_start(self.store[:, k:k + 2, :], self.y[:, k:k + 2, :]).then_inc(self.stored, 16)
            sp.wait_ge(self.stored, 16 * (KT // 2))

    def pe(self, pe):
        e, nc = self.e, self.e.nc
        nc.tensor.matmul(e.bank[6][:, :], e.mean_ones[:, :], self.acc[:, :], start=True, stop=True
                         ).then_inc(self.mean_ready, 1)
        for k in range(KT):
            pe.wait_ge(self.squared, k + 1)
            nc.tensor.matmul(e.bank[7][:, :], e.mean_ones[:, :], self.sq[k % 2][:, :], start=k == 0, stop=k == KT - 1
                             ).then_inc(self.sq_summed, 1)

    def act(self, act):
        e, nc, y = self.e, self.e.nc, self.y
        for k in range(KT):
            act.wait_ge(self.centred, k + 1)
            if k >= 2:
                act.wait_ge(self.sq_summed, k - 1)
            nc.scalar.activation(self.sq[k % 2][:, :], y[:, k, :], ACT.Square).then_inc(self.squared, 1)
        act.wait_ge(self.sq_summed, KT)
        nc.scalar.activation(self.r[:, :], e.bank[7][:, :], ACT.Sqrt, bias=e.eps[:, 1:2]).then_inc(self.std_ready, 1)
        for k in range(KT):
            b = e.params[:, self.shift + k:self.shift + k + 1]
            act.wait_ge(self.scaled, k + 1)
            if self.split is not None:
                nc.scalar.activation(self.split[0][:, k, :], self.ring[k % 4][:, :], ACT.Identity, bias=b
                                     ).then_inc(self.hi_ready, 1)
            nc.scalar.activation(y[:, k, :], self.ring[k % 4][:, :], ACT.Identity, bias=b).then_inc(self.out_ready, 1)

    def dve(self, dve):
        e, nc, y = self.e, self.e.nc, self.y
        dve.wait_ge(self.mean_ready, 1)
        for k in range(KT):
            nc.vector.tensor_tensor(y[:, k, :], y[:, k, :], e.bank[6][:, :], ALU.subtract).then_inc(self.centred, 1)
        dve.wait_ge(self.std_ready, 1)
        nc.vector.reciprocal(self.r[:, :], self.r[:, :]).then_inc(self.rstd_ready, 1)
        dve.wait_ge(self.rstd_ready, 1)

        def scale(k):
            if k >= 4:
                dve.wait_ge(self.out_ready, k - 3)
            nc.vector.scalar_tensor_tensor(self.ring[k % 4][:, :], y[:, k, :],
                                           e.params[:, self.gain + k:self.gain + k + 1], self.r[:, :],
                                           ALU.mult, ALU.mult).then_inc(self.scaled, 1)

        scale(0)
        for k in range(KT):
            if k + 1 < KT:
                scale(k + 1)
            if self.split is not None:
                dve.wait_ge(self.hi_ready, k + 1)
                nc.vector.scalar_tensor_tensor(self.split[1][:, k, :], self.ring[k % 4][:, :],
                                               e.params[:, self.shift + k:self.shift + k + 1],
                                               self.split[0][:, k, :].bitcast(F32), ALU.add, ALU.subtract
                                               ).then_inc(self.lo_ready, 1)


def last_norm(e, norm):
    with e.nc.Block() as block:
        @block.sync
        def _(sp):
            norm.sp(sp)

        @block.tensor
        def _(pe):
            norm.pe(pe)

        @block.scalar
        def _(act):
            norm.act(act)

        @block.vector
        def _(dve):
            norm.dve(dve)
    norm.st.close()


def router(e, xh, xl, CR, front):
    st = Stage(e, "route")
    nc = e.nc
    a, b = START["router"]
    NG, EG = 4, NE // 4
    off = [TMP]

    def small(n, cols):
        t = st.sb(n, [P, NCH, cols], off[0])
        off[0] += (NCH * cols * 4 + 31) // 32 * 32
        return t

    RB, PRI = st.sb("rb", [P, 32], TMP + 5 * W * 4), st.sb("pri", [P, 4], TMP + 5 * W * 4 + 128)
    LG, EX, M1, EQ, MG, IN, TM, MA, MB, M2, ED, SM, GP, W1, W2, CI = (small(n, c) for n, c in (
        ("lg", 32), ("ex", 4), ("m1", 1), ("eq", 4), ("mg", 4), ("in", 4), ("tm", 4), ("ma", 4), ("mb", 4), ("m2", 1),
        ("ed", 1), ("sm", 1), ("gp", 1), ("w1", 1), ("w2", 1), ("ci", 4)))
    CW = small("cw", NE)
    rb_in, e1_pre, e1_ready, e2_pre, e2_ready, cw_ready, cr_psum, cr_ready, chain = (
        st.sem(n) for n in ("rb_in", "e1_pre", "e1_ready", "e2_pre", "e2_ready", "cw_ready", "cr_psum", "cr_ready", "chain"))
    AX = mybir.AxisListType.X
    def sp_part(sp):
        sp.dma_start(RB[:, :], e.dram["router_b"]).then_inc(rb_in, 16)
        sp.dma_start(PRI[:, :], e.dram["priority"]).then_inc(rb_in, 16)

    def pe_part(pe):
        front.pe(pe)
        pe_slot_begin(e, pe, a)
        pe.wait_ge(front.lo_ready, KT)
        pe_token_major(e, a % 2, 32, xh, xl, False).then_inc(e.slot_done, 1)

    def pe_rows(pe):
        pe.wait_ge(cw_ready, 1)
        for t in range(NCH):
            last = nc.tensor.transpose(e.bank[6][0:NE, t * P:(t + 1) * P], CW[:, t, :], e.ident[:, :])
        last.then_inc(cr_psum, 1)

    def act_part(act):
        front.act(act)
        act.wait_ge(e1_pre, 1)
        nc.scalar.activation(EX[:, :, :], TM[:, :, :], ACT.Exp).then_inc(e1_ready, 1)
        act.wait_ge(e2_pre, 1)
        nc.scalar.activation(ED[:, :, :], SM[:, :, :], ACT.Exp).then_inc(e2_ready, 1)
        act.wait_ge(cr_psum, 1)
        nc.scalar.activation(CR[:, :], e.bank[6][0:NE, :], ACT.Copy).then_inc(cr_ready, 1)

    def dve_part(dve):
        front.dve(dve)
        done = [0]
        V = nc.vector

        def link(ins):
            done[0] += 1
            ins.then_inc(chain, 1)
            dve.wait_ge(chain, done[0])

        def wide(x, n=4):
            return x.to_broadcast([P, NCH, n])

        pri = PRI[:, :].unsqueeze(1).to_broadcast([P, NCH, 4])

        def first_max(out, logits, top):
            link(V.tensor_tensor(EQ[:, :, :], logits, wide(top[:, :, :]), ALU.is_equal))
            link(V.tensor_tensor(EQ[:, :, :], EQ[:, :, :], pri, ALU.mult))
            link(V.tensor_reduce(M2[:, :, :], EQ[:, :, :], AX, ALU.max))
            link(V.tensor_tensor(out[:, :, :], EQ[:, :, :], wide(M2[:, :, :]), ALU.is_equal))

        dve.wait_ge(e.slot_done, a + 1)
        dve.wait_ge(rb_in, 32)
        p = a % 2
        for t in range(NCH):
            last = V.tensor_tensor(LG[:, t, :], e.bank[2 * p + t // 2][:, (t % 2) * 32:(t % 2 + 1) * 32], RB[:, :],
                                   ALU.add)
        last.then_inc(e.acc_free, 1)
        dve.wait_ge(e.acc_free, a + 1)
        lg = LG[:, :, 0:NG]
        link(V.tensor_reduce(M1[:, :, :], lg, AX, ALU.max))
        V.tensor_tensor(TM[:, :, :], lg, wide(M1[:, :, :]), ALU.subtract).then_inc(e1_pre, 1)
        first_max(MG, lg, M1)
        dve.wait_ge(e1_ready, 1)
        link(V.tensor_reduce(GP[:, :, :], EX[:, :, :], AX, ALU.add))
        for n in range(NG):
            sub = LG[:, :, NG + EG * n:NG + EG * (n + 1)]
            link(V.tensor_tensor(TM[:, :, :] if n else IN[:, :, :], sub, wide(MG[:, :, n:n + 1]), ALU.mult))
            if n:
                link(V.tensor_tensor(IN[:, :, :], IN[:, :, :], TM[:, :, :], ALU.add))
        link(V.tensor_reduce(M1[:, :, :], IN[:, :, :], AX, ALU.max))
        first_max(MA, IN[:, :, :], M1)
        link(V.scalar_tensor_tensor(IN[:, :, :], MA[:, :, :], -BIG, IN[:, :, :], ALU.mult, ALU.add))
        link(V.tensor_reduce(W2[:, :, :], IN[:, :, :], AX, ALU.max))
        first_max(MB, IN[:, :, :], W2)
        V.tensor_tensor(SM[:, :, :], W2[:, :, :], M1[:, :, :], ALU.subtract).then_inc(e2_pre, 1)
        dve.wait_ge(e2_ready, 1)
        link(V.scalar_tensor_tensor(W1[:, :, :], ED[:, :, :], 1.0, GP[:, :, :], ALU.add, ALU.mult))
        link(V.reciprocal(W1[:, :, :], W1[:, :, :]))
        link(V.tensor_tensor(W2[:, :, :], W1[:, :, :], ED[:, :, :], ALU.mult))
        link(V.tensor_tensor(CI[:, :, :], MA[:, :, :], wide(W1[:, :, :]), ALU.mult))
        link(V.tensor_tensor(TM[:, :, :], MB[:, :, :], wide(W2[:, :, :]), ALU.mult))
        link(V.tensor_tensor(CI[:, :, :], CI[:, :, :], TM[:, :, :], ALU.add))
        for n in range(NG):
            last = V.tensor_tensor(CW[:, :, EG * n:EG * (n + 1)], CI[:, :, :], wide(MG[:, :, n:n + 1]), ALU.mult)
        last.then_inc(cw_ready, 1)
    return sp_part, pe_part, pe_rows, act_part, dve_part, cr_ready, (front.st, st)


def layout_stream(w, kt, ntile, order=None):
    k, n = w.shape
    v = w.reshape(k // P, P, n // P, P).transpose(2, 1, 0, 3)
    if order is not None:
        v = v[order]
    v = v.reshape(-1, ntile, P, kt, P).transpose(0, 2, 1, 3, 4)
    return np.ascontiguousarray(v.reshape(v.shape[0], P, ntile * kt * P))


def pack_params(p):
    cols = [np.asarray(p[n], np.float32).reshape(s, P).T for n, s in PARAM_SIZES]
    return np.ascontiguousarray(np.concatenate(cols, axis=1))


def pad_rows(groups, width=P):
    first = np.asarray(groups[0])
    out = np.zeros(first.shape[:-1] + (width,), np.float32)
    for g, v in enumerate(groups):
        out[..., 32 * g:32 * g + v.shape[-1]] = v
    return out


def feature_major(x):
    return np.ascontiguousarray(x.T.reshape(x.shape[1] // P, P, x.shape[0]).transpose(1, 0, 2))


def layout_token_major(w, ncol):
    k, n = w.shape
    v = w.reshape(k // P, P, n // ncol, ncol).transpose(2, 1, 0, 3)
    return np.ascontiguousarray(v.reshape(n // ncol, P, k // P * ncol))


def layout_inputs(i):
    g = {n: np.asarray(v) for n, v in i.items()}
    dram = {}
    x = np.concatenate([g["x"][0], g["ctx"][0]], axis=0)
    dram["x"] = feature_major(x)
    dram["ident"] = np.eye(P, dtype=np.float32)
    w_in, b_in = g["w_in"][0], g["b_in"][0]
    xf, q, k, v, o, gt, gf, gm = np.split(w_in, np.cumsum([512, 1024, 1024, 1024, 1024, 16, 1024]), axis=1)
    bxf, bq, bk, bv, bo, bgt, bgf, bgm = np.split(b_in, np.cumsum([512, 1024, 1024, 1024, 1024, 16, 1024]))
    order = (0, 2, 1, 3)
    dram["gates"] = layout_stream(pad_rows([gt[:, 4 * m:4 * m + 4] for m in order]), KT, 1)
    params = {
        "c": g["c"][0], "c_ctx": g["c_ctx"], "b_ada": g["b_ada"][0], "norm_g": g["norm_g"][0], "bk": bk, "bq": bq,
        "bgate": pad_rows([bgt[4 * m:4 * m + 4] for m in order]), "bo": bo, "bgf": bgf, "bgm": bgm,
        "conv_w": g["conv_w"][0], "conv_b": g["conv_b"][0], "head_g": g["head_g"][0],
        "conv_w_2": g["conv_w_2"][0], "dn_g": g["dn_norm_g_2"][0], "ln1_g": g["ln1_g_2"][0],
        "ln1_b": g["ln1_b_2"][0], "ln2_g": g["ln2_g_2"][0], "ln2_b": g["ln2_b_2"][0],
        "dt_bias": pad_rows([g["dt_bias_2"][0]]), "a_log": pad_rows([g["a_log_2"][0]]),
    }
    dram["params"] = pack_params(params)
    dram["w_ada"] = layout_token_major(g["w_ada"][0], 512)

    def pair(name, wa, wb, w2, half_tiles):
        n = half_tiles * P
        for h in range(2):
            ha, hb = (m[:, h * n:(h + 1) * n].reshape(D, half_tiles, P) for m in (wa, wb))
            both = np.stack([ha, hb], axis=2).reshape(D, 2 * n)
            dram[f"{name[0]}{h}"] = layout_stream(both, KT, 2)
            dram[f"{name[1]}{h}"] = layout_stream(w2[h * n:(h + 1) * n], half_tiles, 1)

    for s in "ab":
        w13 = g[f"w13_{s}"][0]
        pair((f"gu_{s}", f"dn_{s}"), w13[:, :FFH], w13[:, FFH:], g[f"w2_{s}"][0], HTILES)
    dram["wk"], dram["wq"] = layout_stream(k, KT, 2), layout_stream(q, KT, 2)
    dram["wv"], dram["wxf"] = layout_token_major(v, 256), layout_token_major(xf, 256)
    dram["wo"], dram["wgf"], dram["wgm"] = (layout_stream(m, KT, 2) for m in (o, gf, gm))
    dram["w_four"] = layout_stream(g["w_four"][0], 4, 2)
    dram["w_mproj"], dram["w_out"] = layout_stream(g["w_mproj"][0], KT, 2), layout_stream(g["w_out"][0], KT, 2)
    dram["bias_tok"] = np.ascontiguousarray(np.broadcast_to(np.concatenate([bv, bxf]), (P, D + 512)))
    w_in = g["w_in_2"][0]
    qkv, z, aa, bb, u2, v2, gd, gsg = np.split(w_in, np.cumsum([3072, 1024, 8, 8, 1024, 1024, 1024]), axis=1)
    dram["gates2"] = layout_stream(pad_rows([aa, bb]), KT, 1)
    for n, m in (("wqkv2", qkv), ("wz2", z), ("wgd2", gd), ("wu2", u2), ("wgs2", gsg), ("w_dn", g["w_dn_out_2"][0]),
                 ("w_sgu", g["w_sgu_out_2"][0]), ("w_out2", g["w_out_2"][0])):
        dram[n] = layout_stream(m, KT, 2)
    dram["wv2"] = layout_token_major(v2, 256)
    rw = np.concatenate([g["router_group_w_2"][0], g["router_expert_w_2"][0], np.zeros((D, 12), np.float32)], axis=1)
    dram["router"] = layout_token_major(rw, 32)
    rb = np.concatenate([g["router_group_b_2"][0], g["router_expert_b_2"][0], np.zeros(12, np.float32)])
    dram["router_b"] = np.ascontiguousarray(np.broadcast_to(rb, (P, 32)))
    dram["priority"] = np.ascontiguousarray(np.broadcast_to(np.arange(4, 0, -1, dtype=np.float32), (P, 4)))
    flat = lambda m: m.transpose(1, 0, 2).reshape(D, NE * EFF)
    pair(("e_up", "e_dn"), flat(g["expert_w_gate_2"][0]), flat(g["expert_w_up_2"][0]),
         g["expert_w_down_2"][0].reshape(NE * EFF, D), ETILES)
    dram["sgu_ln"] = np.ascontiguousarray(
        np.broadcast_to(np.concatenate([g["sgu_ln_g_2"][0], g["sgu_ln_b_2"][0]]), (P, 2 * D)))
    dram["spatial_w"] = np.ascontiguousarray(g["spatial_w_2"][0].transpose(2, 0, 1))
    dram["spatial_b"] = np.ascontiguousarray(np.broadcast_to(g["spatial_b_2"][0], (P, D // P, P)))
    ones_at = lambda n: np.ascontiguousarray(np.broadcast_to(np.eye(n, dtype=np.float32)[:, :, None], (n, n, P))
                                             ).reshape(n, n * P)
    dram["sel8"] = ones_at(DNH)
    row, colm = np.meshgrid(np.arange(P), np.arange(P), indexing="ij")
    dram["causal"] = (row <= colm).astype(np.float32)
    dram["level_mask"] = np.concatenate(
        [((row >> (m + 1)) == (colm >> (m + 1))) & ((row >> m) % 2 == 1) & ((colm >> m) % 2 == 0)
         for m in range(7)], axis=1).astype(np.float32)
    dram["decay_mask"] = np.concatenate([np.where(row <= colm, 0, -BIG), np.where(colm < row, 0, BIG)],
                                        axis=1).astype(np.float32)
    sel = np.zeros((36, MH, P), np.float32)
    for h in range(MH):
        sel[h, h] = sel[32 + h, h] = 1.0
    dram["sel"] = sel.reshape(36, MH * P)
    s, t = np.meshgrid(np.arange(P), np.arange(P), indexing="ij")
    dram["scan_mask"] = np.concatenate([np.where(s <= t, 0, BIG), np.where(s >= t, 0, BIG)], axis=1).astype(np.float32)
    dft = lambda n: np.exp(-2j * np.pi * np.outer(np.arange(n), np.arange(n)) / n) / np.sqrt(n)
    tok, ch = np.kron(dft(T // 64), dft(64)), dft(P)
    dram["dft_t"] = np.ascontiguousarray(
        np.stack([tok.real, tok.imag]).reshape(2, NCH, P, T).transpose(2, 0, 1, 3).astype(np.float32))
    dram["dft_c"] = np.ascontiguousarray(np.stack([ch.real, -ch.imag], axis=1).astype(np.float32))
    return dram


INTERNAL = [("h1", [P, KT, T]), ("uh_s", [P, KT, T]), ("ul_s", [P, KT, T])]


def setup(nc, dram):
    e = Env()
    e.nc, e.dram, e.cleared = nc, dram, []
    e.split_upto, e.loaded_upto = 2, 2
    at = lambda n, shape, off, dt=F32: nc.alloc_sbuf_tensor_at(n, shape, dt, offset=off)
    e.raw = [at(f"raw{p}", [P, 2048], RAW + p * 8192) for p in range(2)]
    e.whi = [at(f"whi{p}", [P, 2048], WHI + p * 8192, F32R) for p in range(2)]
    e.wlo = [at(f"wlo{p}", [P, 2048], WLO + p * 8192, F32R) for p in range(2)]
    off = [CONST]

    def resident(n, shape):
        t = at(n, shape, off[0])
        off[0] += (int(np.prod(shape[1:])) * 4 + 31) // 32 * 32
        assert off[0] <= TMP, (n, off[0] - TMP)
        return t

    e.params, e.mods = resident("params", [P, NPARAM]), resident("mods", [P, ADA * KT, 2])
    e.gs, e.gg = resident("gs", [P, 3, KT, 2]), resident("gg", [P, 3, KT, 2])
    e.ident, e.ones, e.mean_ones = (resident(n, [P, P]) for n in ("ident", "ones", "mean_ones"))
    e.one_col, e.eps = resident("one_col", [P, 1]), resident("eps", [P, 2])
    e.bank = [nc.alloc_psum_tensor(f"bank{b}", [P, 512], F32) for b in range(8)]
    e.w_landed = [nc.alloc_semaphore(f"w_landed{p}") for p in range(2)]
    e.w_hi, e.w_split, e.slot_done, e.acc_free = (
        nc.alloc_semaphore(n) for n in ("w_hi", "w_split", "slot_done", "acc_free"))
    return e


def program(nc, dram):
    e = setup(nc, dram)
    prologue(e)
    uh = nc.alloc_sbuf_tensor_at("uh_a", [P, KT, W], F32R, offset=MAIN + 24576)
    ul = nc.alloc_sbuf_tensor_at("ul_a", [P, KT, W], F32R, offset=MAIN + 49152)
    n1 = NormFront(e, "n1", W, e.x0, uh, ul, pre=0, rstd=e.rstd0)
    y = nc.alloc_sbuf_tensor_at("y_a", [P, KT, W], F32, offset=MAIN)
    xr = nc.alloc_sbuf_tensor_at("xr", [P, KT, W], F32, offset=MAIN + 24576)
    acc = ffn(e, "fa", "gu_a", "dn_a", W, HTILES, uh, ul, y, MAIN + 73728, front=n1, late_load=(xr, dram["x"]))
    at = lambda n, shape, off, dt=F32: nc.alloc_sbuf_tensor_at(n, shape, dt, offset=MAIN + off)
    uh, ul = at("uh_m", [P, KT, W], 24576, F32R), at("ul_m", [P, KT, W], 49152, F32R)
    n2 = NormFront(e, "n2", W, y, uh, ul, acc=acc, post=(0, xr), pre=1, store=dram["h1"])
    K, V, Q = at("K", [P, KT, W], 74752), at("V", [P, NCH + NCC, D], 99328), at("Q", [P, KT, T], 123904)
    XF, bias_tok, GR = at("XF", [P, NCH, 512], 0), at("bias_tok", [P, D + 512], 8192), at("GR", [P, W], 14336)
    project_1(e, uh, ul, K, Q, V, XF, GR, bias_tok, n2)
    B, LF, G = at("B", [36, W], 17408), at("LF", [36, W], 20480), at("G", [36, W], 8192)
    SEL, MASK = at("SEL", [36, MH * P], 11264), at("MASK", [P, 2 * P], 13312)
    C = [at(f"C{n}", [P, 2, DH + P], 24576 + n * 3072) for n in range(2 * MH)]
    RT, HT = at("RT", [36, 3, W], 49152), at("HT", [P, KT, T], 58368)
    GC, MP = at("GC", [P, NCH + NCC, 36], 140288), at("MP", [36, 8], 140288 + 896)
    scan_rows(e, GR, B, LF, G, RT, MP, GC)
    scan(e, Q, K, V, C, HT, RT, GC, SEL, MASK)
    uh, ul = at("uh_r", [P, KT, T], 24576, F32R), at("ul_r", [P, KT, T], 40960, F32R)
    yfh, yfl = at("yfh", [P, 4, T], 107520, F32R), at("yfl", [P, 4, T], 115712, F32R)
    fourier(e, XF, yfh, yfl, MAIN + 74752, uh, ul)
    O, GF, GM = at("O", [P, KT, T], 74752), at("GF", [P, KT, T], 91136), at("GM", [P, KT, T], 123904)
    mh, ml = at("mh", [P, KT, T], 0, F32R), at("ml", [P, KT, T], 74752, F32R)
    yh, yl = at("yh", [P, KT, T], 24576, F32R), at("yl", [P, KT, T], 40960, F32R)
    Y1, XR = at("Y1", [P, KT, T], 91136), at("XR1", [P, KT, T], 107520)
    norm = HeadNorm(e, "hn", HT, 2, lambda i, n: column_of(e, PARAM_AT["head_g"], i, n), O, mh, ml)
    mixed, mixed_ready = product_gate_split(e, "w_mproj", mh, ml, GM, GF, yh, yl,
                                            ready=lambda pe, k: pe.wait_ge(norm.lo_ready, k + 1))
    out, acc = product_out(e, "w_out", yh, yl, Y1, XR, dram["h1"], START["w_four"][1], True, mixed_ready)
    products(e, [product_act(e, "wo", uh, ul, O, ACT.Sigmoid, "bo"),
                 product_act(e, "wgf", uh, ul, GF, ACT.Sigmoid, "bgf", norm=norm, norm_ready=START["wo"][1]),
                 product_act(e, "wgm", uh, ul, GM, ACT.Sigmoid, "bgm"),
                 product_gate(e, "w_four", 4, yfh, yfl, GF), mixed, out])
    uh, ul = at("uh_b", [P, KT, T], 0, F32R), at("ul_b", [P, KT, T], 16384, F32R)
    n3 = NormFront(e, "n3", T, Y1, uh, ul, acc=acc, post=(1, XR), pre=2)
    Y2 = at("Y2", [P, KT, T], 107520)
    acc = ffn(e, "fb", "gu_b", "dn_b", T, HTILES, uh, ul, Y2, MAIN + 32768, front=n3)
    xh, xl = at("xh", [P, KT, T], 0, F32R), at("xl", [P, KT, T], 16384, F32R)
    p3 = NormFront(e, "p3", T, Y2, xh, xl, acc=acc, post=(2, Y1), store=dram["h1"])
    QKV, GR2 = at("QKV", [P, 3 * DNH, T], 32768), at("GR2", [P, T], 81920)
    QD = at("QD", [P, DNH, T], 84480)
    R, SEL8 = at("R", [DNH, 4, T], 109056), at("SEL8", [DNH, DNH * P], 117248)
    LMASK, DMASK = at("LMASK", [P, 7 * P], 121344), at("DMASK", [P, 2 * P], 124928)
    COL, GL = at("COL", [P, NCH * 4 * DNH], 125952), at("GL", [P, DNH, NCH], 126464)
    rows = DeltaRows(e, GR2, R, SEL8, QKV, QD, COL, GL, MAIN + 126976)
    project_2(e, xh, xl, QKV, GR2, p3, rows)
    delta(e, QKV, QD, R, SEL8, COL, GL, LMASK, DMASK, MAIN, MAIN + 100864)
    OT = QKV[:, 2 * DNH:3 * DNH, :]
    xh, xl = at("xh_r", [P, KT, T], 0, F32R), at("xl_r", [P, KT, T], 16384, F32R)
    Z, GD = at("Z", [P, KT, T], 32768), at("GD", [P, KT, T], 49152)
    mh, ml = at("oh", [P, KT, T], 81920, F32R), at("ol", [P, KT, T], 98304, F32R)
    dg = PARAM_AT["dn_g"]
    back = Stage(e, "back")
    back_in = [back.sem(f"in{k}") for k in range(4)]

    def reload(sp):
        for k in range(4):
            kk = slice(2 * k, 2 * k + 2)
            for t, src in ((xh, "uh_s"), (xl, "ul_s")):
                sp.dma_start(t[:, kk, :].bitcast(F32), dram[src][:, kk, :]).then_inc(back_in[k], 16)

    def reloaded(eng, k):
        eng.wait_ge(back_in[k // 2], 32)

    norm = HeadNorm(e, "on", OT, 1, lambda i, n: e.params[:, dg:dg + 1], Z, mh, ml)
    products(e, [product_act(e, "wz2", xh, xl, Z, ACT.Silu, sp_start=reload, sp_end=lambda sp: reloaded(sp, KT - 1),
                             ready=reloaded, stages=(back,)),
                 product_act(e, "wgd2", xh, xl, GD, ACT.Sigmoid, norm=norm, norm_ready=START["wz2"][1]),
                 product_gate(e, "w_dn", KT, mh, ml, GD,
                              ready=lambda pe, k: pe.wait_ge(norm.lo_ready, k + 1))])
    VT, LNP = at("VT", [P, NCH, D], 114688), at("LNP", [P, 2 * D], 65536)
    UG = at("UG", [P, KT, T], 32768)
    sgu_project(e, xh, xl, VT, LNP, UG)
    WS, SB = at("WS", [P, D // P, P], 73728), at("SB", [P, D // P, P], 77824)
    gh, gl = at("gh", [P, KT, T], 81920, F32R), at("gl", [P, KT, T], 98304, F32R)
    space = Spatial(e, VT, UG, WS, SB, gh, gl)
    GS = at("GS", [P, KT, T], 32768)
    yh, yl = at("y2h", [P, KT, T], 0, F32R), at("y2l", [P, KT, T], 16384, F32R)
    MX, XR = at("MX", [P, KT, T], 114688), at("XR2", [P, KT, T], 81920)
    mixed, mixed_ready = product_gate_split(e, "w_sgu", gh, gl, GS, GD, yh, yl,
                                            ready=lambda pe, k: pe.wait_ge(space.lo_ready, k + 1))
    out, acc = product_out(e, "w_out2", yh, yl, MX, XR, dram["h1"], START["w_sgu"][1], False, mixed_ready)
    products(e, [product_act(e, "wgs2", xh, xl, GS, ACT.Sigmoid, norm=space, norm_ready=START["wgs2"][0],
                             sp_start=space.sp, sp_end=space.sp_end, straight=True), mixed, out])
    hh, hl = at("h4h", [P, KT, T], 0, F32R), at("h4l", [P, KT, T], 16384, F32R)
    ln1 = DeepNorm(e, "ln1", MX, acc, "ln1_g", "ln1_b", split=(hh, hl))
    CR, CX = at("CR", [NE, T], 131072), at("CX", [NE, T], 133120)
    route = router(e, hh, hl, CR, ln1)
    Y3 = at("Y3", [P, KT, T], 98304)
    acc = ffn(e, "moe", "e_up", "e_dn", T, ETILES, hh, hl, Y3, MAIN + 32768, squares=False, combine=(CR, CX), base=MX,
              route=route)
    last_norm(e, DeepNorm(e, "ln2", Y3, acc, "ln2_g", "ln2_b", store=dram["out"]))


def kernel(**inputs):
    import concourse.bacc as bacc
    from concourse.bass_utils import run_bass_kernel_spmd

    nc = bacc.Bacc("TRN2", target_bir_lowering=False, num_devices=1)
    arrays = {f"{n}_dram": a for n, a in layout_inputs(inputs).items()}
    dram = {n[:-5]: nc.dram_tensor(n, a.shape, F32, kind="ExternalInput").ap() for n, a in arrays.items()}
    for n, shape in INTERNAL:
        dram[n] = nc.dram_tensor(f"{n}_scratch", shape, F32, kind="Internal").ap()
    dram["out"] = nc.dram_tensor("out_dram", [P, KT, T], F32, kind="ExternalOutput").ap()
    program(nc, dram)
    result = run_bass_kernel_spmd(nc, [arrays], core_ids=[0]).results[0]["out_dram"]
    return np.ascontiguousarray(np.asarray(result).transpose(2, 1, 0).reshape(1, T, D))
```
